# Optimizing a Trainium2 kernel written in Bass

```python
import jax, jax.numpy as jnp
from jax import lax
import numpy as np

D_MODEL = 1024
BATCH = 1
SEQ = 512
DEPTH = 1
DEC_BATCH = 1
DEC_SEQ = 32
PAST_LEN = 256

CHUNK = 64
EPS = 1e-6
NEG = -1e30
N_HEADS_A = 16
N_KV_A = 4
GROUP_A = N_HEADS_A // N_KV_A
HEAD_DIM_A = D_MODEL // N_HEADS_A
WINDOW = 128
WIN_CHUNKS = WINDOW // CHUNK
BAND = (WIN_CHUNKS + 1) * CHUNK
N_HEADS_B = 4
DV_B = D_MODEL // N_HEADS_B
DK_B = DV_B // 2
GATE_RANK = 16
GATE_TAU = 16.0
GLA_BLOCK = 16
D_FF = (((8 * D_MODEL + 2) // 3 + 255) // 256) * 256

WA_Q = N_HEADS_A * HEAD_DIM_A
WA_KV = N_KV_A * HEAD_DIM_A
WB_K = N_HEADS_B * DK_B
WB_V = N_HEADS_B * DV_B
SPLIT_SIZES = (WA_Q, WA_KV, WA_KV, WB_K, WB_K, WB_V, WB_V, GATE_RANK, D_MODEL, D_MODEL)
SPLIT_POINTS = tuple(int(v) for v in np.cumsum(SPLIT_SIZES)[:-1])
P_IN = int(sum(SPLIT_SIZES))

kernel_name = "hybrid_swa_sink_gla_stream_step"

def _rmsnorm(x, g):
    xf = x.astype(jnp.float32)
    y = xf * lax.rsqrt(jnp.mean(xf * xf, axis=-1, keepdims=True) + EPS)
    return (y * g.astype(jnp.float32)).astype(x.dtype)

def _alibi_slopes():
    return 2.0 ** (-8.0 * jnp.arange(1, N_HEADS_A + 1, dtype=jnp.float32) / N_HEADS_A)

def _alibi_band_bias(qpos, kpos):
    qc = qpos // CHUNK
    kc = kpos // CHUNK
    ok = ((kpos[:, None, :] >= 0) & (kc[:, None, :] <= qc[:, :, None])
          & (kc[:, None, :] >= qc[:, :, None] - WIN_CHUNKS))
    dist = jnp.abs(qpos[:, :, None] - kpos[:, None, :]).astype(jnp.float32)
    slopes = _alibi_slopes().reshape(N_KV_A, GROUP_A)
    bias = -slopes[None, :, :, None, None] * dist[:, None, None]
    return jnp.where(ok[:, None, None], bias, NEG)

def _band(x):
    B, T = x.shape[:2]
    nC = T // CHUNK
    xp = jnp.pad(x, ((0, 0), (WINDOW, 0), (0, 0), (0, 0)))
    xc = xp.reshape(B, nC + WIN_CHUNKS, CHUNK, *x.shape[2:])
    return jnp.concatenate([xc[:, j:j + nC] for j in range(WIN_CHUNKS + 1)], axis=2)

def _sink_attend(q, k, v, bias, sinks):
    s = jnp.einsum('bnqhgd,bnkhd->bnhgqk', q, k).astype(jnp.float32) * (HEAD_DIM_A ** -0.5) + bias
    sink = sinks.astype(jnp.float32).reshape(N_KV_A, GROUP_A)[None, None, :, :, None, None]
    m = jnp.maximum(jnp.max(s, axis=-1, keepdims=True), sink)
    p = jnp.exp(s - m)
    p = p / (jnp.sum(p, axis=-1, keepdims=True) + jnp.exp(sink - m))
    return jnp.einsum('bnhgqk,bnkhd->bnqhgd', p.astype(v.dtype), v)

def _gla(q, k, v, log_a, s0):
    B, T = q.shape[:2]
    nb = -(-T // GLA_BLOCK)
    pad = nb * GLA_BLOCK - T
    padf = lambda a: jnp.pad(a, ((0, 0), (0, pad), (0, 0), (0, 0)))
    blk = lambda a: padf(a).reshape(B, nb, GLA_BLOCK, *a.shape[2:]).astype(jnp.float32)
    qb, kb, vb, gb = blk(q), blk(k), blk(v), blk(log_a)
    cum = jnp.cumsum(gb, axis=2)
    last = cum[:, :, -1:]
    q_in = qb * jnp.exp(cum)
    k_in = kb * jnp.exp(-cum)
    k_out = kb * jnp.exp(last - cum)
    causal = jnp.tril(jnp.ones((GLA_BLOCK, GLA_BLOCK), jnp.float32))
    att = jnp.einsum('bnthd,bnshd->bnhts', q_in, k_in) * causal
    o_intra = jnp.einsum('bnhts,bnshv->bnthv', att, vb)
    dec = jnp.exp(last[:, :, 0])

    def step(S, xs):
        q_i, k_o, v_i, d_i = xs
        o = jnp.einsum('bthd,bhdv->bthv', q_i, S)
        S = S * d_i[..., None] + jnp.einsum('bshd,bshv->bhdv', k_o, v_i)
        return S, o

    xs = (jnp.moveaxis(q_in, 1, 0), jnp.moveaxis(k_out, 1, 0), jnp.moveaxis(vb, 1, 0), jnp.moveaxis(dec, 1, 0))
    S_T, o_inter = lax.scan(step, s0.astype(jnp.float32), xs)
    o = o_intra + jnp.moveaxis(o_inter, 0, 1)
    o = o.reshape(B, nb * GLA_BLOCK, *o.shape[3:])[:, :T]
    return o.astype(v.dtype), S_T

def _mix_projections(h, w_in, w_a2, b_a, g_q, g_k):
    B, T, _ = h.shape
    qa, ka, va, qb, kb, vb, rb, a1, ga, gb = jnp.split(h @ w_in, SPLIT_POINTS, axis=-1)
    qa = _rmsnorm(qa.reshape(B, T, N_HEADS_A, HEAD_DIM_A), g_q)
    ka = _rmsnorm(ka.reshape(B, T, N_KV_A, HEAD_DIM_A), g_k)
    va = va.reshape(B, T, N_KV_A, HEAD_DIM_A)
    qb = qb.reshape(B, T, N_HEADS_B, DK_B) * (DK_B ** -0.5)
    kb = kb.reshape(B, T, N_HEADS_B, DK_B)
    vb = vb.reshape(B, T, N_HEADS_B, DV_B)
    z = (a1 @ w_a2 + b_a).astype(jnp.float32)
    log_a = (jax.nn.log_sigmoid(z) / GATE_TAU).reshape(B, T, N_HEADS_B, DK_B)
    return qa, ka, va, qb, kb, vb, log_a, rb, ga, gb

def _merge(x, oa, ob, rb, ga, gb, g_ob, w_out):
    B, T, _ = x.shape
    ob = _rmsnorm(ob, g_ob).reshape(B, T, D_MODEL) * jax.nn.silu(rb)
    m = jax.nn.sigmoid(ga) * oa + jax.nn.sigmoid(gb) * ob
    return x + m @ w_out

def _ffn(x, g, w_gate, w_up, w_down):
    h = _rmsnorm(x, g)
    return x + (jax.nn.silu(h @ w_gate) * (h @ w_up)) @ w_down

def setup_inputs(seed: int = 0) -> dict:
    key = jax.random.key(seed)
    ks = jax.random.split(key, 20)
    nrm = lambda k, shape, s: jax.random.normal(k, shape, jnp.float32) * s
    L = min(WINDOW, PAST_LEN)
    return {
        "x_prompt": nrm(ks[0], (BATCH, SEQ, D_MODEL), 1.0),
        "x_sample": nrm(ks[1], (DEC_BATCH, DEC_SEQ, D_MODEL), 1.0),
        "cache_swa_k": nrm(ks[2], (DEPTH, DEC_BATCH, L, N_KV_A, HEAD_DIM_A), 1.0),
        "cache_swa_v": nrm(ks[3], (DEPTH, DEC_BATCH, L, N_KV_A, HEAD_DIM_A), 1.0),
        "state_gla": nrm(ks[4], (DEPTH, DEC_BATCH, N_HEADS_B, DK_B, DV_B), 0.5),
        "w_in": nrm(ks[5], (DEPTH, D_MODEL, P_IN), D_MODEL ** -0.5),
        "w_a2": nrm(ks[6], (DEPTH, GATE_RANK, WB_K), GATE_RANK ** -0.5),
        "b_a": nrm(ks[7], (DEPTH, WB_K), 0.1),
        "g_q": 1.0 + nrm(ks[8], (DEPTH, HEAD_DIM_A), 0.02),
        "g_k": 1.0 + nrm(ks[9], (DEPTH, HEAD_DIM_A), 0.02),
        "sinks": nrm(ks[10], (DEPTH, N_HEADS_A), 0.5),
        "g_ob": 1.0 + nrm(ks[11], (DEPTH, DV_B), 0.02),
        "w_out": nrm(ks[12], (DEPTH, D_MODEL, D_MODEL), D_MODEL ** -0.5),
        "g_mix": 1.0 + nrm(ks[13], (DEPTH, D_MODEL), 0.02),
        "g_ffn": 1.0 + nrm(ks[14], (DEPTH, D_MODEL), 0.02),
        "w_gate": nrm(ks[15], (DEPTH, D_MODEL, D_FF), D_MODEL ** -0.5),
        "w_up": nrm(ks[16], (DEPTH, D_MODEL, D_FF), D_MODEL ** -0.5),
        "w_down": nrm(ks[17], (DEPTH, D_FF, D_MODEL), D_FF ** -0.5),
    }

def reference(x_prompt, x_sample, cache_swa_k, cache_swa_v, state_gla, w_in, w_a2, b_a,
              g_q, g_k, sinks, g_ob, w_out, g_mix, g_ffn, w_gate, w_up, w_down):
    B, T, _ = x_prompt.shape
    nC = T // CHUNK
    qpos_p = jnp.arange(T, dtype=jnp.int32).reshape(nC, CHUNK)
    kpos_p = (jnp.arange(nC, dtype=jnp.int32)[:, None] * CHUNK - WINDOW
              + jnp.arange(BAND, dtype=jnp.int32)[None, :])
    bias_p = _alibi_band_bias(qpos_p, kpos_p)
    x = x_prompt
    pk, pv, ps = [], [], []
    for l in range(DEPTH):
        h = _rmsnorm(x, g_mix[l])
        qa, ka, va, qb, kb, vb, log_a, rb, ga, gb = _mix_projections(h, w_in[l], w_a2[l], b_a[l], g_q[l], g_k[l])
        oa = _sink_attend(qa.reshape(B, nC, CHUNK, N_KV_A, GROUP_A, HEAD_DIM_A),
                          _band(ka), _band(va), bias_p, sinks[l]).reshape(B, T, D_MODEL)
        ob, s_new = _gla(qb, kb, vb, log_a, jnp.zeros((B, N_HEADS_B, DK_B, DV_B), jnp.float32))
        x = _merge(x, oa, ob, rb, ga, gb, g_ob[l], w_out[l])
        x = _ffn(x, g_ffn[l], w_gate[l], w_up[l], w_down[l])
        pk.append(ka[:, T - WINDOW:])
        pv.append(va[:, T - WINDOW:])
        ps.append(s_new)
    y_prompt = x

    Bd, Tq, _ = x_sample.shape
    L = cache_swa_k.shape[2]
    qpos_s = (PAST_LEN + jnp.arange(Tq, dtype=jnp.int32))[None]
    kpos_s = (PAST_LEN - L + jnp.arange(L + Tq, dtype=jnp.int32))[None]
    bias_s = _alibi_band_bias(qpos_s, kpos_s)
    x = x_sample
    sk, sv, ss = [], [], []
    for l in range(DEPTH):
        h = _rmsnorm(x, g_mix[l])
        qa, ka, va, qb, kb, vb, log_a, rb, ga, gb = _mix_projections(h, w_in[l], w_a2[l], b_a[l], g_q[l], g_k[l])
        k_all = jnp.concatenate([cache_swa_k[l].astype(ka.dtype), ka], axis=1)[:, None]
        v_all = jnp.concatenate([cache_swa_v[l].astype(va.dtype), va], axis=1)[:, None]
        oa = _sink_attend(qa.reshape(Bd, 1, Tq, N_KV_A, GROUP_A, HEAD_DIM_A),
                          k_all, v_all, bias_s, sinks[l]).reshape(Bd, Tq, D_MODEL)
        ob, s_new = _gla(qb, kb, vb, log_a, state_gla[l])
        x = _merge(x, oa, ob, rb, ga, gb, g_ob[l], w_out[l])
        x = _ffn(x, g_ffn[l], w_gate[l], w_up[l], w_down[l])
        sk.append(ka)
        sv.append(va)
        ss.append(s_new)
    y_sample = x

    return (y_prompt, y_sample, jnp.stack(pk), jnp.stack(pv), jnp.stack(ps),
            jnp.stack(sk), jnp.stack(sv), jnp.stack(ss))


_drawn_inputs = setup_inputs


def setup_inputs(seed=0):
    import zlib

    import numpy as np

    out = dict(_drawn_inputs(seed))
    spreads = {}
    factors = {'g_q': 40.533, 'sinks': 200.0, 'g_ob': 8.0, 'g_ffn': 4.048}
    for name, (base, spread) in spreads.items():
        noise = np.random.default_rng([zlib.crc32(name.encode()), seed]).standard_normal(out[name].shape)
        drawn = base * np.exp(spread * noise) if base else spread * noise
        out[name] = __import__('jax').numpy.asarray(drawn.astype(out[name].dtype))
    for name, factor in factors.items():
        out[name] = (out[name] * factor).astype(out[name].dtype)
    return out
```

```python
from contextlib import ExitStack

import numpy as np

import concourse.bass as bass
from concourse import mybir

F32 = mybir.dt.float32
F32R = mybir.dt.float32r
I32 = mybir.dt.int32
ALU = mybir.AluOpType
ACT = mybir.ActivationFunctionType

P = 128
D = 1024
SEQ = 512
DEC = 32
T = SEQ + DEC
TH = T // 2
KC = D // P
EPS = 1e-6
NEG = -1e30
HEADS_A, KV_A, HD = 16, 4, 64
CHUNK, WINDOW = 64, 128
HEADS_B, DK, DV = 4, 128, 256
RANK = 16
TAU = 16.0
FF = 2816
O_QA, O_KA, O_VA = 0, 1024, 1280
O_QB, O_KB, O_VB, O_RB = 1536, 2048, 2560, 3584
O_A1, O_GA, O_GB = 4608, 4624, 5648
P_IN = 6672

RING = 4
TOK = [(j * P, P) for j in range(SEQ // P)] + [(SEQ, DEC)]
NJ = len(TOK)
SJ = NJ - 1


def input_tiles():
    tiles = [("a1", 0, [(O_A1, P)])]
    for h in range(HEADS_B):
        tiles += [("kB", h, [(O_KB + h * DK, P)]), ("qB", h, [(O_QB + h * DK, P)])]
        tiles += [("vB", 2 * h + f, [(O_VB + h * DV + f * P, P)]) for f in range(2)]
    tiles += [("kA", i, [(O_KA + i * P, P)]) for i in range(2)]
    tiles += [("vA", i, [(O_VA + i * P, P)]) for i in range(2)]
    tiles += [("qA", 4 * u + i, [(O_QA + (8 * u + i) * HD, HD), (O_QA + (8 * u + 4 + i) * HD, HD)])
              for u in range(2) for i in range(4)]
    tiles += [("ga", i, [(O_GA + i * P, P)]) for i in range(KC)]
    for i in range(KC):
        tiles += [("rb", i, [(O_RB + i * P, P)]), ("gb", i, [(O_GB + i * P, P)])]
    return tiles


IN_TILES = input_tiles()
N_IN = len(IN_TILES)
TILE_OF = {(kind, i): n for n, (kind, i, _) in enumerate(IN_TILES)}
OUT0 = N_IN
FF_GROUPS = [8, 8, 6]
GU0, DN0 = [], []
_n = OUT0 + KC
for _m in FF_GROUPS:
    GU0.append(_n)
    DN0.append(_n + 2 * _m)
    _n += 2 * _m + KC
N_TILES = _n
N_SMALL = 13

USES = [2 if kind in ("vB", "vA", "kA", "qA") else 1 for kind, _, _ in IN_TILES]
USES += [1] * (N_TILES - N_IN)
POST_TILES = [n for n in range(N_IN) if USES[n] == 2]


def uses_before(n):
    return sum(USES[m] for m in range(n % 2, n, 2))


UNITS = [(g, j, par) for g in range(KV_A) for j in range(NJ) for par in range(2)]
NU = len(UNITS)
UNIT0 = TILE_OF["ga", 2]
KEYS_OUT = TILE_OF["qA", 2]


def gla_tile(h, step):
    return 7 + 4 * h + (0, 1, 1, 2)[step]


def norm_order():
    order = []
    for n in range(N_IN + 1):
        if n >= 1 and IN_TILES[n - 1][0] in ("kA", "qA"):
            order.append(("post", n - 1))
        order += [("gla", h) for h in range(HEADS_B) if n == gla_tile(h, 3)]
    return order


NORMS = norm_order()


def unit_shape(u):
    g, j, par = UNITS[u]
    heads = (4 * g + par, 4 * g + 2 + par)
    lo = P if j == 0 else 0
    hi = P + DEC if j == SJ else 2 * P
    return g, j, par, heads, TOK[j][1], lo, hi


def mixer_program(nc, x_prompt, x_sample, cache_k, cache_v, state, w_in, w_a2, b_a, g_q, g_k, sinks,
                  g_ob, w_out, g_mix, g_ffn, w_gate, w_up, w_down,
                  y_prompt, y_sample, nk_p, nv_p, ns_p, nk_s, nv_s, ns_s):
    with ExitStack() as ctx:
        def sem(name):
            return ctx.enter_context(nc.semaphore(name))

        def tensor(where, name, shape, dt=F32):
            return where.enter_context(nc.sbuf_tensor(name, shape, dt))

        h_hi = tensor(ctx, "h_hi", [P, KC, T], F32R)
        h_lo = tensor(ctx, "h_lo", [P, KC, T], F32R)
        wraw = tensor(ctx, "wraw", [P, RING, KC, P])
        w_hi = tensor(ctx, "w_hi", [P, RING, KC, P], F32R)
        w_lo = tensor(ctx, "w_lo", [P, RING, KC, P], F32R)
        ident = tensor(ctx, "ident", [P, P])
        ones = tensor(ctx, "ones", [P, P])
        param = tensor(ctx, "param", [P, 24])
        eps = tensor(ctx, "eps", [P, 1])
        one = tensor(ctx, "one", [P, 1])
        sinkb = tensor(ctx, "sinkb", [P, HEADS_A])
        dist = tensor(ctx, "dist", [P, 2 * P])
        sq = tensor(ctx, "sq", [P, 2, T])
        rs = tensor(ctx, "rs", [P, T])
        rt = tensor(ctx, "rt", [P, T])
        rv = tensor(ctx, "rv", [P, T])
        G_MIX, G_FFN, B_A, G_OB, G_Q, G_K = 0, 8, 16, 20, 22, 23

        mix = ExitStack()
        obT = tensor(mix, "obT", [P, KC, T])
        kAT = tensor(mix, "kAT", [P, 2, T])
        kcT = tensor(mix, "kcT", [P, 2, P])
        vA = tensor(mix, "vA", [P, NJ, KV_A * HD])
        vc = tensor(mix, "vc", [P, KV_A * HD])
        raw = tensor(mix, "raw", [P, 2, T])
        kout = tensor(mix, "kout", [P, 2, 2 * P])

        gla = ExitStack()
        Sin = tensor(gla, "Sin", [P, HEADS_B, DV])
        wa2 = tensor(gla, "wa2", [RANK, HEADS_B * DK])
        prow = tensor(gla, "prow", [24, P])
        srow = tensor(gla, "srow", [1, HEADS_A])
        kc_tok = tensor(gla, "kc_tok", [P, KV_A * HD])
        cmask = tensor(gla, "cmask", [P, P])
        reset = tensor(gla, "reset", [P, NJ, P + 1])
        lab = tensor(gla, "lab", [P, NJ, P + 1])
        a1T = tensor(gla, "a1T", [RANK, T])
        CB = tensor(gla, "CB", [P, HEADS_B, NJ, P + 1])
        dec = tensor(gla, "dec", [P, NJ])
        att = tensor(gla, "att", [P, NJ, P])
        kot = tensor(gla, "kot", [P, NJ, P])
        S = tensor(gla, "S", [P, 3, DV])
        qT = tensor(gla, "qT", [P, 2, T])
        kT = tensor(gla, "kT", [P, 2, T])
        qL = tensor(gla, "qL", [P, T])
        kL = tensor(gla, "kL", [P, T])
        x32 = tensor(gla, "x32", [P, SEQ])
        x64 = tensor(gla, "x64", [P, SEQ])
        tA = tensor(gla, "tA", [P, NJ * P])
        tB = tensor(gla, "tB", [P, NJ * P])
        tC = tensor(gla, "tC", [P, NJ * P])
        vB = tensor(gla, "vB", [P, 2, NJ, DV])
        Ssmp = tensor(gla, "Ssmp", [P, 2, DV])
        Sfin = tensor(gla, "Sfin", [P, 2, DV])
        sqg = [qL, kL]
        gla.close()

        att_mem = ExitStack()
        gaT = tensor(att_mem, "gaT", [P, KC, T])
        qAT = tensor(att_mem, "qAT", [P, KC, T])
        bias = tensor(att_mem, "bias", [P, HEADS_A, 2 * P])
        prob = tensor(att_mem, "prob", [P, 2, 2, 2 * P])
        probT = tensor(att_mem, "probT", [P, 2, 2, 2, P])
        th = tensor(att_mem, "th", [P, 2, T])
        rbu = tensor(att_mem, "rbu", [P, T])
        mx = tensor(att_mem, "mx", [P, 2, 2])
        nm = tensor(att_mem, "nm", [P, 2, 2])
        sd = tensor(att_mem, "sd", [P, 2, 2])
        es = tensor(att_mem, "es", [P, 2, 2])
        sm = tensor(att_mem, "sm", [P, 2, 2])
        den = tensor(att_mem, "den", [P, 2, 2])
        rd = tensor(att_mem, "rd", [P, 2, 2])
        att_mem.close()

        rows = ExitStack()
        tensor(rows, "gap_gaT", [P, KC, T])
        x2T = tensor(rows, "x2T", [P, KC, T])
        ffn_work = ExitStack()
        xtok = tensor(rows, "xtok", [P, NJ, D])
        xTi = tensor(rows, "xTi", [P, 2, T])
        rows.close()
        tensor(ffn_work, "gap_rows", [P, 2 * KC, T])
        ft = tensor(ffn_work, "ft", [P, 2, T])
        fs = tensor(ffn_work, "fs", [P, 2, T])
        fa = tensor(ffn_work, "fa", [P, 2, T])
        ytok = tensor(ffn_work, "ytok", [P, 2, NJ, P])
        ffn_work.close()
        mix.close()

        mid_mem = ExitStack()
        mid_hi = tensor(mid_mem, "mid_hi", [P, 8, T], F32R)
        mid_lo = tensor(mid_mem, "mid_lo", [P, 8, T], F32R)
        mid_mem.close()

        G = [ctx.enter_context(nc.psum_tensor(f"G{s}", [P, 2 * 512], F32)) for s in range(2)]
        X = [ctx.enter_context(nc.psum_tensor(f"X{s}", [P, 2 * 512], F32)) for s in range(2)]
        XB = [X[b // 2][:, 512 * (b % 2):512 * (b % 2) + 512] for b in range(4)]

        def halves(ps):
            return ps[:, :].rearrange("p (b n) -> p b n", b=2)[:, :, 0:TH]

        def h2(ap):
            return ap.rearrange("p (b n) -> p b n", b=2)

        wload = [sem(f"wload{r}") for r in range(RING)]
        w_split = sem("w_split")
        pool_step = sem("pool_step")
        pool_turns = sem("pool_turns")
        gemm_done = sem("gemm_done")
        set_free = [sem("set_free0"), sem("set_free1")]
        post_done = sem("post_done")
        in_x = [sem(f"in_x{j}") for j in range(NJ)]
        in_small = sem("in_small")
        const_pool = sem("const_pool")
        const_dve = sem("const_dve")
        act_step = sem("act_step")
        dve_step = sem("dve_step")
        setup_pe = sem("setup_pe")
        param_ok = sem("param_ok")
        x_sq = sem("x_sq")
        x_scaled = sem("x_scaled")
        x_turned = sem("x_turned")
        h_hi_ok = sem("h_hi_ok")
        h_ok = sem("h_ok")
        r_ok = sem("r_ok")
        norm_done = sem("norm_done")
        z_done = sem("z_done")
        z_abs = sem("z_abs")
        z_free = sem("z_free")
        z_ln = sem("z_ln")
        cum_ok = sem("cum_ok")
        d_ok = sem("d_ok")
        e_ok = sem("e_ok")
        gla_in = sem("gla_in")
        gla_att = sem("gla_att")
        gla_masked = sem("gla_masked")
        gla_kot = sem("gla_kot")
        gla_upd = sem("gla_upd")
        gla_state = sem("gla_state")
        gla_out = sem("gla_out")
        gla_sq = sem("gla_sq")
        gla_ssq = sem("gla_ssq")
        gla_norm = sem("gla_norm")
        kt_done = sem("kt_done")
        kt_out = sem("kt_out")
        out_sem = sem("out_sem")
        s_out = [sem("s_out0"), sem("s_out1")]
        bias_ok = sem("bias_ok")
        qk_done = sem("qk_done")
        smax_ok = sem("smax_ok")
        exp_ok = sem("exp_ok")
        prob_ok = sem("prob_ok")
        pt_done = sem("pt_done")
        pt_copied = sem("pt_copied")
        pv_done = sem("pv_done")
        oa_ok = sem("oa_ok")
        tanh_ok = sem("tanh_ok")
        gb_used = sem("gb_used")
        m_ok = sem("m_ok")
        m_hi_ok = sem("m_hi_ok")
        m_lo_ok = sem("m_lo_ok")
        xr_in = sem("xr_in")
        xt_done = sem("xt_done")
        xt_ok = sem("xt_ok")
        x2_sq = sem("x2_sq")
        x2_ssq = sem("x2_ssq")
        f_in = sem("f_in")
        f_hi_ok = sem("f_hi_ok")
        f_ok = sem("f_ok")
        silu_ok = sem("silu_ok")
        mid_hi_ok = sem("mid_hi_ok")
        mid_ok = sem("mid_ok")
        yt_done = sem("yt_done")
        y_ok = sem("y_ok")
        y_out = [sem("y_out0"), sem("y_out1")]

        block = ctx.enter_context(nc.Block())

        @block.sync
        def _(sp):
            for n, (_kind, _i, runs) in enumerate(IN_TILES):
                if n >= RING:
                    sp.wait_ge(w_split, n - RING + 1)
                at = 0
                for col, width in runs:
                    src = w_in[0, :, col:col + width].rearrange("(k p) n -> p k n", p=P)
                    sp.dma_start(wraw[:, n % RING, :, at:at + width], src).then_inc(
                        wload[n % RING], 32 // len(runs))
                    at += width

            def stream(n0, turns, source, kc=KC):
                with sp.Fori(0, turns) as i:
                    for t in range(RING):
                        sp.wait_ge(w_split, i * RING + (n0 + t - RING + 1))
                        slot = (n0 + t) % RING
                        sp.dma_start(wraw[:, slot, 0:kc, :], source(i, t)).then_inc(wload[slot], 32)

            def block_of(w, row0, kc, col):
                return w[0, row0:row0 + kc * P, bass.ds(col, P)].rearrange("(k p) n -> p k n", p=P)

            stream(OUT0, KC // RING, lambda i, t: block_of(w_out, 0, KC, i * (RING * P) + t * P))
            f0 = 0
            for g, m in enumerate(FF_GROUPS):
                stream(GU0[g], 2 * m // RING, lambda i, t: block_of(
                    (w_gate, w_up)[t % 2], 0, KC, i * (2 * P) + (f0 + t // 2) * P))
                stream(DN0[g], KC // RING, lambda i, t: block_of(
                    w_down, f0 * P, m, i * (RING * P) + t * P), kc=m)
                f0 += m

        @block.gpsimd
        def _(pool):
            pool.memset(ident[:, :], 0.0).then_inc(pool_step, 1)
            pool.memset(cmask[:, :], 1.0).then_inc(pool_step, 1)
            pool.wait_ge(pool_step, 2)
            pool.affine_select(out=ident[:, :], in_=ident[:, :], compare_op=ALU.not_equal, fill=1.0,
                               base=0, pattern=[[-1, P]], channel_multiplier=1).then_inc(const_pool, 1)
            pool.iota(dist[:, :], pattern=[[-1, 2 * P]], base=P, channel_multiplier=1,
                      allow_small_or_imprecise_dtypes=True).then_inc(const_pool, 1)
            pool.affine_select(out=cmask[:, :], in_=cmask[:, :], compare_op=ALU.is_ge, fill=0.0,
                               base=0, pattern=[[1, P]], channel_multiplier=-1).then_inc(pool_step, 1)
            pool.wait_ge(pool_step, 3)
            cm = cmask[:, :].rearrange("p (b n) -> p b n", b=4)
            pool.affine_select(out=cm, in_=cm, compare_op=ALU.is_ge, fill=0.0, base=0,
                               pattern=[[-32, 4], [0, 32]], channel_multiplier=1).then_inc(const_pool, 1)

            def split(slot):
                pool.tensor_copy(w_hi[:, slot, :, :], wraw[:, slot, :, :]).then_inc(pool_step, 1)

            def rest(slot):
                pool.tensor_tensor(w_lo[:, slot, :, :], wraw[:, slot, :, :],
                                   w_hi[:, slot, :, :].bitcast(F32), ALU.subtract).then_inc(w_split, 1)

            for n in range(RING):
                pool.wait_ge(wload[n], 32)
                split(n)
                pool.wait_ge(pool_step, 4 + n)
                rest(n)
            with pool.Fori(1, N_TILES // RING) as i:
                for t in range(RING):
                    pool.wait_ge(wload[t], i * 32 + 32)
                    pool.wait_ge(gemm_done, i * RING + (t - RING + 1))
                    pool.sem_inc(pool_turns, 1)
                    split(t)
                    pool.wait_ge(pool_step, i * RING + (4 + t))
                    rest(t)
            for n in range(N_TILES // RING * RING, N_TILES):
                pool.wait_ge(wload[n % RING], 32 * (n // RING + 1))
                pool.wait_ge(gemm_done, n - RING + 1)
                split(n % RING)
                pool.wait_ge(pool_step, 4 + n)
                rest(n % RING)

        @block.tensor
        def _(pe):
            def chunk(slot, ps, kc, last, b_hi, b_lo):
                for b in range(2):
                    cols = slice(b * TH, (b + 1) * TH)
                    o = ps[:, 512 * b:512 * b + TH]
                    pe.matmul(o, w_hi[:, slot, kc, :], b_hi[:, kc, cols], start=(kc == 0), stop=False)
                    pe.matmul(o, w_hi[:, slot, kc, :], b_lo[:, kc, cols], start=False, stop=False)
                    mm = pe.matmul(o, w_lo[:, slot, kc, :], b_hi[:, kc, cols], start=False, stop=(kc == last))
                return mm

            pe.wait_ge(const_pool, 1)
            pe.wait_ge(const_dve, 1)
            pe.wait_ge(in_small, 16 * N_SMALL)
            pe.transpose(XB[0][:, 0:24], prow[:, :], ident[0:24, 0:24])
            pe.matmul(XB[1][:, 0:HEADS_A], ones[0:1, :], srow[:, :], start=True, stop=True)
            for u in range(2):
                mm = pe.transpose(XB[2][:, u * P:(u + 1) * P], kc_tok[:, u * P:(u + 1) * P], ident[:, :])
            mm.then_inc(setup_pe, 1)

            pe.wait_ge(param_ok, 1)
            pe.wait_ge(x_scaled, NJ)
            for c in range(KC):
                if c >= 2:
                    pe.wait_ge(h_ok, c - 1)
                for j, (t0, nt) in enumerate(TOK):
                    mm = pe.transpose(X[c % 2][:, t0:t0 + nt], xtok[0:nt, j, c * P:(c + 1) * P],
                                      ident[0:nt, 0:nt])
                mm.then_inc(x_turned, 1)

            def gate_logits(h):
                pe.wait_ge(set_free[0], 1)
                pe.wait_ge(h_ok, KC)
                if h >= 2:
                    pe.wait_ge(z_free, h - 1)
                for b in range(2):
                    mm = pe.matmul(X[h % 2][:, 512 * b:512 * b + TH], wa2[:, h * DK:(h + 1) * DK],
                                   a1T[:, b * TH:(b + 1) * TH], start=True, stop=True)
                mm.then_inc(z_done, 1)

            def second_use(n):
                ps = G[n % 2]
                pe.wait_ge(set_free[n % 2], uses_before(n) + 1)
                if IN_TILES[n][0] in ("vB", "vA"):
                    for j, (t0, nt) in enumerate(TOK):
                        mm = pe.transpose(ps[0:nt, j * P:(j + 1) * P], raw[:, n % 2, t0:t0 + nt], ident[:, :])
                else:
                    for b in range(2):
                        for r in (slice(0, HD), slice(HD, P)):
                            mm = pe.matmul(ps[r, 512 * b:512 * b + TH], ones[r, 0:HD],
                                           sq[r, n % 2, b * TH:(b + 1) * TH], start=True, stop=True)
                mm.then_inc(post_done, 1)

            def gla_scores(h):
                pe.wait_ge(gla_in, h + 1)
                pe.wait_ge(z_free, HEADS_B)
                if h >= 1:
                    pe.wait_ge(gla_norm, h)
                for c in range(NJ - 1):
                    k = slice(c * P, (c + 1) * P)
                    pe.matmul(XB[0][:, k], kL[:, k], qL[:, k], start=True, stop=True)
                    pe.matmul(XB[1][0:64, c * P + 64:(c + 1) * P], x64[:, c * P:c * P + 64],
                              x64[:, c * P + 64:(c + 1) * P], start=True, stop=True)
                    for a in (0, 64):
                        pe.matmul(XB[1][a:a + 32, c * P + a + 32:c * P + a + 64], x32[:, c * P + a:c * P + a + 32],
                                  x32[:, c * P + a + 32:c * P + a + 64], start=True, stop=True)
                    pe.transpose(XB[3][:, k], kT[:, h % 2, k], ident[:, :])
                s = slice(SEQ, T)
                pe.matmul(XB[2][0:DEC, 0:DEC], kL[:, s], qL[:, s], start=True, stop=True)
                pe.transpose(XB[2][0:DEC, P:2 * P], kT[:, h % 2, s], ident[:, :]).then_inc(gla_att, 1)

            def gla_updates(h):
                pe.wait_ge(gla_masked, h + 1)
                pe.wait_ge(gla_kot, h + 1)
                for f in range(2):
                    n = TILE_OF["vB", 2 * h + f]
                    pe.wait_ge(set_free[n % 2], uses_before(n) + 2)
                for c in range(NJ - 1):
                    pe.matmul(XB[c // 2][:, (c % 2) * DV:(c % 2 + 1) * DV], kot[:, c, :],
                              vB[:, h % 2, c, :], start=True, stop=True)
                pe.matmul(XB[3][:, 0:DV], kot[0:DEC, SJ, :], vB[0:DEC, h % 2, SJ, :],
                          start=True, stop=True).then_inc(gla_upd, 1)

            def gla_outputs(h):
                pe.wait_ge(gla_state, h + 1)
                for f in range(2):
                    v = slice(f * P, (f + 1) * P)
                    for c in range(NJ - 1):
                        k = slice(c * P, (c + 1) * P)
                        pe.matmul(XB[2 + f][:, k], vB[:, h % 2, c, v], att[:, c, :], start=True, stop=(c == 0))
                        if c >= 1:
                            pe.matmul(XB[2 + f][:, k], S[:, c - 1, v], qT[:, h % 2, k], start=False, stop=True)
                    pe.matmul(XB[f][:, 0:DEC], vB[0:DEC, h % 2, SJ, v], att[0:DEC, SJ, 0:DEC],
                              start=True, stop=False)
                    mm = pe.matmul(XB[f][:, 0:DEC], Sin[:, h, v], qT[:, h % 2, SEQ:T], start=False, stop=True)
                mm.then_inc(gla_out, 1)

            def gla_squares(h):
                pe.wait_ge(gla_sq, h + 1)
                for b in range(2):
                    for f in range(2):
                        mm = pe.matmul(X[0][:, 512 * b:512 * b + TH], ones[:, :],
                                       sqg[f][:, b * TH:(b + 1) * TH], start=(f == 0), stop=(f == 1))
                mm.then_inc(gla_ssq, 1)

            def keys_out():
                pe.wait_ge(norm_done, NORMS.index(("post", TILE_OF["kA", 1])) + 1)
                pe.wait_ge(gla_norm, HEADS_B)
                for u in range(2):
                    pe.transpose(XB[0][:, u * P:(u + 1) * P], kAT[:, u, SEQ - P:SEQ], ident[:, :])
                    mm = pe.transpose(XB[1][0:DEC, u * P:(u + 1) * P], kAT[:, u, SEQ:T], ident[:, :])
                mm.then_inc(kt_done, 1)

            def unit_scores(u):
                g, j, par, heads, nq, lo, hi = unit_shape(u)
                if u == 0:
                    pe.wait_ge(kt_out, 1)
                    pe.wait_ge(norm_done, len(NORMS))
                if u >= 2:
                    pe.wait_ge(smax_ok, u - 1)
                hf = slice((g % 2) * HD, (g % 2) * HD + HD)
                t0 = TOK[j][0]
                for a, head in enumerate(heads):
                    q = qAT[hf, 4 * (g // 2) + head % 4, t0:t0 + nq]
                    o = XB[u % 2][0:nq, a * 2 * P:(a + 1) * 2 * P]
                    if j == SJ:
                        pe.matmul(o[:, 0:P], q, kcT[hf, g // 2, :], start=True, stop=True)
                        mm = pe.matmul(o[:, P:P + DEC], q, kAT[hf, g // 2, SEQ:T], start=True, stop=True)
                    else:
                        mm = pe.matmul(o[:, lo:hi], q, kAT[hf, g // 2, t0 - P + lo:t0 - P + hi],
                                       start=True, stop=True)
                mm.then_inc(qk_done, 1)

            def unit_turn(u):
                g, j, par, heads, nq, lo, hi = unit_shape(u)
                pe.wait_ge(prob_ok, u + 1)
                if u >= 1:
                    pe.wait_ge(pt_copied, u)
                for a in range(2):
                    for kt in range(lo // P, 2):
                        nk = min(hi - kt * P, P)
                        c0 = (2 * a + kt) * P
                        mm = pe.transpose(XB[2][0:nk, c0:c0 + nq], prob[0:nq, u % 2, a, kt * P:kt * P + nk],
                                          ident[0:nq, 0:nq])
                mm.then_inc(pt_done, 1)

            def unit_values(u):
                g, j, par, heads, nq, lo, hi = unit_shape(u)
                pe.wait_ge(pt_copied, u + 1)
                if u >= 1:
                    pe.wait_ge(oa_ok, u)
                o = XB[3][par * HD:(par + 1) * HD, 0:2 * P].rearrange("p (a n) -> p a n", a=2)[:, :, 0:nq]
                for kt in range(lo // P, 2):
                    nk = min(hi - kt * P, P)
                    if j == SJ:
                        v = vc[:, g * HD:(g + 1) * HD] if kt == 0 else vA[0:nk, SJ, g * HD:(g + 1) * HD]
                    else:
                        v = vA[:, j - 1 + kt, g * HD:(g + 1) * HD]
                    mm = pe.matmul(o, v, probT[0:nk, u % 2, :, kt, 0:nq], start=(kt == lo // P), stop=(kt == 1))
                mm.then_inc(pv_done, 1)

            beside = {}

            def put(n, k, step, *args):
                beside.setdefault((n, k), []).append((step, args))

            for h in range(HEADS_B):
                put(1 + h, 3, gate_logits, h)
            for n in POST_TILES:
                put(n + 1, 3, second_use, n)
            for h in range(HEADS_B):
                put(gla_tile(h, 0), 3, gla_scores, h)
                put(gla_tile(h, 1), 1, gla_updates, h)
                put(gla_tile(h, 2), 6, gla_outputs, h)
                put(gla_tile(h, 3), 5, gla_squares, h)
            put(KEYS_OUT, 7, keys_out)
            for u in range(NU + 2):
                n, k = UNIT0 + u // 2, 3 + 4 * (u % 2)
                if u < NU:
                    put(n, k, unit_scores, u)
                if 1 <= u <= NU:
                    put(n, k, unit_turn, u - 1)
                if u >= 2:
                    put(n, k, unit_values, u - 2)

            for n in range(N_IN):
                pe.wait_ge(w_split, n + 1)
                if n >= 2:
                    pe.wait_ge(set_free[n % 2], uses_before(n))
                for kc in range(KC):
                    if n == 0:
                        pe.wait_ge(h_ok, kc + 1)
                    mm = chunk(n % RING, G[n % 2], kc, KC - 1, h_hi, h_lo)
                    if kc == KC - 1:
                        mm.then_inc(gemm_done, 1)
                    for step, args in beside.get((n, kc), ()):
                        step(*args)

            def residual_squares(i):
                pe.wait_ge(x2_sq, i + 1)
                for b in range(2):
                    mm = pe.matmul(X[1][:, 512 * b:512 * b + TH], ones[:, :],
                                   sq[:, i % 2, b * TH:(b + 1) * TH], start=(i == 0), stop=(i == KC - 1))
                mm.then_inc(x2_ssq, 1)

            for i in range(KC):
                n = OUT0 + i
                pe.wait_ge(w_split, n + 1)
                pe.wait_ge(set_free[n % 2], uses_before(n))
                for kc in range(KC):
                    if i == 0:
                        pe.wait_ge(m_lo_ok, kc + 1)
                    mm = chunk(n % RING, G[n % 2], kc, KC - 1, h_hi, h_lo)
                mm.then_inc(gemm_done, 1)
                if i == 0:
                    for j in range(NJ):
                        pe.wait_ge(in_x[j], 32)
                    pe.wait_ge(oa_ok, NU)
                else:
                    pe.wait_ge(xt_ok, i)
                for j, (t0, nt) in enumerate(TOK):
                    mm = pe.transpose(X[0][:, t0:t0 + nt], xtok[0:nt, j, i * P:(i + 1) * P], ident[0:nt, 0:nt])
                mm.then_inc(xt_done, 1)
                if i >= 1:
                    residual_squares(i - 1)
            residual_squares(KC - 1)

            def turn_rows(i):
                n = DN0[-1] + i
                pe.wait_ge(set_free[n % 2], uses_before(n) + 1)
                if i >= 2:
                    pe.wait_ge(y_ok, i - 1)
                for j, (t0, nt) in enumerate(TOK):
                    mm = pe.transpose(X[i % 2][0:nt, j * P:(j + 1) * P], x2T[:, i, t0:t0 + nt], ident[:, :])
                mm.then_inc(yt_done, 1)

            for g, m in enumerate(FF_GROUPS):
                with pe.Fori(0, 2 * m // RING) as i:
                    for t in range(RING):
                        n = GU0[g] + t
                        pe.wait_ge(w_split, i * RING + (n + 1))
                        pe.wait_ge(set_free[n % 2], i * 2 + uses_before(n))
                        for kc in range(KC):
                            if g == 0 and t == 0:
                                pe.wait_ge(f_ok, kc + 1)
                            mm = chunk(n % RING, G[n % 2], kc, KC - 1, h_hi, h_lo)
                        mm.then_inc(gemm_done, 1)
                before = sum(FF_GROUPS[:g])
                if g < len(FF_GROUPS) - 1:
                    with pe.Fori(0, KC // RING) as i:
                        for t in range(RING):
                            n = DN0[g] + t
                            pe.wait_ge(w_split, i * RING + (n + 1))
                            pe.wait_ge(set_free[n % 2], i * 2 + uses_before(n))
                            for kc in range(m):
                                if t == 0:
                                    pe.wait_ge(mid_ok, before + kc + 1)
                                mm = chunk(n % RING, G[n % 2], kc, m - 1, mid_hi, mid_lo)
                            mm.then_inc(gemm_done, 1)
                else:
                    for i in range(KC):
                        n = DN0[g] + i
                        pe.wait_ge(w_split, n + 1)
                        pe.wait_ge(set_free[n % 2], uses_before(n))
                        for kc in range(m):
                            if i == 0:
                                pe.wait_ge(mid_ok, before + kc + 1)
                            mm = chunk(n % RING, G[n % 2], kc, m - 1, mid_hi, mid_lo)
                        mm.then_inc(gemm_done, 1)
                        if i >= 1:
                            turn_rows(i - 1)
                    turn_rows(KC - 1)

        @block.scalar
        def _(act):
            steps = [0]

            def link(ins):
                steps[0] += 1
                ins.then_inc(act_step, 1)
                act.wait_ge(act_step, steps[0])

            def load_rows():
                for j, (t0, nt) in enumerate(TOK):
                    src = x_sample[0] if j == SJ else x_prompt[0, t0:t0 + nt, :]
                    act.dma_start(xtok[0:nt, j, :], src).then_inc(in_x[j], 16)

            load_rows()
            smalls = [
                (prow[G_MIX:G_MIX + 8, :], g_mix[0].rearrange("(r n) -> r n", n=P)),
                (prow[G_FFN:G_FFN + 8, :], g_ffn[0].rearrange("(r n) -> r n", n=P)),
                (prow[B_A:B_A + 4, :], b_a[0].rearrange("(r n) -> r n", n=P)),
                (prow[G_OB:G_OB + 2, :], g_ob[0].rearrange("(r n) -> r n", n=P)),
                (prow[G_Q:G_Q + 1, 0:HD], g_q), (prow[G_Q:G_Q + 1, HD:P], g_q),
                (prow[G_K:G_K + 1, 0:HD], g_k), (prow[G_K:G_K + 1, HD:P], g_k),
                (srow[:, :], sinks),
                (wa2[:, :], w_a2[0]),
                (kc_tok[:, :], cache_k[0, 0].rearrange("t h d -> t (h d)")),
                (vc[:, :], cache_v[0, 0].rearrange("t h d -> t (h d)")),
                (Sin[:, :, :], state[0, 0].rearrange("h k v -> k h v")),
            ]
            assert len(smalls) == N_SMALL
            for dst, src in smalls:
                act.dma_start(dst, src).then_inc(in_small, 16)

            act.wait_ge(const_dve, 3)
            for j, (t0, nt) in enumerate(TOK):
                act.wait_ge(in_x[j], 16)
                if j >= 2:
                    act.wait_ge(x_sq, j - 1)
                act.activation(G[j % 2][0:nt, :], xtok[0:nt, j, :], ACT.Square,
                               accum_out=rv[0:nt, j:j + 1]).then_inc(x_sq, 1)
            act.wait_ge(x_sq, NJ)
            link(act.activation(rs[:, 0:NJ], rv[:, 0:NJ], ACT.Ln, scale=1.0 / D, bias=eps[:, :]))
            act.activation(rt[:, 0:NJ], rs[:, 0:NJ], ACT.Exp, scale=-0.5).then_inc(r_ok, 1)
            act.wait_ge(param_ok, 1)
            for c in range(KC):
                act.wait_ge(x_turned, c + 1)
                act.activation(h_hi[:, c, :], X[c % 2][:, 0:T], ACT.Copy,
                               scale=param[:, G_MIX + c:G_MIX + c + 1]).then_inc(h_hi_ok, 1)

            def gate_logs(h):
                act.wait_ge(z_done, h + 1)
                if h >= 1:
                    act.wait_ge(z_ln, h)
                act.activation(h2(tB[:, 0:T]), halves(X[h % 2]), ACT.Abs,
                               bias=param[:, B_A + h:B_A + h + 1]).then_inc(z_abs, 1)
                act.wait_ge(z_abs, h + 1)
                link(act.activation(tB[:, 0:T], tB[:, 0:T], ACT.Exp, scale=-1.0))
                if h >= 1:
                    act.wait_ge(cum_ok, h)
                act.activation(tC[:, 0:T], tB[:, 0:T], ACT.Ln, bias=one[:, :]).then_inc(z_ln, 1)

            def gla_exps(h):
                if h >= 1:
                    act.wait_ge(gla_state, h)
                act.wait_ge(cum_ok, HEADS_B)
                act.activation(dec[:, :], CB[:, h, :, P], ACT.Exp, scale=1.0 / TAU).then_inc(e_ok, 1)
                act.wait_ge(d_ok, 5 * h + 1)
                act.activation(tB[:, 0:T], tA[:, 0:T], ACT.Exp, scale=1.0 / TAU).then_inc(e_ok, 1)
                act.activation(tC[:, 0:T], tA[:, 0:T], ACT.Exp, scale=-1.0 / TAU).then_inc(e_ok, 1)
                act.wait_ge(d_ok, 5 * h + 2)
                act.activation(tB[:, 0:SEQ], tA[:, 0:SEQ], ACT.Exp, scale=1.0 / TAU).then_inc(e_ok, 1)
                act.wait_ge(d_ok, 5 * h + 3)
                act.activation(tC[:, 0:SEQ], tA[:, 0:SEQ], ACT.Exp, scale=1.0 / TAU).then_inc(e_ok, 1)
                act.wait_ge(d_ok, 5 * h + 4)
                act.activation(tB[:, 0:T], tA[:, 0:T], ACT.Exp, scale=1.0 / TAU).then_inc(e_ok, 1)
                act.wait_ge(d_ok, 5 * h + 5)
                act.activation(tC[:, :].rearrange("p (c n) -> p c n", n=P), CB[:, h, :, 1:P + 1],
                               ACT.Exp, scale=1.0 / TAU).then_inc(e_ok, 1)

            def gla_copy_keys(h):
                act.wait_ge(gla_att, h + 1)
                link(act.activation(kot[:, 0:4, :], XB[3].rearrange("p (c n) -> p c n", c=4), ACT.Copy))
                act.activation(kot[0:DEC, SJ, :], XB[2][0:DEC, P:2 * P], ACT.Copy).then_inc(gla_kot, 1)

            def gla_copy_out(h):
                act.wait_ge(gla_out, h + 1)
                for f in range(2):
                    link(act.activation(obT[:, 2 * h + f, 0:SEQ], XB[2 + f], ACT.Copy))
                    link(act.activation(obT[:, 2 * h + f, SEQ:T], XB[f][:, 0:DEC], ACT.Copy))
                link(act.activation(sqg[0][:, :], obT[:, 2 * h, :], ACT.Square))
                act.activation(sqg[1][:, :], obT[:, 2 * h + 1, :], ACT.Square).then_inc(gla_sq, 1)

            def root(k, ps, scale):
                if k >= 1:
                    act.wait_ge(norm_done, k)
                link(act.activation(h2(rs[:, :]), halves(ps), ACT.Ln, scale=scale, bias=eps[:, :]))
                act.activation(rt[:, :], rs[:, :], ACT.Exp, scale=-0.5).then_inc(r_ok, 1)

            def free_raw(n):
                last = [m for m in POST_TILES if m < n and m % 2 == n % 2]
                if last and IN_TILES[last[-1]][0] in ("kA", "qA"):
                    act.wait_ge(norm_done, NORMS.index(("post", last[-1])) + 1)
                elif last:
                    act.wait_ge(post_done, POST_TILES.index(last[-1]) + 1)

            def read_out(n):
                kind, i, _ = IN_TILES[n]
                s = n % 2
                ps = halves(G[s])
                act.wait_ge(gemm_done, n + 1)
                if kind == "a1":
                    act.activation(h2(a1T[:, :]), ps[0:RANK], ACT.Copy).then_inc(set_free[s], 1)
                elif kind in ("kB", "qB"):
                    if i >= 2:
                        act.wait_ge(gla_out, i - 1)
                    dst = (kT if kind == "kB" else qT)[:, i % 2, :]
                    act.activation(h2(dst), ps, ACT.Copy,
                                   scale=1.0 if kind == "kB" else float(DK) ** -0.5).then_inc(set_free[s], 1)
                elif kind in ("vB", "vA"):
                    free_raw(n)
                    act.activation(h2(raw[:, s, :]), ps, ACT.Copy).then_inc(set_free[s], 1)
                elif kind in ("kA", "qA"):
                    free_raw(n)
                    link(act.activation(h2(sq[:, s, :]), ps, ACT.Square))
                    act.activation(h2(raw[:, s, :]), ps, ACT.Copy).then_inc(set_free[s], 1)
                elif kind == "ga":
                    if i == 0:
                        act.wait_ge(gla_norm, HEADS_B)
                        for r in range(2):
                            act.wait_ge(s_out[r], 32 * HEADS_B // 2)
                    act.activation(h2(gaT[:, i, :]), ps, ACT.Tanh, scale=0.5).then_inc(set_free[s], 1)
                elif kind == "rb":
                    if i >= 1:
                        act.wait_ge(set_free[s], uses_before(n))
                    act.activation(h2(th[:, 0, :]), ps, ACT.Tanh, scale=0.5).then_inc(tanh_ok, 1)
                elif kind == "gb":
                    if i >= 1:
                        act.wait_ge(gb_used, i)
                    act.activation(h2(th[:, 1, :]), ps, ACT.Tanh, scale=0.5).then_inc(set_free[s], 1)

            def keys_out():
                act.wait_ge(kt_done, 1)
                link(act.activation(kout[:, 0, :], XB[0][:, 0:2 * P], ACT.Copy))
                act.activation(kout[0:DEC, 1, :], XB[1][0:DEC, 0:2 * P], ACT.Copy).then_inc(kt_out, 1)
                act.wait_ge(kt_out, 1)
                act.dma_start(nk_p[0, 0].rearrange("t h d -> t (h d)"), kout[:, 0, :]).then_inc(out_sem, 16)
                act.dma_start(nk_s[0, 0].rearrange("t h d -> t (h d)"), kout[0:DEC, 1, :]).then_inc(out_sem, 16)
                for i in range(2):
                    n = TILE_OF["vA", i]
                    act.wait_ge(set_free[n % 2], uses_before(n) + 2)
                act.dma_start(nv_p[0, 0].rearrange("t h d -> t (h d)"), vA[:, SJ - 1, :]).then_inc(out_sem, 16)
                act.dma_start(nv_s[0, 0].rearrange("t h d -> t (h d)"), vA[0:DEC, SJ, :]).then_inc(out_sem, 16)

            def states_out(h):
                act.wait_ge(gla_state, h + 1)
                act.dma_start(ns_p[0, 0, h], Sfin[:, h % 2, :]).then_inc(s_out[h % 2], 16)
                act.dma_start(ns_s[0, 0, h], Ssmp[:, h % 2, :]).then_inc(s_out[h % 2], 16)

            def unit_exp(u):
                g, j, par, heads, nq, lo, hi = unit_shape(u)
                s = u % 2
                act.wait_ge(smax_ok, u + 1)
                for a in range(2):
                    link(act.activation(prob[0:nq, s, a, lo:hi], prob[0:nq, s, a, lo:hi], ACT.Exp,
                                        bias=nm[0:nq, s, a:a + 1], accum_out=sm[0:nq, s, a:a + 1]))
                act.activation(es[0:nq, s, :], sd[0:nq, s, :], ACT.Exp).then_inc(exp_ok, 1)

            def unit_copy(u):
                g, j, par, heads, nq, lo, hi = unit_shape(u)
                act.wait_ge(pt_done, u + 1)
                if u >= 2:
                    act.wait_ge(pv_done, u - 1)
                src = XB[2].rearrange("p (a k n) -> p a k n", a=2, k=2)
                if j < SJ and lo == 0:
                    act.activation(probT[:, u % 2, :, :, :], src, ACT.Copy).then_inc(pt_copied, 1)
                    return
                for kt in range(lo // P, 2):
                    nk = min(hi - kt * P, P)
                    ins = act.activation(probT[0:nk, u % 2, :, kt, 0:nq], src[0:nk, :, kt, 0:nq], ACT.Copy)
                    if kt == 0:
                        link(ins)
                ins.then_inc(pt_copied, 1)

            def slot(u):
                if 0 <= u < NU:
                    unit_exp(u)
                if 1 <= u <= NU:
                    unit_copy(u - 1)

            for n in range(N_IN):
                if 1 <= n <= HEADS_B:
                    gate_logs(n - 1)
                if n >= 1 and IN_TILES[n - 1][0] in ("kA", "qA"):
                    act.wait_ge(post_done, POST_TILES.index(n - 1) + 1)
                    root(NORMS.index(("post", n - 1)), G[(n - 1) % 2], 1.0 / HD)
                for h in range(HEADS_B):
                    if n == gla_tile(h, 0):
                        gla_copy_keys(h)
                slot(2 * (n - UNIT0))
                read_out(n)
                slot(2 * (n - UNIT0) + 1)
                for h in range(HEADS_B):
                    if n == gla_tile(h, 2):
                        states_out(h)
                        gla_copy_out(h)
                    if n == gla_tile(h, 3):
                        act.wait_ge(gla_ssq, h + 1)
                        root(NORMS.index(("gla", h)), X[0], 1.0 / DV)
                for h in range(HEADS_B):
                    if n == gla_tile(h, 0) - 2:
                        gla_exps(h)
                if n == KEYS_OUT:
                    keys_out()

            act.wait_ge(gemm_done, N_IN)
            for i in range(KC):
                act.wait_ge(m_ok, i + 1)
                act.activation(h_hi[:, i, :], obT[:, i, :], ACT.Copy).then_inc(m_hi_ok, 1)
                if i == 0:
                    act.wait_ge(oa_ok, NU)
                    act.wait_ge(gb_used, KC)
                    load_rows()
            for i in range(KC):
                n = OUT0 + i
                act.wait_ge(xt_done, i + 1)
                if i >= 2:
                    act.wait_ge(set_free[n % 2], uses_before(n))
                act.activation(xTi[:, i % 2, :], X[0][:, 0:T], ACT.Copy).then_inc(xt_ok, 1)
                act.wait_ge(set_free[n % 2], uses_before(n) + 1)
                if i >= 2:
                    act.wait_ge(x2_ssq, i - 1)
                act.activation(sq[:, i % 2, :], x2T[:, i, :], ACT.Square).then_inc(x2_sq, 1)
            act.wait_ge(x2_ssq, KC)
            root(len(NORMS), X[1], 1.0 / D)
            for c in range(KC):
                act.wait_ge(f_in, c + 1)
                act.activation(h_hi[:, c, :], fs[:, c % 2, :], ACT.Copy).then_inc(f_hi_ok, 1)

            act.wait_ge(out_sem, 64)
            before = 0
            for g, m in enumerate(FF_GROUPS):
                with act.Fori(0, m // 2) as i:
                    for r in range(2):
                        n = GU0[g] + 2 * r
                        act.wait_ge(gemm_done, i * RING + (n + 1))
                        act.activation(h2(ft[:, r, :]), halves(G[n % 2]), ACT.Tanh, scale=0.5)\
                            .then_inc(silu_ok, 1)
                        act.wait_ge(set_free[(n + 1) % 2], i * 2 + (uses_before(n + 1) + 1))
                        act.activation(mid_hi[:, bass.ds(i * 2 + r, 1), :], fa[:, r:r + 1, :], ACT.Copy)\
                            .then_inc(mid_hi_ok, 1)
                before += m

            for i in range(KC):
                act.wait_ge(yt_done, i + 1)
                if i >= 2:
                    act.wait_ge(y_out[i % 2], 32 * (i // 2))
                link(act.activation(ytok[:, i % 2, 0:4, :], X[i % 2][:, 0:SEQ].rearrange("p (j n) -> p j n", n=P),
                                    ACT.Copy))
                act.activation(ytok[0:DEC, i % 2, SJ, :], X[i % 2][0:DEC, SEQ:SEQ + P], ACT.Copy).then_inc(y_ok, 1)
                act.wait_ge(y_ok, i + 1)
                c = slice(i * P, (i + 1) * P)
                act.dma_start(y_prompt[0, :, c].rearrange("(j p) n -> p j n", p=P), ytok[:, i % 2, 0:4, :])\
                    .then_inc(y_out[i % 2], 16)
                act.dma_start(y_sample[0, :, c], ytok[0:DEC, i % 2, SJ, :]).then_inc(y_out[i % 2], 16)
            for s in range(2):
                act.wait_ge(y_out[s], 32 * KC // 2)

        @block.vector
        def _(dve):
            steps = [0]

            def link(ins):
                steps[0] += 1
                ins.then_inc(dve_step, 1)
                dve.wait_ge(dve_step, steps[0])

            def refine(x, r, t):
                link(dve.tensor_tensor(t, x, r, ALU.mult))
                link(dve.tensor_tensor(t, t, r, ALU.mult))
                link(dve.tensor_scalar(t, t, -0.5, 1.5, ALU.mult, ALU.add))
                link(dve.tensor_tensor(r, r, t, ALU.mult))

            dve.memset(ones[:, :], 1.0).then_inc(const_dve, 1)
            dve.memset(rv[:, 0:NJ], 1.0).then_inc(const_dve, 1)
            link(dve.memset(one[:, :], 1.0))
            dve.memset(eps[:, :], EPS).then_inc(const_dve, 1)
            link(dve.memset(lab[:, :, :], 0.0))
            link(dve.memset(reset[:, :, :], 1.0))
            link(dve.memset(reset[:, :, 0], 0.0))

            dve.wait_ge(setup_pe, 1)
            link(dve.tensor_copy(param[:, :], XB[0][:, 0:24]))
            link(dve.tensor_scalar(param[:, G_Q:G_Q + 1], param[:, G_Q:G_Q + 1], HD ** -0.5, None, ALU.mult))
            link(dve.tensor_scalar(param[:, G_OB:G_OB + 2], param[:, G_OB:G_OB + 2], 0.25, None, ALU.mult))
            link(dve.tensor_copy(sinkb[:, :], XB[1][:, 0:HEADS_A]))
            dve.tensor_copy(kcT[:, :, :], XB[2][:, 0:2 * P].rearrange("p (u n) -> p u n", u=2)).then_inc(param_ok, 1)

            dve.wait_ge(r_ok, 1)
            link(dve.tensor_scalar(rv[:, 0:NJ], rv[:, 0:NJ], 1.0 / D, EPS, ALU.mult, ALU.add))
            refine(rv[:, 0:NJ], rt[:, 0:NJ], rs[:, 0:NJ])
            for j, (t0, nt) in enumerate(TOK):
                dve.tensor_scalar(xtok[0:nt, j, :], xtok[0:nt, j, :], rt[0:nt, j:j + 1], None, ALU.mult)\
                    .then_inc(x_scaled, 1)
            for c in range(KC):
                dve.wait_ge(h_hi_ok, c + 1)
                dve.scalar_tensor_tensor(out=h_lo[:, c, :], in0=X[c % 2][:, 0:T],
                                         scalar=param[:, G_MIX + c:G_MIX + c + 1],
                                         in1=h_hi[:, c, :].bitcast(F32), op0=ALU.mult, op1=ALU.subtract)\
                    .then_inc(h_ok, 1)
            dve.wait_ge(const_pool, 2)
            link(dve.tensor_scalar(rs[:, 0:2 * P], dist[:, :], -1.0, None, ALU.mult))
            link(dve.tensor_tensor(dist[:, :], dist[:, :], rs[:, 0:2 * P], ALU.max))

            def gate_sums(h):
                dve.wait_ge(z_abs, h + 1)
                if h >= 1:
                    dve.wait_ge(cum_ok, h)
                dve.tensor_scalar(h2(tA[:, 0:T]), halves(X[h % 2]), param[:, B_A + h:B_A + h + 1], 0.0,
                                  ALU.add, ALU.min).then_inc(z_free, 1)
                dve.wait_ge(z_free, h + 1)
                dve.wait_ge(z_ln, h + 1)
                chunks = lambda t: t[:, 0:SEQ].rearrange("p (c n) -> p c n", n=P)
                link(dve.tensor_tensor(lab[:, 0:4, 1:P + 1], chunks(tA), chunks(tC), ALU.subtract))
                link(dve.tensor_tensor(lab[:, SJ, 1:DEC + 1], tA[:, SEQ:T], tC[:, SEQ:T], ALU.subtract))
                dve.tensor_tensor_scan(CB[:, h, :, :].rearrange("p c n -> p (c n)"),
                                       reset[:, :, :].rearrange("p c n -> p (c n)"),
                                       lab[:, :, :].rearrange("p c n -> p (c n)"), 0.0,
                                       ALU.mult, ALU.add).then_inc(cum_ok, 1)

            def gla_inputs(h):
                for kind in ("kB", "qB"):
                    n = TILE_OF[kind, h]
                    dve.wait_ge(set_free[n % 2], uses_before(n) + 1)
                if h >= 1:
                    dve.wait_ge(gla_ssq, h)
                q, k = qT[:, h % 2, :], kT[:, h % 2, :]
                dve.wait_ge(cum_ok, HEADS_B)
                c = CB[:, h, :, 1:P + 1]

                def by(step, ap, count):
                    return ap.rearrange("p c (b n) -> p c b n", n=step)[:, 0:count]

                mid = CB[:, h, :, 16:P:32].unsqueeze(3).broadcast_to([P, NJ, 4, 32])
                dve.tensor_tensor(by(32, tA[:, :].rearrange("p (c n) -> p c n", n=P), NJ), by(32, c, NJ), mid,
                                  ALU.subtract).then_inc(d_ok, 1)
                dve.wait_ge(e_ok, 7 * h + 2)
                link(dve.tensor_tensor(qL[:, :], q, tB[:, 0:T], ALU.mult))
                dve.wait_ge(e_ok, 7 * h + 3)
                link(dve.tensor_tensor(kL[:, :], k, tC[:, 0:T], ALU.mult))

                def halves_of(w, ap):
                    v = ap.rearrange("p (b a n) -> p b a n", a=2, n=w // 2)
                    return v[:, :, 0], v[:, :, 1]

                def from_boundary(w):
                    d1, d2 = halves_of(w, tA[:, 0:SEQ])
                    nb = P // w
                    cc = CB[:, h, 0:4, 1:P + 1].rearrange("p c (b n) -> p c b n", n=w)
                    edge = CB[:, h, 0:4, w // 2:P:w].unsqueeze(3).broadcast_to([P, 4, nb, w // 2])
                    d1 = d1.rearrange("p (c b) n -> p c b n", b=nb)
                    d2 = d2.rearrange("p (c b) n -> p c b n", b=nb)
                    link(dve.tensor_tensor(d1, edge, cc[:, :, :, 0:w // 2], ALU.subtract))
                    dve.tensor_tensor(d2, cc[:, :, :, w // 2:w], edge, ALU.subtract).then_inc(d_ok, 1)

                def decayed(w, x, t):
                    x1, x2 = halves_of(w, x[:, :])
                    e1, e2 = halves_of(w, t[:, 0:SEQ])
                    k1, _ = halves_of(w, k[:, 0:SEQ])
                    _, q2 = halves_of(w, q[:, 0:SEQ])
                    link(dve.tensor_tensor(x1, k1, e1, ALU.mult))
                    link(dve.tensor_tensor(x2, q2, e2, ALU.mult))

                from_boundary(64)
                dve.wait_ge(e_ok, 7 * h + 4)
                from_boundary(P)
                decayed(64, x32, tB)
                dve.wait_ge(e_ok, 7 * h + 5)
                last = CB[:, h, :, P:P + 1].broadcast_to([P, NJ, P])
                dve.tensor_tensor(tA[:, :].rearrange("p (c n) -> p c n", n=P), last, c, ALU.subtract)\
                    .then_inc(d_ok, 1)
                x1, x2 = halves_of(P, x64[:, :])
                e1, e2 = halves_of(P, tC[:, 0:SEQ])
                link(dve.tensor_tensor(x1, halves_of(P, k[:, 0:SEQ])[0], e1, ALU.mult))
                dve.tensor_tensor(x2, halves_of(P, q[:, 0:SEQ])[1], e2, ALU.mult).then_inc(d_ok, 1)
                dve.wait_ge(d_ok, 5 * h + 5)
                dve.wait_ge(e_ok, 7 * h + 6)
                link(dve.tensor_tensor(k, k, tB[:, 0:T], ALU.mult))
                dve.wait_ge(e_ok, 7 * h + 7)
                dve.tensor_tensor(q, q, tC[:, 0:T], ALU.mult).then_inc(gla_in, 1)

            def gla_mask(h):
                dve.wait_ge(gla_att, h + 1)
                b4 = lambda ap: ap.rearrange("p (c n) -> p c n", n=P)
                link(dve.tensor_tensor(att[:, 0:4, :], b4(XB[0]),
                                       cmask[:, :].unsqueeze(1).broadcast_to([P, 4, P]), ALU.mult))
                link(dve.tensor_copy(att[0:64, 0:4, 64:P], b4(XB[1])[0:64, :, 64:P]))
                for a in (0, 64):
                    link(dve.tensor_copy(att[a:a + 32, 0:4, a + 32:a + 64], b4(XB[1])[a:a + 32, :, a + 32:a + 64]))
                dve.wait_ge(gla_kot, h + 1)
                dve.tensor_tensor(att[0:DEC, SJ, 0:DEC], XB[2][0:DEC, 0:DEC], cmask[0:DEC, 0:DEC],
                                  ALU.mult).then_inc(gla_masked, 1)

            def gla_states(h):
                dve.wait_ge(gla_upd, h + 1)
                if h >= 2:
                    dve.wait_ge(s_out[h % 2], 32 * (h // 2))
                add = lambda c: XB[c // 2][:, (c % 2) * DV:(c % 2 + 1) * DV]
                link(dve.tensor_copy(S[:, 0, :], add(0)))
                for c in range(1, 4):
                    dst = S[:, c, :] if c < 3 else Sfin[:, h % 2, :]
                    link(dve.scalar_tensor_tensor(out=dst, in0=S[:, c - 1, :], scalar=dec[:, c:c + 1],
                                                  in1=add(c), op0=ALU.mult, op1=ALU.add))
                dve.scalar_tensor_tensor(out=Ssmp[:, h % 2, :], in0=Sin[:, h, :], scalar=dec[:, SJ:SJ + 1],
                                         in1=XB[3][:, 0:DV], op0=ALU.mult, op1=ALU.add).then_inc(gla_state, 1)

            def mean_square(k, ps, scale, read):
                dve.wait_ge(r_ok, k + 2)
                dve.tensor_scalar(h2(rv[:, :]), halves(ps), scale, EPS, ALU.mult, ALU.add).then_inc(*read)

            def gla_norms(h):
                k = NORMS.index(("gla", h))
                mean_square(k, X[0], 1.0 / DV, (gla_norm, 1))
                dve.wait_ge(gla_norm, h + 1)
                refine(rv[:, :], rt[:, :], rs[:, :])
                for f in range(2):
                    o = obT[:, 2 * h + f, :]
                    ins = dve.scalar_tensor_tensor(out=o, in0=o, scalar=param[:, G_OB + f:G_OB + f + 1],
                                                   in1=rt[:, :], op0=ALU.mult, op1=ALU.mult)
                    if f == 0:
                        link(ins)
                ins.then_inc(norm_done, 1)

            def second_use(n):
                kind, i, _ = IN_TILES[n]
                dve.wait_ge(post_done, POST_TILES.index(n) + 1)
                ps, s = G[n % 2], n % 2
                if kind in ("vB", "vA"):
                    dst = vB[:, (i // 2) % 2] if kind == "vB" else vA
                    f = slice((i % 2) * P, (i % 2) * P + P)
                    link(dve.tensor_copy(dst[:, 0:4, f], ps[:, 0:SEQ].rearrange("p (j n) -> p j n", n=P)))
                    dve.tensor_copy(dst[0:DEC, SJ, f], ps[0:DEC, SEQ:SEQ + P]).then_inc(set_free[s], 1)
                else:
                    mean_square(NORMS.index(("post", n)), ps, 1.0 / HD, (set_free[s], 1))
                    dve.wait_ge(set_free[s], uses_before(n) + 2)
                    refine(rv[:, :], rt[:, :], rs[:, :])
                    dst, g = (kAT, G_K) if kind == "kA" else (qAT, G_Q)
                    dve.scalar_tensor_tensor(out=dst[:, i, :], in0=raw[:, s, :], scalar=param[:, g:g + 1],
                                             in1=rt[:, :], op0=ALU.mult, op1=ALU.mult).then_inc(norm_done, 1)

            def biases():
                for r in range(2):
                    dve.wait_ge(s_out[r], 32 * HEADS_B // 2)
                dve.wait_ge(gla_ssq, HEADS_B)
                for h in range(HEADS_A):
                    slope = float(np.float32(2.0 ** (-8.0 * (h + 1) / HEADS_A)))
                    link(dve.tensor_scalar(bias[:, h, :], dist[:, :], -slope, None, ALU.mult))
                link(dve.memset(bias[0:CHUNK, :, 2 * P - CHUNK:2 * P], NEG))
                dve.memset(bias[CHUNK:P, :, 0:CHUNK], NEG).then_inc(bias_ok, 1)
                dve.wait_ge(bias_ok, 1)

            def unit_max(u):
                g, j, par, heads, nq, lo, hi = unit_shape(u)
                s = u % 2
                dve.wait_ge(qk_done, u + 1)
                if u >= 2:
                    dve.wait_ge(pt_done, u - 1)
                for a, head in enumerate(heads):
                    link(dve.tensor_tensor_reduce(
                        prob[0:nq, s, a, lo:hi], XB[s][0:nq, a * 2 * P + lo:a * 2 * P + hi],
                        bias[0:nq, head, lo:hi], 1.0, NEG, ALU.add, ALU.max, mx[0:nq, s, a:a + 1]))
                sink = sinkb[0:nq, heads[0]:heads[1] + 1:2]
                link(dve.tensor_tensor(mx[0:nq, s, :], mx[0:nq, s, :], sink, ALU.max))
                link(dve.tensor_scalar(nm[0:nq, s, :], mx[0:nq, s, :], -1.0, None, ALU.mult))
                dve.tensor_tensor(sd[0:nq, s, :], sink, nm[0:nq, s, :], ALU.add).then_inc(smax_ok, 1)

            def unit_scale(u):
                g, j, par, heads, nq, lo, hi = unit_shape(u)
                s = u % 2
                dve.wait_ge(exp_ok, u + 1)
                link(dve.tensor_tensor(den[0:nq, s, :], sm[0:nq, s, :], es[0:nq, s, :], ALU.add))
                link(dve.reciprocal(rd[0:nq, s, :], den[0:nq, s, :]))
                for a in range(2):
                    o = prob[0:nq, s, a, lo:hi]
                    ins = dve.tensor_scalar(o, o, rd[0:nq, s, a:a + 1], 0.5, ALU.mult, ALU.mult)
                    if a == 0:
                        link(ins)
                ins.then_inc(prob_ok, 1)

            def unit_out(u):
                g, j, par, heads, nq, lo, hi = unit_shape(u)
                dve.wait_ge(pv_done, u + 1)
                for i in (2 * g, 2 * g + 1):
                    n = TILE_OF["ga", i]
                    dve.wait_ge(set_free[n % 2], uses_before(n) + 1)
                r = slice(par * HD, (par + 1) * HD)
                o = gaT[r, 2 * g:2 * g + 2, TOK[j][0]:TOK[j][0] + nq]
                src = XB[3][r, 0:2 * P].rearrange("p (a n) -> p a n", a=2)[:, :, 0:nq]
                dve.scalar_tensor_tensor(out=o, in0=o, scalar=1.0, in1=src, op0=ALU.add, op1=ALU.mult)\
                    .then_inc(oa_ok, 1)

            def slot(u):
                if 1 <= u <= NU:
                    unit_scale(u - 1)
                if 0 <= u < NU:
                    unit_max(u)
                if 2 <= u <= NU + 1:
                    unit_out(u - 2)

            def gates(n):
                kind, i, _ = IN_TILES[n]
                s = n % 2
                if kind == "rb":
                    dve.wait_ge(tanh_ok, i + 1)
                    dve.scalar_tensor_tensor(out=h2(rbu[:, :]), in0=h2(th[:, 0, :]), scalar=1.0,
                                             in1=halves(G[s]), op0=ALU.add, op1=ALU.mult)\
                        .then_inc(set_free[s], 1)
                    dve.wait_ge(set_free[s], uses_before(n) + 1)
                elif kind == "gb":
                    dve.wait_ge(set_free[s], uses_before(n) + 1)
                    dve.scalar_tensor_tensor(out=rbu[:, :], in0=th[:, 1, :], scalar=1.0, in1=rbu[:, :],
                                             op0=ALU.add, op1=ALU.mult).then_inc(gb_used, 1)
                    dve.wait_ge(gb_used, i + 1)
                    link(dve.tensor_tensor(obT[:, i, :], obT[:, i, :], rbu[:, :], ALU.mult))

            def merge(i):
                dve.wait_ge(oa_ok, 2 * NJ * (i // 2 + 1))
                dve.tensor_tensor(obT[:, i, :], obT[:, i, :], gaT[:, i, :], ALU.add).then_inc(m_ok, 1)

            merged = 0
            for n in range(N_IN):
                if 1 <= n <= HEADS_B:
                    gate_sums(n - 1)
                if n >= 1 and USES[n - 1] == 2:
                    second_use(n - 1)
                for h in range(HEADS_B):
                    if n == gla_tile(h, 0):
                        gla_mask(h)
                    if n == gla_tile(h, 1):
                        gla_states(h)
                slot(2 * (n - UNIT0))
                gates(n)
                slot(2 * (n - UNIT0) + 1)
                for h in range(HEADS_B):
                    if n == gla_tile(h, 3):
                        gla_norms(h)
                for h in range(HEADS_B):
                    if n == gla_tile(h, 0) - 2:
                        gla_inputs(h)
                if n == TILE_OF["qA", 7]:
                    biases()
                while merged < KC and TILE_OF["gb", merged] <= n and \
                        UNIT0 + (2 * NJ * (merged // 2 + 1) + 1) // 2 <= n:
                    merge(merged)
                    merged += 1

            dve.wait_ge(gemm_done, N_IN)
            for i in range(KC):
                dve.wait_ge(m_hi_ok, i + 1)
                dve.tensor_tensor(h_lo[:, i, :], obT[:, i, :], h_hi[:, i, :].bitcast(F32), ALU.subtract)\
                    .then_inc(m_lo_ok, 1)
            dve.wait_ge(qk_done, NU)
            for i in range(KC):
                n = OUT0 + i
                dve.wait_ge(gemm_done, n + 1)
                dve.wait_ge(xt_ok, i + 1)
                dve.tensor_tensor(h2(x2T[:, i, :]), halves(G[n % 2]), h2(xTi[:, i % 2, :]), ALU.add)\
                    .then_inc(set_free[n % 2], 1)
            k = len(NORMS)
            mean_square(k, X[1], 1.0 / D, (norm_done, 1))
            dve.wait_ge(norm_done, k + 1)
            refine(rv[:, :], rt[:, :], rs[:, :])

            def low_part(c):
                dve.wait_ge(f_hi_ok, c + 1)
                dve.tensor_tensor(h_lo[:, c, :], fs[:, c % 2, :], h_hi[:, c, :].bitcast(F32), ALU.subtract)\
                    .then_inc(f_ok, 1)

            dve.wait_ge(xt_done, KC)
            dve.wait_ge(gemm_done, OUT0 + KC)
            for c in range(KC):
                if c >= 2:
                    dve.wait_ge(f_ok, c - 1)
                dve.scalar_tensor_tensor(out=fs[:, c % 2, :], in0=x2T[:, c, :],
                                         scalar=param[:, G_FFN + c:G_FFN + c + 1], in1=rt[:, :],
                                         op0=ALU.mult, op1=ALU.mult).then_inc(f_in, 1)
                if c >= 1:
                    low_part(c - 1)
            low_part(KC - 1)
            dve.wait_ge(f_ok, KC)

            dve.wait_ge(out_sem, 64)
            before = 0
            for g, m in enumerate(FF_GROUPS):
                with dve.Fori(0, m // 2) as i:
                    for r in range(2):
                        n = GU0[g] + 2 * r
                        s, s1 = n % 2, (n + 1) % 2
                        dve.wait_ge(silu_ok, i * 2 + (before + r + 1))
                        dve.scalar_tensor_tensor(out=h2(fs[:, r, :]), in0=h2(ft[:, r, :]), scalar=1.0,
                                                 in1=halves(G[s]), op0=ALU.add, op1=ALU.mult)\
                            .then_inc(set_free[s], 1)
                        dve.wait_ge(gemm_done, i * RING + (n + 2))
                        dve.wait_ge(set_free[s], i * 2 + (uses_before(n) + 1))
                        dve.scalar_tensor_tensor(out=h2(fa[:, r, :]), in0=h2(fs[:, r, :]), scalar=0.5,
                                                 in1=halves(G[s1]), op0=ALU.mult, op1=ALU.mult)\
                            .then_inc(set_free[s1], 1)
                        dve.wait_ge(mid_hi_ok, i * 2 + (before + r + 1))
                        at = bass.ds(i * 2 + r, 1)
                        dve.tensor_tensor(mid_lo[:, at, :], fa[:, r:r + 1, :], mid_hi[:, at, :].bitcast(F32),
                                          ALU.subtract).then_inc(mid_ok, 1)
                before += m
                with dve.Fori(0, KC // RING) as i:
                    for t in range(RING):
                        n = DN0[g] + t
                        dve.wait_ge(gemm_done, i * RING + (n + 1))
                        x = x2T[:, bass.ds(i * RING + t, 1), :].rearrange("p a (b n) -> p (a b) n", b=2)
                        dve.tensor_tensor(x, halves(G[n % 2]), x, ALU.add).then_inc(set_free[n % 2], 1)


_INS = ["x_prompt", "x_sample", "cache_swa_k", "cache_swa_v", "state_gla", "w_in", "w_a2", "b_a", "g_q", "g_k",
        "sinks", "g_ob", "w_out", "g_mix", "g_ffn", "w_gate", "w_up", "w_down"]
_OUTS = [(1, SEQ, D), (1, DEC, D), (1, 1, WINDOW, KV_A, HD), (1, 1, WINDOW, KV_A, HD),
         (1, 1, HEADS_B, DK, DV), (1, 1, DEC, KV_A, HD), (1, 1, DEC, KV_A, HD), (1, 1, HEADS_B, DK, DV)]


def kernel(**inputs):
    import concourse.bacc as bacc
    from concourse.bass_utils import run_bass_kernel_spmd

    nc = bacc.Bacc("TRN2", target_bir_lowering=False, num_devices=1)
    arrays, args = {}, []
    for name in _INS:
        a = np.ascontiguousarray(inputs[name])
        arrays[f"in_{name}_dram"] = a
        args.append(nc.dram_tensor(f"in_{name}_dram", a.shape, mybir.dt.from_np(a.dtype),
                                   kind="ExternalInput").ap())
    for i, shape in enumerate(_OUTS):
        args.append(nc.dram_tensor(f"out_{i}_dram", shape, F32, kind="ExternalOutput").ap())
    mixer_program(nc, *args)
    r = run_bass_kernel_spmd(nc, [arrays], core_ids=[0])
    return tuple(r.results[0][f"out_{i}_dram"] for i in range(len(_OUTS)))
```

```python
from contextlib import ExitStack

import numpy as np

import concourse.bass as bass
from concourse import mybir

F32 = mybir.dt.float32
F32R = mybir.dt.float32r
I32 = mybir.dt.int32
ALU = mybir.AluOpType
ACT = mybir.ActivationFunctionType

P = 128
D = 1024
SEQ = 512
DEC = 32
T = SEQ + DEC
TH = T // 2
KC = D // P
EPS = 1e-6
NEG = -1e30
HEADS_A, KV_A, HD = 16, 4, 64
CHUNK, WINDOW = 64, 128
HEADS_B, DK, DV = 4, 128, 256
RANK = 16
TAU = 16.0
FF = 2816
O_QA, O_KA, O_VA = 0, 1024, 1280
O_QB, O_KB, O_VB, O_RB = 1536, 2048, 2560, 3584
O_A1, O_GA, O_GB = 4608, 4624, 5648
P_IN = 6672

RING = 4
LN_EXP, EXP_TANH = "natural_log_exp_and_others", "exp_and_others"
TOK = [(j * P, P) for j in range(SEQ // P)] + [(SEQ, DEC)]
NJ = len(TOK)
SJ = NJ - 1


def input_tiles():
    tiles = [("a1", 0, [(O_A1, P)])]
    for h in range(HEADS_B):
        tiles += [("kB", h, [(O_KB + h * DK, P)]), ("qB", h, [(O_QB + h * DK, P)])]
        tiles += [("vB", 2 * h + f, [(O_VB + h * DV + f * P, P)]) for f in range(2)]
    tiles += [("kA", i, [(O_KA + i * P, P)]) for i in range(2)]
    tiles += [("vA", i, [(O_VA + i * P, P)]) for i in range(2)]
    tiles += [("qA", 4 * u + i, [(O_QA + (8 * u + i) * HD, HD), (O_QA + (8 * u + 4 + i) * HD, HD)])
              for u in range(2) for i in range(4)]
    tiles += [("ga", i, [(O_GA + i * P, P)]) for i in range(KC)]
    for i in range(KC):
        tiles += [("rb", i, [(O_RB + i * P, P)]), ("gb", i, [(O_GB + i * P, P)])]
    return tiles


IN_TILES = input_tiles()
N_IN = len(IN_TILES)
TILE_OF = {(kind, i): n for n, (kind, i, _) in enumerate(IN_TILES)}
OUT0 = N_IN
FF_GROUPS = [8, 8, 6]
GU0, DN0 = [], []
_n = OUT0 + KC
for _m in FF_GROUPS:
    GU0.append(_n)
    DN0.append(_n + 2 * _m)
    _n += 2 * _m + KC
N_TILES = _n
N_SMALL = 13

USES = [2 if kind in ("vB", "vA", "kA", "qA") else 1 for kind, _, _ in IN_TILES]
USES += [1] * (N_TILES - N_IN)
POST_TILES = [n for n in range(N_IN) if USES[n] == 2]


def uses_before(n):
    return sum(USES[m] for m in range(n % 2, n, 2))


UNITS = [(g, j, par) for g in range(KV_A) for j in range(NJ) for par in range(2)]
NU = len(UNITS)
NB = 3
LAG_T, LAG_V = 2, 3
UNIT0 = TILE_OF["ga", 1]
KEYS_OUT = TILE_OF["qA", 2]


def gla_tile(h, step):
    return 7 + 4 * h + (0, 1, 1, 2)[step]


GLA_INPUTS = [max(3 + 4 * h, HEADS_B) for h in range(HEADS_B)]


def norm_order():
    order = []
    for n in range(N_IN + 1):
        if n >= 1 and IN_TILES[n - 1][0] in ("kA", "qA"):
            order.append(("post", n - 1))
        order += [("gla", h) for h in range(HEADS_B) if n == gla_tile(h, 3)]
    return order


NORMS = norm_order()


def unit_shape(u):
    g, j, par = UNITS[u]
    heads = (4 * g + par, 4 * g + 2 + par)
    lo = P if j == 0 else 0
    hi = P + DEC if j == SJ else 2 * P
    return g, j, par, heads, TOK[j][1], lo, hi


def mixer_program(nc, x_prompt, x_sample, cache_k, cache_v, state, w_in, w_a2, b_a, g_q, g_k, sinks,
                  g_ob, w_out, g_mix, g_ffn, w_gate, w_up, w_down,
                  y_prompt, y_sample, nk_p, nv_p, ns_p, nk_s, nv_s, ns_s):
    with ExitStack() as ctx:
        def sem(name):
            return ctx.enter_context(nc.semaphore(name))

        def tensor(where, name, shape, dt=F32):
            return where.enter_context(nc.sbuf_tensor(name, shape, dt))

        h_hi = tensor(ctx, "h_hi", [P, KC, T], F32R)
        h_lo = tensor(ctx, "h_lo", [P, KC, T], F32R)
        wraw = tensor(ctx, "wraw", [P, RING, KC, P])
        w_hi = tensor(ctx, "w_hi", [P, RING, KC, P], F32R)
        w_lo = tensor(ctx, "w_lo", [P, RING, KC, P], F32R)
        ident = tensor(ctx, "ident", [P, P])
        ones = tensor(ctx, "ones", [P, P])
        param = tensor(ctx, "param", [P, 24])
        eps = tensor(ctx, "eps", [P, 1])
        one = tensor(ctx, "one", [P, 1])
        sinkb = tensor(ctx, "sinkb", [P, HEADS_A])
        dist = tensor(ctx, "dist", [P, 2 * P])
        sq = tensor(ctx, "sq", [P, 2, T])
        rs = tensor(ctx, "rs", [P, T])
        rt = tensor(ctx, "rt", [P, T])
        rv = tensor(ctx, "rv", [P, T])
        G_MIX, G_FFN, B_A, G_OB, G_Q, G_K = 0, 8, 16, 20, 22, 23

        mix = ExitStack()
        obT = tensor(mix, "obT", [P, KC, T])
        kAT = tensor(mix, "kAT", [P, 2, T])
        kcT = tensor(mix, "kcT", [P, 2, P])
        vA = tensor(mix, "vA", [P, NJ, KV_A * HD])
        vc = tensor(mix, "vc", [P, KV_A * HD])
        raw = tensor(mix, "raw", [P, 2, T])
        kout = tensor(mix, "kout", [P, 2, 2 * P])

        gla = ExitStack()
        Sin = tensor(gla, "Sin", [P, HEADS_B, DV])
        wa2 = tensor(gla, "wa2", [RANK, HEADS_B * DK])
        prow = tensor(gla, "prow", [24, P])
        srow = tensor(gla, "srow", [1, HEADS_A])
        kc_tok = tensor(gla, "kc_tok", [P, KV_A * HD])
        cmask = tensor(gla, "cmask", [P, P])
        reset = tensor(gla, "reset", [P, NJ, P + 1])
        lab = tensor(gla, "lab", [P, NJ, P + 1])
        a1T = tensor(gla, "a1T", [RANK, T])
        CB = tensor(gla, "CB", [P, HEADS_B, NJ, P + 1])
        dec = tensor(gla, "dec", [P, 2, NJ])
        att = tensor(gla, "att", [P, NJ, P])
        kot = tensor(gla, "kot", [P, NJ, P])
        S = tensor(gla, "S", [P, 3, DV])
        qT = tensor(gla, "qT", [P, 2, T])
        kT = tensor(gla, "kT", [P, 2, T])
        qL = tensor(gla, "qL", [P, T])
        kL = tensor(gla, "kL", [P, T])
        x32 = tensor(gla, "x32", [P, SEQ])
        x64 = tensor(gla, "x64", [P, SEQ])
        tA = tensor(gla, "tA", [P, NJ * P])
        tB = tensor(gla, "tB", [P, NJ * P])
        tC = tensor(gla, "tC", [P, NJ * P])
        vB = tensor(gla, "vB", [P, 2, NJ, DV])
        Ssmp = tensor(gla, "Ssmp", [P, 2, DV])
        Sfin = tensor(gla, "Sfin", [P, 2, DV])
        gla.close()

        att_mem = ExitStack()
        gaT = tensor(att_mem, "gaT", [P, KC, T])
        qAT = tensor(att_mem, "qAT", [P, KC, T])
        bias = tensor(att_mem, "bias", [P, HEADS_A, 2 * P])
        prob = tensor(att_mem, "prob", [P, NB, 2, 2 * P])
        probT = tensor(att_mem, "probT", [P, 2, 2, 2, P])
        th = tensor(att_mem, "th", [P, 2, T])
        rbu = tensor(att_mem, "rbu", [P, T])
        mx = tensor(att_mem, "mx", [P, NB, 2])
        nm = tensor(att_mem, "nm", [P, NB, 2])
        sd = tensor(att_mem, "sd", [P, NB, 2])
        es = tensor(att_mem, "es", [P, NB, 2])
        sm = tensor(att_mem, "sm", [P, NB, 2])
        den = tensor(att_mem, "den", [P, NB, 2])
        rd = tensor(att_mem, "rd", [P, NB, 2])
        att_mem.close()

        rows = ExitStack()
        tensor(rows, "gap_gaT", [P, KC, T])
        x2T = tensor(rows, "x2T", [P, KC, T])
        ffn_work = ExitStack()
        xtok = tensor(rows, "xtok", [P, NJ, D])
        xTi = tensor(rows, "xTi", [P, 2, T])
        x2g = tensor(rows, "x2g", [P, 2, T])
        rows.close()
        tensor(ffn_work, "gap_rows", [P, 2 * KC, T])
        ft = tensor(ffn_work, "ft", [P, 2, T])
        fs = tensor(ffn_work, "fs", [P, 2, T])
        fa = tensor(ffn_work, "fa", [P, 2, T])
        fg = tensor(ffn_work, "fg", [P, 2, T])
        ytok = tensor(ffn_work, "ytok", [P, 2, NJ, P])
        ffn_work.close()
        mix.close()

        f_mem = ExitStack()
        f_hi = tensor(f_mem, "f_hi", [P, KC, T], F32R)
        f_lo = tensor(f_mem, "f_lo", [P, KC, T], F32R)
        f_mem.close()

        G = [ctx.enter_context(nc.psum_tensor(f"G{s}", [P, 2 * 512], F32)) for s in range(2)]
        X = [ctx.enter_context(nc.psum_tensor(f"X{s}", [P, 2 * 512], F32)) for s in range(2)]
        XB = [X[b // 2][:, 512 * (b % 2):512 * (b % 2) + 512] for b in range(4)]

        def halves(ps):
            return ps[:, :].rearrange("p (b n) -> p b n", b=2)[:, :, 0:TH]

        def h2(ap):
            return ap.rearrange("p (b n) -> p b n", b=2)

        wload = [sem(f"wload{r}") for r in range(RING)]
        w_split = sem("w_split")
        pool_step = sem("pool_step")
        gemm_done = sem("gemm_done")
        set_free = [sem("set_free0"), sem("set_free1")]
        post_done = sem("post_done")
        in_x = [sem(f"in_x{j}") for j in range(NJ)]
        in_small = sem("in_small")
        in_caches = sem("in_caches")
        hi_done = sem("hi_done")
        const_pool = sem("const_pool")
        const_dve = sem("const_dve")
        act_step = sem("act_step")
        dve_step = sem("dve_step")
        setup_pe = sem("setup_pe")
        param_ok = sem("param_ok")
        x_sq = sem("x_sq")
        x_scaled = sem("x_scaled")
        x_turned = sem("x_turned")
        h_hi_ok = sem("h_hi_ok")
        h_ok = sem("h_ok")
        r_ok = sem("r_ok")
        norm_done = sem("norm_done")
        z_done = sem("z_done")
        z_abs = sem("z_abs")
        z_free = sem("z_free")
        z_ln = sem("z_ln")
        cum_ok = sem("cum_ok")
        d_ok = sem("d_ok")
        e_ok = sem("e_ok")
        gla_in = sem("gla_in")
        gla_att = sem("gla_att")
        gla_masked = sem("gla_masked")
        gla_kot = sem("gla_kot")
        gla_upd = sem("gla_upd")
        gla_state = sem("gla_state")
        gla_out = sem("gla_out")
        gla_sq = sem("gla_sq")
        gla_ssq = sem("gla_ssq")
        gla_norm = sem("gla_norm")
        kt_done = sem("kt_done")
        kt_out = sem("kt_out")
        out_sem = sem("out_sem")
        s_out = [sem("s_out0"), sem("s_out1")]
        bias_ok = sem("bias_ok")
        qk_done = sem("qk_done")
        smax_ok = sem("smax_ok")
        exp_ok = sem("exp_ok")
        prob_ok = sem("prob_ok")
        pt_done = sem("pt_done")
        pt_copied = sem("pt_copied")
        pv_done = sem("pv_done")
        oa_ok = sem("oa_ok")
        tanh_ok = sem("tanh_ok")
        gb_used = sem("gb_used")
        m_ok = sem("m_ok")
        m_hi_ok = sem("m_hi_ok")
        m_lo_ok = sem("m_lo_ok")
        xt_done = sem("xt_done")
        xt_ok = sem("xt_ok")
        x2_sq = sem("x2_sq")
        x2_ssq = sem("x2_ssq")
        f_in = sem("f_in")
        f_hi_ok = sem("f_hi_ok")
        f_ok = sem("f_ok")
        silu_ok = sem("silu_ok")
        fs_ok = sem("fs_ok")
        fr_ok = sem("fr_ok")
        mid_hi_ok = sem("mid_hi_ok")
        mid_ok = sem("mid_ok")
        yt_done = sem("yt_done")
        y_ok = sem("y_ok")
        y_out = [sem("y_out0"), sem("y_out1")]

        block = ctx.enter_context(nc.Block())

        @block.sync
        def _(sp):
            for n, (_kind, _i, runs) in enumerate(IN_TILES):
                if n >= RING:
                    sp.wait_ge(w_split, n - RING + 1)
                at = 0
                for col, width in runs:
                    src = w_in[0, :, col:col + width].rearrange("(k p) n -> p k n", p=P)
                    sp.dma_start(wraw[:, n % RING, :, at:at + width], src).then_inc(
                        wload[n % RING], 32 // len(runs))
                    at += width

            def stream(n0, turns, source, kc=KC):
                with sp.Fori(0, turns) as i:
                    for t in range(RING):
                        sp.wait_ge(w_split, i * RING + (n0 + t - RING + 1))
                        slot = (n0 + t) % RING
                        sp.dma_start(wraw[:, slot, 0:kc, :], source(i, t)).then_inc(wload[slot], 32)

            def block_of(w, row0, kc, col):
                return w[0, row0:row0 + kc * P, bass.ds(col, P)].rearrange("(k p) n -> p k n", p=P)

            stream(OUT0, KC // RING, lambda i, t: block_of(w_out, 0, KC, i * (RING * P) + t * P))
            f0 = 0
            for g, m in enumerate(FF_GROUPS):
                stream(GU0[g], 2 * m // RING, lambda i, t: block_of(
                    (w_gate, w_up)[t % 2], 0, KC, i * (2 * P) + (f0 + t // 2) * P))
                stream(DN0[g], KC // RING, lambda i, t: block_of(
                    w_down, f0 * P, m, i * (RING * P) + t * P), kc=m)
                f0 += m

        @block.gpsimd
        def _(pool):
            pool.memset(ident[:, :], 0.0).then_inc(pool_step, 1)
            pool.memset(cmask[:, :], 1.0).then_inc(pool_step, 1)
            pool.wait_ge(pool_step, 2)
            pool.affine_select(out=ident[:, :], in_=ident[:, :], compare_op=ALU.not_equal, fill=1.0,
                               base=0, pattern=[[-1, P]], channel_multiplier=1).then_inc(const_pool, 1)
            pool.iota(dist[:, :], pattern=[[-1, 2 * P]], base=P, channel_multiplier=1,
                      allow_small_or_imprecise_dtypes=True).then_inc(const_pool, 1)
            pool.affine_select(out=cmask[:, :], in_=cmask[:, :], compare_op=ALU.is_ge, fill=0.0,
                               base=0, pattern=[[1, P]], channel_multiplier=-1).then_inc(pool_step, 1)
            pool.wait_ge(pool_step, 3)
            cm = cmask[:, :].rearrange("p (b n) -> p b n", b=4)
            pool.affine_select(out=cm, in_=cm, compare_op=ALU.is_ge, fill=0.0, base=0,
                               pattern=[[-32, 4], [0, 32]], channel_multiplier=1).then_inc(const_pool, 1)

            def low_part(slot):
                pool.tensor_tensor(w_lo[:, slot, :, :], wraw[:, slot, :, :],
                                   w_hi[:, slot, :, :].bitcast(F32), ALU.subtract).then_inc(w_split, 1)

            for n in range(RING):
                pool.wait_ge(hi_done, n + 1)
                low_part(n)
            with pool.Fori(1, N_TILES // RING) as i:
                for t in range(RING):
                    pool.wait_ge(hi_done, i * RING + (t + 1))
                    low_part(t)
            for n in range(N_TILES // RING * RING, N_TILES):
                pool.wait_ge(hi_done, n + 1)
                low_part(n % RING)

        @block.tensor
        def _(pe):
            def chunk(slot, ps, kc, last, b_hi, b_lo):
                for b in range(2):
                    cols = slice(b * TH, (b + 1) * TH)
                    o = ps[:, 512 * b:512 * b + TH]
                    pe.matmul(o, w_hi[:, slot, kc, :], b_hi[:, kc, cols], start=(kc == 0), stop=False)
                    pe.matmul(o, w_hi[:, slot, kc, :], b_lo[:, kc, cols], start=False, stop=False)
                    mm = pe.matmul(o, w_lo[:, slot, kc, :], b_hi[:, kc, cols], start=False, stop=(kc == last))
                return mm

            pe.wait_ge(const_pool, 1)
            pe.wait_ge(const_dve, 1)
            pe.wait_ge(in_small, 16 * 9)
            pe.transpose(XB[0][:, 0:24], prow[:, :], ident[0:24, 0:24])
            pe.matmul(XB[1][:, 0:HEADS_A], ones[0:1, :], srow[:, :], start=True, stop=True).then_inc(setup_pe, 1)

            pe.wait_ge(param_ok, 1)
            pe.wait_ge(x_scaled, NJ)
            for c in range(KC):
                if c >= 2:
                    pe.wait_ge(h_ok, c - 1)
                for j, (t0, nt) in enumerate(TOK):
                    mm = pe.transpose(X[c % 2][:, t0:t0 + nt], xtok[0:nt, j, c * P:(c + 1) * P],
                                      ident[0:nt, 0:nt])
                mm.then_inc(x_turned, 1)

            def gate_logits(h):
                pe.wait_ge(set_free[0], 1)
                pe.wait_ge(in_caches, 16 * (N_SMALL - 9))
                pe.wait_ge(h_ok, KC)
                if h >= 2:
                    pe.wait_ge(z_free, h - 1)
                for b in range(2):
                    mm = pe.matmul(X[h % 2][:, 512 * b:512 * b + TH], wa2[:, h * DK:(h + 1) * DK],
                                   a1T[:, b * TH:(b + 1) * TH], start=True, stop=True)
                mm.then_inc(z_done, 1)

            def second_use(n):
                ps = G[n % 2]
                pe.wait_ge(set_free[n % 2], uses_before(n) + 1)
                if IN_TILES[n][0] in ("vB", "vA"):
                    for j, (t0, nt) in enumerate(TOK):
                        mm = pe.transpose(ps[0:nt, j * P:(j + 1) * P], raw[:, n % 2, t0:t0 + nt], ident[:, :])
                else:
                    for b in range(2):
                        for r in (slice(0, HD), slice(HD, P)):
                            mm = pe.matmul(ps[r, 512 * b:512 * b + TH], ones[r, 0:HD],
                                           sq[r, n % 2, b * TH:(b + 1) * TH], start=True, stop=True)
                mm.then_inc(post_done, 1)

            def gla_scores(h):
                pe.wait_ge(gla_in, h + 1)
                pe.wait_ge(z_free, HEADS_B)
                if h >= 1:
                    pe.wait_ge(gla_norm, h)
                for c in range(NJ - 1):
                    k = slice(c * P, (c + 1) * P)
                    pe.matmul(XB[0][:, k], kL[:, k], qL[:, k], start=True, stop=True)
                    pe.matmul(XB[1][0:64, c * P + 64:(c + 1) * P], x64[:, c * P:c * P + 64],
                              x64[:, c * P + 64:(c + 1) * P], start=True, stop=True)
                    for a in (0, 64):
                        pe.matmul(XB[1][a:a + 32, c * P + a + 32:c * P + a + 64], x32[:, c * P + a:c * P + a + 32],
                                  x32[:, c * P + a + 32:c * P + a + 64], start=True, stop=True)
                    pe.transpose(XB[3][:, k], kT[:, h % 2, k], ident[:, :])
                s = slice(SEQ, T)
                pe.matmul(XB[2][0:DEC, 0:DEC], kL[:, s], qL[:, s], start=True, stop=True)
                pe.transpose(XB[2][0:DEC, P:2 * P], kT[:, h % 2, s], ident[:, :]).then_inc(gla_att, 1)

            def gla_updates(h):
                pe.wait_ge(gla_masked, h + 1)
                pe.wait_ge(gla_kot, h + 1)
                for f in range(2):
                    n = TILE_OF["vB", 2 * h + f]
                    pe.wait_ge(set_free[n % 2], uses_before(n) + 2)
                for c in range(NJ - 1):
                    pe.matmul(XB[c // 2][:, (c % 2) * DV:(c % 2 + 1) * DV], kot[:, c, :],
                              vB[:, h % 2, c, :], start=True, stop=True)
                pe.matmul(XB[3][:, 0:DV], kot[0:DEC, SJ, :], vB[0:DEC, h % 2, SJ, :],
                          start=True, stop=True).then_inc(gla_upd, 1)

            def gla_outputs(h):
                pe.wait_ge(gla_state, h + 1)
                for f in range(2):
                    v = slice(f * P, (f + 1) * P)
                    for c in range(NJ - 1):
                        k = slice(c * P, (c + 1) * P)
                        pe.matmul(XB[2 + f][:, k], vB[:, h % 2, c, v], att[:, c, :], start=True, stop=(c == 0))
                        if c >= 1:
                            pe.matmul(XB[2 + f][:, k], S[:, c - 1, v], qT[:, h % 2, k], start=False, stop=True)
                    pe.matmul(XB[f][:, 0:DEC], vB[0:DEC, h % 2, SJ, v], att[0:DEC, SJ, 0:DEC],
                              start=True, stop=False)
                    mm = pe.matmul(XB[f][:, 0:DEC], Sin[:, h, v], qT[:, h % 2, SEQ:T], start=False, stop=True)
                mm.then_inc(gla_out, 1)

            def gla_squares(h):
                pe.wait_ge(gla_sq, h + 1)
                for b in range(2):
                    for f in range(2):
                        mm = pe.matmul(X[0][:, 512 * b:512 * b + TH], ones[:, :],
                                       sq[:, f, b * TH:(b + 1) * TH], start=(f == 0), stop=(f == 1))
                mm.then_inc(gla_ssq, 1)

            def keys_out():
                pe.wait_ge(norm_done, NORMS.index(("post", TILE_OF["kA", 1])) + 1)
                pe.wait_ge(gla_norm, HEADS_B)
                for u in range(2):
                    pe.transpose(XB[0][:, u * P:(u + 1) * P], kAT[:, u, SEQ - P:SEQ], ident[:, :])
                    pe.transpose(XB[1][0:DEC, u * P:(u + 1) * P], kAT[:, u, SEQ:T], ident[:, :])
                    mm = pe.transpose(XB[2][:, u * P:(u + 1) * P], kc_tok[:, u * P:(u + 1) * P], ident[:, :])
                mm.then_inc(kt_done, 1)

            def unit_scores(u):
                g, j, par, heads, nq, lo, hi = unit_shape(u)
                if u == 0:
                    pe.wait_ge(kt_out, 1)
                    pe.wait_ge(norm_done, len(NORMS))
                if u >= 2:
                    pe.wait_ge(smax_ok, u - 1)
                hf = slice((g % 2) * HD, (g % 2) * HD + HD)
                t0 = TOK[j][0]
                for a, head in enumerate(heads):
                    q = qAT[hf, 4 * (g // 2) + head % 4, t0:t0 + nq]
                    o = XB[u % 2][0:nq, a * 2 * P:(a + 1) * 2 * P]
                    if j == SJ:
                        pe.matmul(o[:, 0:P], q, kcT[hf, g // 2, :], start=True, stop=True)
                        mm = pe.matmul(o[:, P:P + DEC], q, kAT[hf, g // 2, SEQ:T], start=True, stop=True)
                    else:
                        mm = pe.matmul(o[:, lo:hi], q, kAT[hf, g // 2, t0 - P + lo:t0 - P + hi],
                                       start=True, stop=True)
                mm.then_inc(qk_done, 1)

            def unit_turn(u):
                g, j, par, heads, nq, lo, hi = unit_shape(u)
                pe.wait_ge(prob_ok, u + 1)
                if u >= 1:
                    pe.wait_ge(pt_copied, u)
                for a in range(2):
                    for kt in range(lo // P, 2):
                        nk = min(hi - kt * P, P)
                        c0 = (2 * a + kt) * P
                        mm = pe.transpose(XB[2][0:nk, c0:c0 + nq], prob[0:nq, u % NB, a, kt * P:kt * P + nk],
                                          ident[0:nq, 0:nq])
                mm.then_inc(pt_done, 1)

            def unit_values(u):
                g, j, par, heads, nq, lo, hi = unit_shape(u)
                pe.wait_ge(pt_copied, u + 1)
                if u >= 1:
                    pe.wait_ge(oa_ok, u)
                o = XB[3][par * HD:(par + 1) * HD, 0:2 * P].rearrange("p (a n) -> p a n", a=2)[:, :, 0:nq]
                for kt in range(lo // P, 2):
                    nk = min(hi - kt * P, P)
                    if j == SJ:
                        v = vc[:, g * HD:(g + 1) * HD] if kt == 0 else vA[0:nk, SJ, g * HD:(g + 1) * HD]
                    else:
                        v = vA[:, j - 1 + kt, g * HD:(g + 1) * HD]
                    mm = pe.matmul(o, v, probT[0:nk, u % 2, :, kt, 0:nq], start=(kt == lo // P), stop=(kt == 1))
                mm.then_inc(pv_done, 1)

            beside = {}

            def put(n, k, step, *args):
                beside.setdefault((n, k), []).append((step, args))

            for h in range(HEADS_B):
                put(1 + h, 3, gate_logits, h)
            for n in POST_TILES:
                put(n + 1, 3, second_use, n)
            for h in range(HEADS_B):
                put(gla_tile(h, 0), 3, gla_scores, h)
                put(gla_tile(h, 1), 1, gla_updates, h)
                put(gla_tile(h, 2), 6, gla_outputs, h)
                put(gla_tile(h, 3), 5, gla_squares, h)
            put(KEYS_OUT, 7, keys_out)
            for u in range(NU + LAG_V):
                n, k = UNIT0 + u // 2, 3 + 4 * (u % 2)
                if u < NU:
                    put(n, k, unit_scores, u)
                if LAG_T <= u < NU + LAG_T:
                    put(n, k, unit_turn, u - LAG_T)
                if u >= LAG_V:
                    put(n, k, unit_values, u - LAG_V)

            for n in range(N_IN):
                pe.wait_ge(w_split, n + 1)
                if n >= 2:
                    pe.wait_ge(set_free[n % 2], uses_before(n))
                for kc in range(KC):
                    if n == 0:
                        pe.wait_ge(h_ok, kc + 1)
                    mm = chunk(n % RING, G[n % 2], kc, KC - 1, h_hi, h_lo)
                    if kc == KC - 1:
                        mm.then_inc(gemm_done, 1)
                    for step, args in beside.get((n, kc), ()):
                        step(*args)

            def residual_squares(i):
                pe.wait_ge(x2_sq, i + 1)
                for b in range(2):
                    mm = pe.matmul(X[1][:, 512 * b:512 * b + TH], ones[:, :],
                                   sq[:, i % 2, b * TH:(b + 1) * TH], start=(i == 0), stop=(i == KC - 1))
                mm.then_inc(x2_ssq, 1)

            for i in range(KC):
                n = OUT0 + i
                pe.wait_ge(w_split, n + 1)
                pe.wait_ge(set_free[n % 2], uses_before(n))
                for kc in range(KC):
                    if i == 0:
                        pe.wait_ge(m_lo_ok, kc + 1)
                    mm = chunk(n % RING, G[n % 2], kc, KC - 1, h_hi, h_lo)
                mm.then_inc(gemm_done, 1)
                if i == 0:
                    for j in range(NJ):
                        pe.wait_ge(in_x[j], 32)
                    pe.wait_ge(oa_ok, NU)
                else:
                    pe.wait_ge(xt_ok, i)
                for j, (t0, nt) in enumerate(TOK):
                    mm = pe.transpose(X[0][:, t0:t0 + nt], xtok[0:nt, j, i * P:(i + 1) * P], ident[0:nt, 0:nt])
                mm.then_inc(xt_done, 1)
                if i >= 1:
                    residual_squares(i - 1)

            def turn_rows(i):
                n = DN0[-1] + i
                pe.wait_ge(set_free[n % 2], uses_before(n) + 1)
                if i >= 2:
                    pe.wait_ge(y_ok, i - 1)
                for j, (t0, nt) in enumerate(TOK):
                    mm = pe.transpose(X[i % 2][0:nt, j * P:(j + 1) * P], x2T[:, i, t0:t0 + nt], ident[:, :])
                mm.then_inc(yt_done, 1)

            for n in range(GU0[0], GU0[0] + RING):
                pe.wait_ge(w_split, n + 1)
                pe.wait_ge(set_free[n % 2], uses_before(n))
                for kc in range(KC):
                    if n == GU0[0]:
                        pe.wait_ge(f_ok, kc + 1)
                    mm = chunk(n % RING, G[n % 2], kc, KC - 1, f_hi, f_lo)
                    if kc == KC - 1:
                        mm.then_inc(gemm_done, 1)
                    if n == GU0[0] and kc == KC - 2:
                        residual_squares(KC - 1)
            for g, m in enumerate(FF_GROUPS):
                with pe.Fori(1 if g == 0 else 0, 2 * m // RING) as i:
                    for t in range(RING):
                        n = GU0[g] + t
                        pe.wait_ge(w_split, i * RING + (n + 1))
                        pe.wait_ge(set_free[n % 2], i * 2 + uses_before(n))
                        for kc in range(KC):
                            mm = chunk(n % RING, G[n % 2], kc, KC - 1, f_hi, f_lo)
                        mm.then_inc(gemm_done, 1)
                before = sum(FF_GROUPS[:g])
                if g < len(FF_GROUPS) - 1:
                    with pe.Fori(0, KC // RING) as i:
                        for t in range(RING):
                            n = DN0[g] + t
                            pe.wait_ge(w_split, i * RING + (n + 1))
                            pe.wait_ge(set_free[n % 2], i * 2 + uses_before(n))
                            for kc in range(m):
                                if t == 0:
                                    pe.wait_ge(mid_ok, before + kc + 1)
                                mm = chunk(n % RING, G[n % 2], kc, m - 1, h_hi, h_lo)
                            mm.then_inc(gemm_done, 1)
                else:
                    for i in range(KC):
                        n = DN0[g] + i
                        pe.wait_ge(w_split, n + 1)
                        pe.wait_ge(set_free[n % 2], uses_before(n))
                        for kc in range(m):
                            if i == 0:
                                pe.wait_ge(mid_ok, before + kc + 1)
                            mm = chunk(n % RING, G[n % 2], kc, m - 1, h_hi, h_lo)
                        mm.then_inc(gemm_done, 1)
                        if i >= 1:
                            turn_rows(i - 1)
                    turn_rows(KC - 1)

        @block.scalar
        def _(act):
            steps = [0]

            def link(ins):
                steps[0] += 1
                ins.then_inc(act_step, 1)
                act.wait_ge(act_step, steps[0])

            def high_part(n, turn=None):
                slot = n % RING
                if turn is None:
                    act.wait_ge(wload[slot], 32 * (n // RING + 1))
                    if n >= RING:
                        act.wait_ge(gemm_done, n - RING + 1)
                else:
                    act.wait_ge(wload[slot], turn * 32 + 32 * (n // RING + 1))
                    act.wait_ge(gemm_done, turn * RING + (n - RING + 1))
                act.activation(w_hi[:, slot, :, :], wraw[:, slot, :, :], ACT.Copy).then_inc(hi_done, 1)

            def load_rows():
                for j, (t0, nt) in enumerate(TOK):
                    src = x_sample[0] if j == SJ else x_prompt[0, t0:t0 + nt, :]
                    act.dma_start(xtok[0:nt, j, :], src).then_inc(in_x[j], 16)

            small_loads = [
                (prow[G_MIX:G_MIX + 8, :], g_mix[0].rearrange("(r n) -> r n", n=P)),
                (prow[G_FFN:G_FFN + 8, :], g_ffn[0].rearrange("(r n) -> r n", n=P)),
                (prow[B_A:B_A + 4, :], b_a[0].rearrange("(r n) -> r n", n=P)),
                (prow[G_OB:G_OB + 2, :], g_ob[0].rearrange("(r n) -> r n", n=P)),
                (prow[G_Q:G_Q + 1, 0:HD], g_q), (prow[G_Q:G_Q + 1, HD:P], g_q),
                (prow[G_K:G_K + 1, 0:HD], g_k), (prow[G_K:G_K + 1, HD:P], g_k),
                (srow[:, :], sinks),
                (wa2[:, :], w_a2[0]),
                (kc_tok[:, :], cache_k[0, 0].rearrange("t h d -> t (h d)")),
                (vc[:, :], cache_v[0, 0].rearrange("t h d -> t (h d)")),
                (Sin[:, :, :], state[0, 0].rearrange("h k v -> k h v")),
            ]
            assert len(small_loads) == N_SMALL
            for dst, src in small_loads[:9]:
                act.dma_start(dst, src).then_inc(in_small, 16)
            load_rows()
            for dst, src in small_loads[9:]:
                act.dma_start(dst, src).then_inc(in_caches, 16)
            act.preload_act_table_set(LN_EXP)

            act.wait_ge(const_dve, 3)
            for j, (t0, nt) in enumerate(TOK):
                act.wait_ge(in_x[j], 16)
                if j >= 2:
                    act.wait_ge(x_sq, j - 1)
                act.activation(G[j % 2][0:nt, :], xtok[0:nt, j, :], ACT.Square,
                               accum_out=rv[0:nt, j:j + 1]).then_inc(x_sq, 1)
            act.wait_ge(x_sq, NJ)
            link(act.activation(rs[:, 0:NJ], rv[:, 0:NJ], ACT.Ln, scale=1.0 / D, bias=eps[:, :]))
            act.activation(rt[:, 0:NJ], rs[:, 0:NJ], ACT.Exp, scale=-0.5).then_inc(r_ok, 1)
            act.wait_ge(param_ok, 1)
            for c in range(KC):
                if c < RING:
                    high_part(c)
                act.wait_ge(x_turned, c + 1)
                act.activation(h_hi[:, c, :], X[c % 2][:, 0:T], ACT.Copy,
                               scale=param[:, G_MIX + c:G_MIX + c + 1]).then_inc(h_hi_ok, 1)

            def gate_logs(h):
                act.wait_ge(z_done, h + 1)
                if h >= 1:
                    act.wait_ge(z_ln, h)
                act.activation(h2(tB[:, 0:T]), halves(X[h % 2]), ACT.Abs,
                               bias=param[:, B_A + h:B_A + h + 1]).then_inc(z_abs, 1)
                act.wait_ge(z_abs, h + 1)
                link(act.activation(tB[:, 0:T], tB[:, 0:T], ACT.Exp, scale=-1.0))
                if h >= 1:
                    act.wait_ge(cum_ok, h)
                act.activation(tC[:, 0:T], tB[:, 0:T], ACT.Ln, bias=one[:, :]).then_inc(z_ln, 1)

            def gla_exps(h):
                if h >= 2:
                    act.wait_ge(gla_state, h - 1)
                act.wait_ge(cum_ok, HEADS_B)
                act.activation(dec[:, h % 2, :], CB[:, h, :, P], ACT.Exp, scale=1.0 / TAU).then_inc(e_ok, 1)
                act.wait_ge(d_ok, 5 * h + 1)
                act.activation(tB[:, 0:T], tA[:, 0:T], ACT.Exp, scale=1.0 / TAU).then_inc(e_ok, 1)
                act.activation(tC[:, 0:T], tA[:, 0:T], ACT.Exp, scale=-1.0 / TAU).then_inc(e_ok, 1)
                act.wait_ge(d_ok, 5 * h + 2)
                act.activation(tB[:, 0:SEQ], tA[:, 0:SEQ], ACT.Exp, scale=1.0 / TAU).then_inc(e_ok, 1)
                act.wait_ge(d_ok, 5 * h + 3)
                act.activation(tC[:, 0:SEQ], tA[:, 0:SEQ], ACT.Exp, scale=1.0 / TAU).then_inc(e_ok, 1)
                act.wait_ge(d_ok, 5 * h + 4)
                act.activation(tB[:, 0:T], tA[:, 0:T], ACT.Exp, scale=1.0 / TAU).then_inc(e_ok, 1)
                act.wait_ge(d_ok, 5 * h + 5)
                act.activation(tC[:, :].rearrange("p (c n) -> p c n", n=P), CB[:, h, :, 1:P + 1],
                               ACT.Exp, scale=1.0 / TAU).then_inc(e_ok, 1)

            def gla_copy_keys(h):
                act.wait_ge(gla_att, h + 1)
                link(act.activation(kot[:, 0:4, :], XB[3].rearrange("p (c n) -> p c n", c=4), ACT.Copy))
                act.activation(kot[0:DEC, SJ, :], XB[2][0:DEC, P:2 * P], ACT.Copy).then_inc(gla_kot, 1)

            def gla_copy_out(h):
                act.wait_ge(gla_out, h + 1)
                for f in range(2):
                    link(act.activation(obT[:, 2 * h + f, 0:SEQ], XB[2 + f], ACT.Copy))
                    link(act.activation(obT[:, 2 * h + f, SEQ:T], XB[f][:, 0:DEC], ACT.Copy))
                link(act.activation(sq[:, 0, :], obT[:, 2 * h, :], ACT.Square))
                act.activation(sq[:, 1, :], obT[:, 2 * h + 1, :], ACT.Square).then_inc(gla_sq, 1)

            def root(k, ps, scale):
                if k >= 1:
                    act.wait_ge(norm_done, k)
                link(act.activation(h2(rs[:, :]), halves(ps), ACT.Ln, scale=scale, bias=eps[:, :]))
                act.activation(rt[:, :], rs[:, :], ACT.Exp, scale=-0.5).then_inc(r_ok, 1)

            def free_raw(n):
                last = [m for m in POST_TILES if m < n and m % 2 == n % 2]
                if last and IN_TILES[last[-1]][0] in ("kA", "qA"):
                    act.wait_ge(norm_done, NORMS.index(("post", last[-1])) + 1)
                elif last:
                    act.wait_ge(post_done, POST_TILES.index(last[-1]) + 1)

            def read_out(n):
                kind, i, _ = IN_TILES[n]
                s = n % 2
                ps = halves(G[s])
                act.wait_ge(gemm_done, n + 1)
                if kind == "a1":
                    act.activation(h2(a1T[:, :]), ps[0:RANK], ACT.Copy).then_inc(set_free[s], 1)
                elif kind in ("kB", "qB"):
                    if i >= 2:
                        act.wait_ge(gla_out, i - 1)
                    dst = (kT if kind == "kB" else qT)[:, i % 2, :]
                    act.activation(h2(dst), ps, ACT.Copy,
                                   scale=1.0 if kind == "kB" else float(DK) ** -0.5).then_inc(set_free[s], 1)
                elif kind in ("vB", "vA"):
                    free_raw(n)
                    act.activation(h2(raw[:, s, :]), ps, ACT.Copy).then_inc(set_free[s], 1)
                elif kind in ("kA", "qA"):
                    free_raw(n)
                    act.wait_ge(gla_ssq, sum(gla_tile(h, 2) < n for h in range(HEADS_B)))
                    link(act.activation(h2(sq[:, s, :]), ps, ACT.Square))
                    act.activation(h2(raw[:, s, :]), ps, ACT.Copy).then_inc(set_free[s], 1)
                elif kind == "ga":
                    if i == 0:
                        act.wait_ge(gla_norm, HEADS_B)
                        for r in range(2):
                            act.wait_ge(s_out[r], 32 * HEADS_B // 2)
                    act.activation(h2(gaT[:, i, :]), ps, ACT.Tanh, scale=0.5).then_inc(set_free[s], 1)
                elif kind == "rb":
                    if i >= 1:
                        act.wait_ge(set_free[s], uses_before(n))
                    act.activation(h2(th[:, 0, :]), ps, ACT.Tanh, scale=0.5).then_inc(tanh_ok, 1)
                elif kind == "gb":
                    if i >= 1:
                        act.wait_ge(gb_used, i)
                    act.activation(h2(th[:, 1, :]), ps, ACT.Tanh, scale=0.5).then_inc(set_free[s], 1)

            def keys_out():
                act.wait_ge(kt_done, 1)
                link(act.activation(kout[:, 0, :], XB[0][:, 0:2 * P], ACT.Copy))
                link(act.activation(kcT[:, :, :], XB[2][:, 0:2 * P].rearrange("p (u n) -> p u n", u=2), ACT.Copy))
                act.activation(kout[0:DEC, 1, :], XB[1][0:DEC, 0:2 * P], ACT.Copy).then_inc(kt_out, 1)
                act.wait_ge(kt_out, 1)
                act.dma_start(nk_p[0, 0].rearrange("t h d -> t (h d)"), kout[:, 0, :]).then_inc(out_sem, 16)
                act.dma_start(nk_s[0, 0].rearrange("t h d -> t (h d)"), kout[0:DEC, 1, :]).then_inc(out_sem, 16)
                for i in range(2):
                    n = TILE_OF["vA", i]
                    act.wait_ge(set_free[n % 2], uses_before(n) + 2)
                act.dma_start(nv_p[0, 0].rearrange("t h d -> t (h d)"), vA[:, SJ - 1, :]).then_inc(out_sem, 16)
                act.dma_start(nv_s[0, 0].rearrange("t h d -> t (h d)"), vA[0:DEC, SJ, :]).then_inc(out_sem, 16)

            def states_out(h):
                act.wait_ge(gla_state, h + 1)
                act.dma_start(ns_p[0, 0, h], Sfin[:, h % 2, :]).then_inc(s_out[h % 2], 16)
                act.dma_start(ns_s[0, 0, h], Ssmp[:, h % 2, :]).then_inc(s_out[h % 2], 16)

            def unit_exp(u):
                g, j, par, heads, nq, lo, hi = unit_shape(u)
                s = u % NB
                act.wait_ge(smax_ok, u + 1)
                for a in range(2):
                    link(act.activation(prob[0:nq, s, a, lo:hi], prob[0:nq, s, a, lo:hi], ACT.Exp,
                                        bias=nm[0:nq, s, a:a + 1], accum_out=sm[0:nq, s, a:a + 1]))
                act.activation(es[0:nq, s, :], sd[0:nq, s, :], ACT.Exp).then_inc(exp_ok, 1)

            def unit_copy(u):
                g, j, par, heads, nq, lo, hi = unit_shape(u)
                act.wait_ge(pt_done, u + 1)
                if u >= 2:
                    act.wait_ge(pv_done, u - 1)
                src = XB[2].rearrange("p (a k n) -> p a k n", a=2, k=2)
                if j < SJ and lo == 0:
                    act.activation(probT[:, u % 2, :, :, :], src, ACT.Copy).then_inc(pt_copied, 1)
                    return
                for kt in range(lo // P, 2):
                    nk = min(hi - kt * P, P)
                    ins = act.activation(probT[0:nk, u % 2, :, kt, 0:nq], src[0:nk, :, kt, 0:nq], ACT.Copy)
                    if kt == 0:
                        link(ins)
                ins.then_inc(pt_copied, 1)

            def slot(u):
                if 0 <= u < NU:
                    unit_exp(u)
                if LAG_T <= u < NU + LAG_T:
                    unit_copy(u - LAG_T)

            for n in range(N_IN):
                if n == TILE_OF["ga", 1]:
                    act.preload_act_table_set(EXP_TANH)
                if 1 <= n <= HEADS_B:
                    gate_logs(n - 1)
                if n >= 1 and IN_TILES[n - 1][0] in ("kA", "qA"):
                    act.wait_ge(post_done, POST_TILES.index(n - 1) + 1)
                    root(NORMS.index(("post", n - 1)), G[(n - 1) % 2], 1.0 / HD)
                for h in range(HEADS_B):
                    if n == gla_tile(h, 0):
                        gla_copy_keys(h)
                slot(2 * (n - UNIT0))
                read_out(n)
                high_part(n + RING)
                slot(2 * (n - UNIT0) + 1)
                for h in range(HEADS_B):
                    if n == gla_tile(h, 2):
                        states_out(h)
                        gla_copy_out(h)
                    if n == gla_tile(h, 3):
                        act.wait_ge(gla_ssq, h + 1)
                        root(NORMS.index(("gla", h)), X[0], 1.0 / DV)
                for h in range(HEADS_B):
                    if n == GLA_INPUTS[h]:
                        gla_exps(h)
                if n == KEYS_OUT:
                    keys_out()

            act.wait_ge(gemm_done, N_IN)
            for i in range(KC):
                act.wait_ge(m_ok, i + 1)
                act.activation(h_hi[:, i, :], obT[:, i, :], ACT.Copy).then_inc(m_hi_ok, 1)
                if i == 0:
                    act.wait_ge(oa_ok, NU)
                    act.wait_ge(gb_used, KC)
                    load_rows()
            act.wait_ge(out_sem, 64)
            for i in range(KC):
                n = OUT0 + i
                act.wait_ge(xt_done, i + 1)
                if i >= 2:
                    act.wait_ge(set_free[n % 2], uses_before(n))
                act.activation(xTi[:, i % 2, :], X[0][:, 0:T], ACT.Copy).then_inc(xt_ok, 1)
                act.wait_ge(f_in, i + 1)
                if i >= 2:
                    act.wait_ge(x2_ssq, i - 1)
                act.activation(sq[:, i % 2, :], x2T[:, i, :], ACT.Square).then_inc(x2_sq, 1)
                act.activation(f_hi[:, i, :], x2g[:, i % 2, :], ACT.Copy).then_inc(f_hi_ok, 1)
                high_part(n + RING)
            act.wait_ge(x2_ssq, KC)
            act.preload_act_table_set(LN_EXP)
            root(len(NORMS), X[1], 1.0 / D)
            act.preload_act_table_set(EXP_TANH)

            before = 0
            for g, m in enumerate(FF_GROUPS):
                with act.Fori(0, m // 2) as i:
                    for r in range(2):
                        n = GU0[g] + 2 * r
                        act.wait_ge(set_free[n % 2], i * 2 + (uses_before(n) + 1))
                        act.activation(ft[:, r, :], fg[:, r, :], ACT.Tanh, scale=0.5).then_inc(silu_ok, 1)
                        high_part(n + RING, i)
                        act.wait_ge(set_free[(n + 1) % 2], i * 2 + (uses_before(n + 1) + 1))
                        act.activation(h_hi[:, bass.ds(i * 2 + r, 1), :], fa[:, r:r + 1, :], ACT.Copy)\
                            .then_inc(mid_hi_ok, 1)
                        high_part(n + 1 + RING, i)
                before += m
                if g < len(FF_GROUPS) - 1:
                    with act.Fori(0, KC // RING) as i:
                        for t in range(RING):
                            high_part(DN0[g] + t + RING, i)
                else:
                    for n in range(DN0[g] + RING, N_TILES):
                        high_part(n)

            for i in range(KC):
                act.wait_ge(yt_done, i + 1)
                if i >= 2:
                    act.wait_ge(y_out[i % 2], 32 * (i // 2))
                link(act.activation(ytok[:, i % 2, 0:4, :], X[i % 2][:, 0:SEQ].rearrange("p (j n) -> p j n", n=P),
                                    ACT.Copy))
                act.activation(ytok[0:DEC, i % 2, SJ, :], X[i % 2][0:DEC, SEQ:SEQ + P], ACT.Copy).then_inc(y_ok, 1)
                act.wait_ge(y_ok, i + 1)
                c = slice(i * P, (i + 1) * P)
                act.dma_start(y_prompt[0, :, c].rearrange("(j p) n -> p j n", p=P), ytok[:, i % 2, 0:4, :])\
                    .then_inc(y_out[i % 2], 16)
                act.dma_start(y_sample[0, :, c], ytok[0:DEC, i % 2, SJ, :]).then_inc(y_out[i % 2], 16)
            for s in range(2):
                act.wait_ge(y_out[s], 32 * KC // 2)

        @block.vector
        def _(dve):
            steps = [0]

            def link(ins):
                steps[0] += 1
                ins.then_inc(dve_step, 1)
                dve.wait_ge(dve_step, steps[0])

            def refine(x, r, t):
                link(dve.tensor_tensor(t, x, r, ALU.mult))
                link(dve.tensor_tensor(t, t, r, ALU.mult))
                link(dve.tensor_scalar(t, t, -0.5, 1.5, ALU.mult, ALU.add))
                link(dve.tensor_tensor(r, r, t, ALU.mult))

            dve.memset(ones[:, :], 1.0).then_inc(const_dve, 1)
            dve.memset(rv[:, 0:NJ], 1.0).then_inc(const_dve, 1)
            link(dve.memset(one[:, :], 1.0))
            dve.memset(eps[:, :], EPS).then_inc(const_dve, 1)
            link(dve.memset(lab[:, :, :], 0.0))
            link(dve.memset(reset[:, :, :], 1.0))
            link(dve.memset(reset[:, :, 0], 0.0))

            dve.wait_ge(setup_pe, 1)
            link(dve.tensor_copy(param[:, :], XB[0][:, 0:24]))
            link(dve.tensor_scalar(param[:, G_Q:G_Q + 1], param[:, G_Q:G_Q + 1], HD ** -0.5, None, ALU.mult))
            link(dve.tensor_scalar(param[:, G_OB:G_OB + 2], param[:, G_OB:G_OB + 2], 0.25, None, ALU.mult))
            dve.tensor_copy(sinkb[:, :], XB[1][:, 0:HEADS_A]).then_inc(param_ok, 1)

            dve.wait_ge(r_ok, 1)
            link(dve.tensor_scalar(rv[:, 0:NJ], rv[:, 0:NJ], 1.0 / D, EPS, ALU.mult, ALU.add))
            refine(rv[:, 0:NJ], rt[:, 0:NJ], rs[:, 0:NJ])
            for j, (t0, nt) in enumerate(TOK):
                dve.tensor_scalar(xtok[0:nt, j, :], xtok[0:nt, j, :], rt[0:nt, j:j + 1], None, ALU.mult)\
                    .then_inc(x_scaled, 1)
            for c in range(KC):
                dve.wait_ge(h_hi_ok, c + 1)
                dve.scalar_tensor_tensor(out=h_lo[:, c, :], in0=X[c % 2][:, 0:T],
                                         scalar=param[:, G_MIX + c:G_MIX + c + 1],
                                         in1=h_hi[:, c, :].bitcast(F32), op0=ALU.mult, op1=ALU.subtract)\
                    .then_inc(h_ok, 1)
            dve.wait_ge(const_pool, 2)
            link(dve.tensor_scalar(rs[:, 0:2 * P], dist[:, :], -1.0, None, ALU.mult))
            link(dve.tensor_tensor(dist[:, :], dist[:, :], rs[:, 0:2 * P], ALU.max))

            def gate_sums(h):
                dve.wait_ge(z_abs, h + 1)
                if h >= 1:
                    dve.wait_ge(cum_ok, h)
                dve.tensor_scalar(h2(tA[:, 0:T]), halves(X[h % 2]), param[:, B_A + h:B_A + h + 1], 0.0,
                                  ALU.add, ALU.min).then_inc(z_free, 1)
                dve.wait_ge(z_free, h + 1)
                dve.wait_ge(z_ln, h + 1)
                chunks = lambda t: t[:, 0:SEQ].rearrange("p (c n) -> p c n", n=P)
                link(dve.tensor_tensor(lab[:, 0:4, 1:P + 1], chunks(tA), chunks(tC), ALU.subtract))
                link(dve.tensor_tensor(lab[:, SJ, 1:DEC + 1], tA[:, SEQ:T], tC[:, SEQ:T], ALU.subtract))
                dve.tensor_tensor_scan(CB[:, h, :, :].rearrange("p c n -> p (c n)"),
                                       reset[:, :, :].rearrange("p c n -> p (c n)"),
                                       lab[:, :, :].rearrange("p c n -> p (c n)"), 0.0,
                                       ALU.mult, ALU.add).then_inc(cum_ok, 1)

            def gla_inputs(h):
                for kind in ("kB", "qB"):
                    n = TILE_OF[kind, h]
                    dve.wait_ge(set_free[n % 2], uses_before(n) + 1)
                if h >= 1:
                    dve.wait_ge(gla_att, h)
                q, k = qT[:, h % 2, :], kT[:, h % 2, :]
                dve.wait_ge(cum_ok, HEADS_B)
                c = CB[:, h, :, 1:P + 1]

                def by(step, ap, count):
                    return ap.rearrange("p c (b n) -> p c b n", n=step)[:, 0:count]

                mid = CB[:, h, :, 16:P:32].unsqueeze(3).broadcast_to([P, NJ, 4, 32])
                dve.tensor_tensor(by(32, tA[:, :].rearrange("p (c n) -> p c n", n=P), NJ), by(32, c, NJ), mid,
                                  ALU.subtract).then_inc(d_ok, 1)
                dve.wait_ge(e_ok, 7 * h + 2)
                link(dve.tensor_tensor(qL[:, :], q, tB[:, 0:T], ALU.mult))
                dve.wait_ge(e_ok, 7 * h + 3)
                link(dve.tensor_tensor(kL[:, :], k, tC[:, 0:T], ALU.mult))

                def halves_of(w, ap):
                    v = ap.rearrange("p (b a n) -> p b a n", a=2, n=w // 2)
                    return v[:, :, 0], v[:, :, 1]

                def from_boundary(w):
                    d1, d2 = halves_of(w, tA[:, 0:SEQ])
                    nb = P // w
                    cc = CB[:, h, 0:4, 1:P + 1].rearrange("p c (b n) -> p c b n", n=w)
                    edge = CB[:, h, 0:4, w // 2:P:w].unsqueeze(3).broadcast_to([P, 4, nb, w // 2])
                    d1 = d1.rearrange("p (c b) n -> p c b n", b=nb)
                    d2 = d2.rearrange("p (c b) n -> p c b n", b=nb)
                    link(dve.tensor_tensor(d1, edge, cc[:, :, :, 0:w // 2], ALU.subtract))
                    dve.tensor_tensor(d2, cc[:, :, :, w // 2:w], edge, ALU.subtract).then_inc(d_ok, 1)

                def decayed(w, x, t):
                    x1, x2 = halves_of(w, x[:, :])
                    e1, e2 = halves_of(w, t[:, 0:SEQ])
                    k1, _ = halves_of(w, k[:, 0:SEQ])
                    _, q2 = halves_of(w, q[:, 0:SEQ])
                    link(dve.tensor_tensor(x1, k1, e1, ALU.mult))
                    link(dve.tensor_tensor(x2, q2, e2, ALU.mult))

                from_boundary(64)
                dve.wait_ge(e_ok, 7 * h + 4)
                from_boundary(P)
                decayed(64, x32, tB)
                dve.wait_ge(e_ok, 7 * h + 5)
                last = CB[:, h, :, P:P + 1].broadcast_to([P, NJ, P])
                dve.tensor_tensor(tA[:, :].rearrange("p (c n) -> p c n", n=P), last, c, ALU.subtract)\
                    .then_inc(d_ok, 1)
                x1, x2 = halves_of(P, x64[:, :])
                e1, e2 = halves_of(P, tC[:, 0:SEQ])
                link(dve.tensor_tensor(x1, halves_of(P, k[:, 0:SEQ])[0], e1, ALU.mult))
                dve.tensor_tensor(x2, halves_of(P, q[:, 0:SEQ])[1], e2, ALU.mult).then_inc(d_ok, 1)
                dve.wait_ge(d_ok, 5 * h + 5)
                dve.wait_ge(e_ok, 7 * h + 6)
                link(dve.tensor_tensor(k, k, tB[:, 0:T], ALU.mult))
                dve.wait_ge(e_ok, 7 * h + 7)
                dve.tensor_tensor(q, q, tC[:, 0:T], ALU.mult).then_inc(gla_in, 1)

            def gla_mask(h):
                dve.wait_ge(gla_att, h + 1)
                b4 = lambda ap: ap.rearrange("p (c n) -> p c n", n=P)
                link(dve.tensor_tensor(att[:, 0:4, :], b4(XB[0]),
                                       cmask[:, :].unsqueeze(1).broadcast_to([P, 4, P]), ALU.mult))
                link(dve.tensor_copy(att[0:64, 0:4, 64:P], b4(XB[1])[0:64, :, 64:P]))
                for a in (0, 64):
                    link(dve.tensor_copy(att[a:a + 32, 0:4, a + 32:a + 64], b4(XB[1])[a:a + 32, :, a + 32:a + 64]))
                dve.wait_ge(gla_kot, h + 1)
                dve.tensor_tensor(att[0:DEC, SJ, 0:DEC], XB[2][0:DEC, 0:DEC], cmask[0:DEC, 0:DEC],
                                  ALU.mult).then_inc(gla_masked, 1)

            def gla_states(h):
                dve.wait_ge(gla_upd, h + 1)
                if h >= 2:
                    dve.wait_ge(s_out[h % 2], 32 * (h // 2))
                add = lambda c: XB[c // 2][:, (c % 2) * DV:(c % 2 + 1) * DV]
                link(dve.tensor_copy(S[:, 0, :], add(0)))
                for c in range(1, 4):
                    dst = S[:, c, :] if c < 3 else Sfin[:, h % 2, :]
                    link(dve.scalar_tensor_tensor(out=dst, in0=S[:, c - 1, :], scalar=dec[:, h % 2, c:c + 1],
                                                  in1=add(c), op0=ALU.mult, op1=ALU.add))
                dve.scalar_tensor_tensor(out=Ssmp[:, h % 2, :], in0=Sin[:, h, :], scalar=dec[:, h % 2, SJ:SJ + 1],
                                         in1=XB[3][:, 0:DV], op0=ALU.mult, op1=ALU.add).then_inc(gla_state, 1)

            def mean_square(k, ps, scale, read):
                dve.wait_ge(r_ok, k + 2)
                dve.tensor_scalar(h2(rv[:, :]), halves(ps), scale, EPS, ALU.mult, ALU.add).then_inc(*read)

            def gla_norms(h):
                k = NORMS.index(("gla", h))
                mean_square(k, X[0], 1.0 / DV, (gla_norm, 1))
                dve.wait_ge(gla_norm, h + 1)
                refine(rv[:, :], rt[:, :], rs[:, :])
                for f in range(2):
                    o = obT[:, 2 * h + f, :]
                    ins = dve.scalar_tensor_tensor(out=o, in0=o, scalar=param[:, G_OB + f:G_OB + f + 1],
                                                   in1=rt[:, :], op0=ALU.mult, op1=ALU.mult)
                    if f == 0:
                        link(ins)
                ins.then_inc(norm_done, 1)

            def second_use(n):
                kind, i, _ = IN_TILES[n]
                dve.wait_ge(post_done, POST_TILES.index(n) + 1)
                ps, s = G[n % 2], n % 2
                if kind in ("vB", "vA"):
                    dst = vB[:, (i // 2) % 2] if kind == "vB" else vA
                    f = slice((i % 2) * P, (i % 2) * P + P)
                    link(dve.tensor_copy(dst[:, 0:4, f], ps[:, 0:SEQ].rearrange("p (j n) -> p j n", n=P)))
                    dve.tensor_copy(dst[0:DEC, SJ, f], ps[0:DEC, SEQ:SEQ + P]).then_inc(set_free[s], 1)
                else:
                    mean_square(NORMS.index(("post", n)), ps, 1.0 / HD, (set_free[s], 1))
                    dve.wait_ge(set_free[s], uses_before(n) + 2)
                    refine(rv[:, :], rt[:, :], rs[:, :])
                    dst, g = (kAT, G_K) if kind == "kA" else (qAT, G_Q)
                    dve.scalar_tensor_tensor(out=dst[:, i, :], in0=raw[:, s, :], scalar=param[:, g:g + 1],
                                             in1=rt[:, :], op0=ALU.mult, op1=ALU.mult).then_inc(norm_done, 1)

            def biases():
                for r in range(2):
                    dve.wait_ge(s_out[r], 32 * HEADS_B // 2)
                dve.wait_ge(gla_ssq, HEADS_B)
                for h in range(HEADS_A):
                    slope = float(np.float32(2.0 ** (-8.0 * (h + 1) / HEADS_A)))
                    link(dve.tensor_scalar(bias[:, h, :], dist[:, :], -slope, None, ALU.mult))
                link(dve.memset(bias[0:CHUNK, :, 2 * P - CHUNK:2 * P], NEG))
                dve.memset(bias[CHUNK:P, :, 0:CHUNK], NEG).then_inc(bias_ok, 1)
                dve.wait_ge(bias_ok, 1)

            def unit_max(u):
                g, j, par, heads, nq, lo, hi = unit_shape(u)
                s = u % NB
                dve.wait_ge(qk_done, u + 1)
                if u >= NB:
                    dve.wait_ge(pt_done, u - NB + 1)
                for a, head in enumerate(heads):
                    link(dve.tensor_tensor_reduce(
                        prob[0:nq, s, a, lo:hi], XB[u % 2][0:nq, a * 2 * P + lo:a * 2 * P + hi],
                        bias[0:nq, head, lo:hi], 1.0, NEG, ALU.add, ALU.max, mx[0:nq, s, a:a + 1]))
                sink = sinkb[0:nq, heads[0]:heads[1] + 1:2]
                link(dve.tensor_tensor(mx[0:nq, s, :], mx[0:nq, s, :], sink, ALU.max))
                link(dve.tensor_scalar(nm[0:nq, s, :], mx[0:nq, s, :], -1.0, None, ALU.mult))
                dve.tensor_tensor(sd[0:nq, s, :], sink, nm[0:nq, s, :], ALU.add).then_inc(smax_ok, 1)

            def unit_scale(u):
                g, j, par, heads, nq, lo, hi = unit_shape(u)
                s = u % NB
                dve.wait_ge(exp_ok, u + 1)
                link(dve.tensor_tensor(den[0:nq, s, :], sm[0:nq, s, :], es[0:nq, s, :], ALU.add))
                link(dve.reciprocal(rd[0:nq, s, :], den[0:nq, s, :]))
                for a in range(2):
                    o = prob[0:nq, s, a, lo:hi]
                    ins = dve.tensor_scalar(o, o, rd[0:nq, s, a:a + 1], 0.5, ALU.mult, ALU.mult)
                    if a == 0:
                        link(ins)
                ins.then_inc(prob_ok, 1)

            def unit_out(u):
                g, j, par, heads, nq, lo, hi = unit_shape(u)
                dve.wait_ge(pv_done, u + 1)
                for i in (2 * g, 2 * g + 1):
                    n = TILE_OF["ga", i]
                    dve.wait_ge(set_free[n % 2], uses_before(n) + 1)
                r = slice(par * HD, (par + 1) * HD)
                o = gaT[r, 2 * g:2 * g + 2, TOK[j][0]:TOK[j][0] + nq]
                src = XB[3][r, 0:2 * P].rearrange("p (a n) -> p a n", a=2)[:, :, 0:nq]
                dve.scalar_tensor_tensor(out=o, in0=o, scalar=1.0, in1=src, op0=ALU.add, op1=ALU.mult)\
                    .then_inc(oa_ok, 1)

            def slot(u):
                if 1 <= u <= NU:
                    unit_scale(u - 1)
                if 0 <= u < NU:
                    unit_max(u)
                if LAG_V <= u < NU + LAG_V:
                    unit_out(u - LAG_V)

            def gates(n):
                kind, i, _ = IN_TILES[n]
                s = n % 2
                if kind == "rb":
                    dve.wait_ge(tanh_ok, i + 1)
                    dve.scalar_tensor_tensor(out=h2(rbu[:, :]), in0=h2(th[:, 0, :]), scalar=1.0,
                                             in1=halves(G[s]), op0=ALU.add, op1=ALU.mult)\
                        .then_inc(set_free[s], 1)
                    dve.wait_ge(set_free[s], uses_before(n) + 1)
                elif kind == "gb":
                    dve.wait_ge(set_free[s], uses_before(n) + 1)
                    dve.scalar_tensor_tensor(out=rbu[:, :], in0=th[:, 1, :], scalar=1.0, in1=rbu[:, :],
                                             op0=ALU.add, op1=ALU.mult).then_inc(gb_used, 1)
                    dve.wait_ge(gb_used, i + 1)
                    link(dve.tensor_tensor(obT[:, i, :], obT[:, i, :], rbu[:, :], ALU.mult))

            def merge(i):
                dve.wait_ge(oa_ok, 2 * NJ * (i // 2 + 1))
                dve.tensor_tensor(obT[:, i, :], obT[:, i, :], gaT[:, i, :], ALU.add).then_inc(m_ok, 1)

            merged = 0
            for n in range(N_IN):
                if 1 <= n <= HEADS_B:
                    gate_sums(n - 1)
                if n >= 1 and USES[n - 1] == 2:
                    second_use(n - 1)
                for h in range(HEADS_B):
                    if n == gla_tile(h, 0):
                        gla_mask(h)
                    if n == gla_tile(h, 1):
                        gla_states(h)
                slot(2 * (n - UNIT0))
                gates(n)
                slot(2 * (n - UNIT0) + 1)
                for h in range(HEADS_B):
                    if n == gla_tile(h, 3):
                        gla_norms(h)
                for h in range(HEADS_B):
                    if n == GLA_INPUTS[h]:
                        gla_inputs(h)
                if n == TILE_OF["qA", 7]:
                    biases()
                while merged < KC and TILE_OF["gb", merged] <= n and \
                        UNIT0 + (2 * NJ * (merged // 2 + 1) - 1 + LAG_V) // 2 <= n:
                    merge(merged)
                    merged += 1

            dve.wait_ge(gemm_done, N_IN)
            for i in range(KC):
                dve.wait_ge(m_hi_ok, i + 1)
                dve.tensor_tensor(h_lo[:, i, :], obT[:, i, :], h_hi[:, i, :].bitcast(F32), ALU.subtract)\
                    .then_inc(m_lo_ok, 1)
            def f_low_part(c):
                dve.wait_ge(f_hi_ok, c + 1)
                dve.tensor_tensor(f_lo[:, c, :], x2g[:, c % 2, :], f_hi[:, c, :].bitcast(F32), ALU.subtract)\
                    .then_inc(f_ok, 1)

            dve.wait_ge(qk_done, NU)
            dve.wait_ge(out_sem, 64)
            for i in range(KC):
                n = OUT0 + i
                dve.wait_ge(gemm_done, n + 1)
                dve.wait_ge(xt_ok, i + 1)
                dve.tensor_tensor(h2(x2T[:, i, :]), halves(G[n % 2]), h2(xTi[:, i % 2, :]), ALU.add)\
                    .then_inc(set_free[n % 2], 1)
                dve.wait_ge(set_free[n % 2], uses_before(n) + 1)
                if i >= 2:
                    dve.wait_ge(f_ok, i - 1)
                dve.tensor_scalar(x2g[:, i % 2, :], x2T[:, i, :], param[:, G_FFN + i:G_FFN + i + 1], None,
                                  ALU.mult).then_inc(f_in, 1)
                if i >= 1:
                    f_low_part(i - 1)
            f_low_part(KC - 1)
            k = len(NORMS)
            mean_square(k, X[1], 1.0 / D, (norm_done, 1))
            dve.wait_ge(norm_done, k + 1)
            refine(rv[:, :], rt[:, :], rs[:, :])

            dve.wait_ge(xt_done, KC)
            before = 0
            for g, m in enumerate(FF_GROUPS):
                with dve.Fori(0, m // 2) as i:
                    for r in range(2):
                        n = GU0[g] + 2 * r
                        s, s1 = n % 2, (n + 1) % 2
                        gate = i * 2 + (before + r + 1)
                        dve.wait_ge(gemm_done, i * RING + (n + 1))
                        dve.tensor_tensor(h2(fg[:, r, :]), halves(G[s]), h2(rt[:, :]), ALU.mult)\
                            .then_inc(set_free[s], 1)
                        dve.wait_ge(set_free[s], i * 2 + (uses_before(n) + 1))
                        dve.wait_ge(silu_ok, gate)
                        dve.scalar_tensor_tensor(out=fs[:, r, :], in0=ft[:, r, :], scalar=1.0,
                                                 in1=fg[:, r, :], op0=ALU.add, op1=ALU.mult)\
                            .then_inc(fs_ok, 1)
                        dve.wait_ge(fs_ok, gate)
                        dve.scalar_tensor_tensor(out=fs[:, r, :], in0=fs[:, r, :], scalar=0.5,
                                                 in1=rt[:, :], op0=ALU.mult, op1=ALU.mult)\
                            .then_inc(fr_ok, 1)
                        dve.wait_ge(fr_ok, gate)
                        dve.wait_ge(gemm_done, i * RING + (n + 2))
                        dve.tensor_tensor(h2(fa[:, r, :]), h2(fs[:, r, :]), halves(G[s1]), ALU.mult)\
                            .then_inc(set_free[s1], 1)
                        dve.wait_ge(set_free[s1], i * 2 + (uses_before(n + 1) + 1))
                        dve.wait_ge(mid_hi_ok, gate)
                        at = bass.ds(i * 2 + r, 1)
                        dve.tensor_tensor(h_lo[:, at, :], fa[:, r:r + 1, :], h_hi[:, at, :].bitcast(F32),
                                          ALU.subtract).then_inc(mid_ok, 1)
                before += m
                with dve.Fori(0, KC // RING) as i:
                    for t in range(RING):
                        n = DN0[g] + t
                        dve.wait_ge(gemm_done, i * RING + (n + 1))
                        x = x2T[:, bass.ds(i * RING + t, 1), :].rearrange("p a (b n) -> p (a b) n", b=2)
                        dve.tensor_tensor(x, halves(G[n % 2]), x, ALU.add).then_inc(set_free[n % 2], 1)


_INS = ["x_prompt", "x_sample", "cache_swa_k", "cache_swa_v", "state_gla", "w_in", "w_a2", "b_a", "g_q", "g_k",
        "sinks", "g_ob", "w_out", "g_mix", "g_ffn", "w_gate", "w_up", "w_down"]
_OUTS = [(1, SEQ, D), (1, DEC, D), (1, 1, WINDOW, KV_A, HD), (1, 1, WINDOW, KV_A, HD),
         (1, 1, HEADS_B, DK, DV), (1, 1, DEC, KV_A, HD), (1, 1, DEC, KV_A, HD), (1, 1, HEADS_B, DK, DV)]


def kernel(**inputs):
    import concourse.bacc as bacc
    from concourse.bass_utils import run_bass_kernel_spmd

    nc = bacc.Bacc("TRN2", target_bir_lowering=False, num_devices=1)
    arrays, args = {}, []
    for name in _INS:
        a = np.ascontiguousarray(inputs[name])
        arrays[f"in_{name}_dram"] = a
        args.append(nc.dram_tensor(f"in_{name}_dram", a.shape, mybir.dt.from_np(a.dtype),
                                   kind="ExternalInput").ap())
    for i, shape in enumerate(_OUTS):
        args.append(nc.dram_tensor(f"out_{i}_dram", shape, F32, kind="ExternalOutput").ap())
    mixer_program(nc, *args)
    r = run_bass_kernel_spmd(nc, [arrays], core_ids=[0])
    return tuple(r.results[0][f"out_{i}_dram"] for i in range(len(_OUTS)))
```

```python
from contextlib import ExitStack

import numpy as np

import concourse.bass as bass
from concourse import mybir

F32 = mybir.dt.float32
F32R = mybir.dt.float32r
ALU = mybir.AluOpType
ACT = mybir.ActivationFunctionType

P = 128
D = 1024
SEQ = 512
DEC = 32
T = SEQ + DEC
TH = T // 2
KC = D // P
EPS = 1e-6
NEG = -1e30
HEADS_A, KV_A, HD = 16, 4, 64
CHUNK, WINDOW = 64, 128
HEADS_B, DK, DV = 4, 128, 256
RANK = 16
TAU = 16.0
O_QA, O_KA, O_VA = 0, 1024, 1280
O_QB, O_KB, O_VB, O_RB = 1536, 2048, 2560, 3584
O_A1, O_GA, O_GB = 4608, 4624, 5648

RING = 4
LN_EXP, EXP_TANH = "natural_log_exp_and_others", "exp_and_others"
TOK = [(j * P, P) for j in range(SEQ // P)] + [(SEQ, DEC)]
NJ = len(TOK)
SJ = NJ - 1
ROWS_ACT, ROWS_DVE = (0, 2, 4), (1, 3)
SCALE_ACT, SCALE_DVE = (0, 2), (1, 3, 4)


def input_tiles():
    tiles = [("a1", 0, [(O_A1, P)])]
    for h in range(HEADS_B):
        tiles += [("kB", h, [(O_KB + h * DK, P)]), ("qB", h, [(O_QB + h * DK, P)])]
        tiles += [("vB", 2 * h + f, [(O_VB + h * DV + f * P, P)]) for f in range(2)]
    tiles += [("kA", i, [(O_KA + i * P, P)]) for i in range(2)]
    tiles += [("vA", i, [(O_VA + i * P, P)]) for i in range(2)]
    tiles += [("qA", 4 * u + i, [(O_QA + (8 * u + i) * HD, HD), (O_QA + (8 * u + 4 + i) * HD, HD)])
              for u in range(2) for i in range(4)]
    tiles += [("ga", i, [(O_GA + i * P, P)]) for i in range(KC)]
    for i in range(KC):
        tiles += [("rb", i, [(O_RB + i * P, P)]), ("gb", i, [(O_GB + i * P, P)])]
    return tiles


IN_TILES = input_tiles()
N_IN = len(IN_TILES)
TILE_OF = {(kind, i): n for n, (kind, i, _) in enumerate(IN_TILES)}
OUT0 = N_IN
FF_GROUPS = [8, 8, 6]
GU0, DN0 = [], []
_n = OUT0 + KC
for _m in FF_GROUPS:
    GU0.append(_n)
    DN0.append(_n + 2 * _m)
    _n += 2 * _m + KC
N_TILES = _n
N_SMALL = 7

USES = [2 if kind in ("vB", "vA", "kA", "qA") else 1 for kind, _, _ in IN_TILES]
USES += [1] * (N_TILES - N_IN)
POST_TILES = [n for n in range(N_IN) if USES[n] == 2]


def uses_before(n):
    return sum(USES[m] for m in range(n % 2, n, 2))


UNITS = [(g, j, par) for g in range(KV_A) for j in range(NJ) for par in range(2)]
NU = len(UNITS)
NB = 4
LAG_T, LAG_V = 3, 4
UNIT0 = TILE_OF["ga", 1]
EARLY = 3
SOON = 5
KEYS_OUT = TILE_OF["qA", 2]
BIAS0 = TILE_OF["qA", 1]


def gla_tile(h, step):
    return 7 + 4 * h + (0, 1, 1, 2)[step]


def gate_tile(h):
    return 1 + h // 2


GLA_INPUTS = [4 * h + (4 if h else 3) for h in range(HEADS_B)]
GLA_FINISH = [n + (2 if h == HEADS_B - 1 else 1) for h, n in enumerate(GLA_INPUTS)]


def norm_order():
    order = []
    for n in range(N_IN + 1):
        if n >= 1 and IN_TILES[n - 1][0] in ("kA", "qA"):
            order.append(("post", n - 1))
        order += [("gla", h) for h in range(HEADS_B) if n == gla_tile(h, 3)]
    return order


NORMS = norm_order()


def unit_shape(u):
    g, j, par = UNITS[u]
    heads = (4 * g + par, 4 * g + 2 + par)
    lo = P if j == 0 else 0
    hi = P + DEC if j == SJ else 2 * P
    return g, j, par, heads, TOK[j][1], lo, hi


def mixer_program(nc, x_prompt, x_sample, cache_k, cache_v, state, w_in, w_a2, b_a, g_q, g_k, sinks,
                  g_ob, w_out, g_mix, g_ffn, w_gate, w_up, w_down,
                  y_prompt, y_sample, nk_p, nv_p, ns_p, nk_s, nv_s, ns_s):
    with ExitStack() as ctx:
        def sem(name):
            return ctx.enter_context(nc.semaphore(name))

        def tensor(where, name, shape, dt=F32):
            return where.enter_context(nc.sbuf_tensor(name, shape, dt))

        h_hi = tensor(ctx, "h_hi", [P, KC, T], F32R)
        h_lo = tensor(ctx, "h_lo", [P, KC, T], F32R)
        wraw = tensor(ctx, "wraw", [P, RING, KC, P])
        w_hi = tensor(ctx, "w_hi", [P, RING, KC, P], F32R)
        w_lo = tensor(ctx, "w_lo", [P, RING, KC, P], F32R)
        ident = tensor(ctx, "ident", [P, P])
        ones = tensor(ctx, "ones", [P, P])
        head_ones = tensor(ctx, "head_ones", [P, P])
        param = tensor(ctx, "param", [P, 24])
        eps = tensor(ctx, "eps", [P, 1])
        one = tensor(ctx, "one", [P, 1])
        sinkb = tensor(ctx, "sinkb", [P, HEADS_A])
        dist = tensor(ctx, "dist", [P, 2 * P])
        sq = tensor(ctx, "sq", [P, 2, T])
        rs = tensor(ctx, "rs", [P, T])
        rt = tensor(ctx, "rt", [P, T])
        rv = tensor(ctx, "rv", [P, T])
        G_MIX, G_FFN, B_A, G_OB, G_Q, G_K = 0, 8, 16, 20, 22, 23

        mix = ExitStack()
        obT = tensor(mix, "obT", [P, KC, T])
        kAT = tensor(mix, "kAT", [P, 2, T])
        kcT = tensor(mix, "kcT", [P, 2, P])
        vA = tensor(mix, "vA", [P, NJ, KV_A * HD])
        vc = tensor(mix, "vc", [P, KV_A * HD])
        raw = tensor(mix, "raw", [P, 2, T])
        kout = tensor(mix, "kout", [P, 2, 2 * P])

        gla = ExitStack()
        Sin = tensor(gla, "Sin", [P, HEADS_B, DV])
        wa2 = tensor(gla, "wa2", [RANK, HEADS_B * DK])
        prow = tensor(gla, "prow", [24, P])
        srow = tensor(gla, "srow", [1, HEADS_A])
        kc_tok = tensor(gla, "kc_tok", [P, KV_A * HD])
        cmask = tensor(gla, "cmask", [P, P])
        reset = tensor(gla, "reset", [P, NJ, P + 1])
        lab = tensor(gla, "lab", [P, NJ, P + 1])
        a1T = tensor(gla, "a1T", [RANK, T])
        CB = tensor(gla, "CB", [P, HEADS_B, NJ, P + 1])
        dec = tensor(gla, "dec", [P, 2, NJ])
        att = tensor(gla, "att", [P, NJ, P])
        kot = tensor(gla, "kot", [P, NJ, P])
        S = tensor(gla, "S", [P, 3, DV])
        qT = tensor(gla, "qT", [P, 2, T])
        kT = tensor(gla, "kT", [P, 2, T])
        qL = tensor(gla, "qL", [P, T])
        kL = tensor(gla, "kL", [P, T])
        x32 = tensor(gla, "x32", [P, SEQ])
        x64 = tensor(gla, "x64", [P, SEQ])
        tA = tensor(gla, "tA", [P, NJ * P])
        tB = tensor(gla, "tB", [P, NJ * P])
        tC = tensor(gla, "tC", [P, NJ * P])
        vB = tensor(gla, "vB", [P, 2, NJ, DV])
        Ssmp = tensor(gla, "Ssmp", [P, 2, DV])
        Sfin = tensor(gla, "Sfin", [P, 2, DV])
        gla.close()

        att_mem = ExitStack()
        gaT = tensor(att_mem, "gaT", [P, KC, T])
        qAT = tensor(att_mem, "qAT", [P, KC, T])
        bias = tensor(att_mem, "bias", [P, HEADS_A, 2 * P])
        prob = tensor(att_mem, "prob", [P, NB, 2, 2 * P])
        probT = tensor(att_mem, "probT", [P, 2, 2, 2, P])
        th = tensor(att_mem, "th", [P, 2, T])
        rbu = tensor(att_mem, "rbu", [P, T])
        mx = tensor(att_mem, "mx", [P, NB, 2])
        nm = tensor(att_mem, "nm", [P, NB, 2])
        sd = tensor(att_mem, "sd", [P, NB, 2])
        es = tensor(att_mem, "es", [P, NB, 2])
        sm = tensor(att_mem, "sm", [P, NB, 2])
        den = tensor(att_mem, "den", [P, NB, 2])
        rd = tensor(att_mem, "rd", [P, NB, 2])
        att_mem.close()

        early = ExitStack()
        e_hi = tensor(early, "e_hi", [P, EARLY, T], F32R)
        e_lo = tensor(early, "e_lo", [P, EARLY, T], F32R)
        early.close()

        rows = ExitStack()
        ffn_work = ExitStack()
        tensor(rows, "gap_gaT", [P, KC, T])
        x2T = tensor(rows, "x2T", [P, KC, T])
        xtok = tensor(rows, "xtok", [P, NJ, D])
        xTi = tensor(rows, "xTi", [P, 2, T])
        x2g = tensor(rows, "x2g", [P, 2, T])
        rows.close()
        tensor(ffn_work, "gap_rows", [P, 2 * KC, T])
        ft = tensor(ffn_work, "ft", [P, 2, T])
        fs = tensor(ffn_work, "fs", [P, 2, T])
        fa = tensor(ffn_work, "fa", [P, 2, T])
        fg = tensor(ffn_work, "fg", [P, 2, T])
        ytok = tensor(ffn_work, "ytok", [P, 2, NJ, P])
        ffn_work.close()
        mix.close()

        f_mem = ExitStack()
        f_hi = tensor(f_mem, "f_hi", [P, KC, T], F32R)
        f_lo = tensor(f_mem, "f_lo", [P, KC, T], F32R)
        f_mem.close()

        G = [ctx.enter_context(nc.psum_tensor(f"G{s}", [P, 2 * 512], F32)) for s in range(2)]
        X = [ctx.enter_context(nc.psum_tensor(f"X{s}", [P, 2 * 512], F32)) for s in range(2)]
        XB = [X[b // 2][:, 512 * (b % 2):512 * (b % 2) + 512] for b in range(4)]
        TURNED = [X[0], X[1], G[1]]

        def halves(ps):
            return ps[:, :].rearrange("p (b n) -> p b n", b=2)[:, :, 0:TH]

        def h2(ap):
            return ap.rearrange("p (b n) -> p b n", b=2)

        wload = [sem(f"wload{r}") for r in range(RING)]
        w_split = sem("w_split")
        pool_step = sem("pool_step")
        gemm_done = sem("gemm_done")
        set_free = [sem("set_free0"), sem("set_free1")]
        post_done = sem("post_done")
        in_x = [sem(f"in_x{j}") for j in range(NJ)]
        in_small = sem("in_small")
        in_caches = sem("in_caches")
        hi_done = sem("hi_done")
        const_pool = sem("const_pool")
        const_dve = sem("const_dve")
        act_step = sem("act_step")
        dve_step = sem("dve_step")
        setup_pe = sem("setup_pe")
        param_ok = sem("param_ok")
        x_sq = sem("x_sq")
        x_sums = sem("x_sums")
        x_root = sem("x_root")
        x_scaled_act = sem("x_scaled_act")
        x_scaled_dve = sem("x_scaled_dve")
        x_turned = sem("x_turned")
        h_hi_ok = sem("h_hi_ok")
        h_ok = sem("h_ok")
        r_ok = sem("r_ok")
        norm_done = sem("norm_done")
        z_done = sem("z_done")
        z_abs = sem("z_abs")
        z_free = sem("z_free")
        z_ln = sem("z_ln")
        cum_ok = sem("cum_ok")
        d_ok = sem("d_ok")
        e_ok = sem("e_ok")
        gla_in = sem("gla_in")
        gla_att = sem("gla_att")
        gla_masked = sem("gla_masked")
        gla_kot = sem("gla_kot")
        gla_upd = sem("gla_upd")
        gla_state = sem("gla_state")
        gla_out = sem("gla_out")
        gla_sq = sem("gla_sq")
        gla_sum = sem("gla_sum")
        gla_ssq = sem("gla_ssq")
        gla_norm = sem("gla_norm")
        kt_done = sem("kt_done")
        kt_out = sem("kt_out")
        out_sem = sem("out_sem")
        s_out = [sem("s_out0"), sem("s_out1")]
        qk_done = sem("qk_done")
        smax_ok = sem("smax_ok")
        exp_ok = sem("exp_ok")
        prob_ok = sem("prob_ok")
        pt_done = sem("pt_done")
        pt_copied = sem("pt_copied")
        pv_done = sem("pv_done")
        oa_ok = sem("oa_ok")
        tanh_ok = sem("tanh_ok")
        gb_used = sem("gb_used")
        m_ok = sem("m_ok")
        m_hi_ok = sem("m_hi_ok")
        m_lo_ok = sem("m_lo_ok")
        xt_done = sem("xt_done")
        xt_ok = sem("xt_ok")
        x2_sq = sem("x2_sq")
        x2_sum = sem("x2_sum")
        x2_ssq = sem("x2_ssq")
        f_in = sem("f_in")
        f_hi_ok = sem("f_hi_ok")
        f_ok = sem("f_ok")
        silu_ok = sem("silu_ok")
        fs_ok = sem("fs_ok")
        fr_ok = sem("fr_ok")
        mid_hi_ok = sem("mid_hi_ok")
        mid_ok = sem("mid_ok")
        yt_done = sem("yt_done")
        y_ok = sem("y_ok")
        y_out = [sem("y_out0"), sem("y_out1")]

        block = ctx.enter_context(nc.Block())

        @block.sync
        def _(sp):
            def load_rows(js):
                for j in js:
                    t0, nt = TOK[j]
                    src = x_sample[0] if j == SJ else x_prompt[0, t0:t0 + nt, :]
                    sp.dma_start(xtok[0:nt, j, :], src).then_inc(in_x[j], 16)

            def twice(g):
                return g.unsqueeze(1).broadcast_to([1, 2, HD])

            load_rows(range(NJ))
            for dst, src in [
                    (prow[G_MIX:G_MIX + 8, :], g_mix[0].rearrange("(r n) -> r n", n=P)),
                    (prow[G_FFN:G_FFN + 8, :], g_ffn[0].rearrange("(r n) -> r n", n=P)),
                    (prow[B_A:B_A + 4, :], b_a[0].rearrange("(r n) -> r n", n=P)),
                    (prow[G_OB:G_OB + 2, :], g_ob[0].rearrange("(r n) -> r n", n=P)),
                    (prow[G_Q:G_Q + 1, :].rearrange("r (a n) -> r a n", a=2), twice(g_q)),
                    (prow[G_K:G_K + 1, :].rearrange("r (a n) -> r a n", a=2), twice(g_k)),
                    (srow[:, :], sinks)]:
                sp.dma_start(dst, src).then_inc(in_small, 16)

            for n, (_kind, _i, runs) in enumerate(IN_TILES):
                if n == 1:
                    sp.wait_ge(in_small, 16 * N_SMALL)
                    sp.wait_ge(in_x[SJ], 16)
                if n >= RING:
                    sp.wait_ge(w_split, n - RING + 1)
                at = 0
                for col, width in runs:
                    src = w_in[0, :, col:col + width].rearrange("(k p) n -> p k n", p=P)
                    sp.dma_start(wraw[:, n % RING, :, at:at + width], src).then_inc(
                        wload[n % RING], 32 // len(runs))
                    at += width
                if n == RING - 1:
                    for dst, src in [(wa2[:, :], w_a2[0]),
                                     (kc_tok[:, :], cache_k[0, 0].rearrange("t h d -> t (h d)")),
                                     (vc[:, :], cache_v[0, 0].rearrange("t h d -> t (h d)")),
                                     (Sin[:, :, :], state[0, 0].rearrange("h k v -> k h v"))]:
                        sp.dma_start(dst, src).then_inc(in_caches, 16)

            def stream(n0, turns, source, kc=KC):
                with sp.Fori(0, turns) as i:
                    for t in range(RING):
                        sp.wait_ge(w_split, i * RING + (n0 + t - RING + 1))
                        slot = (n0 + t) % RING
                        sp.dma_start(wraw[:, slot, 0:kc, :], source(i, t)).then_inc(wload[slot], 32)

            def block_of(w, row0, kc, col):
                return w[0, row0:row0 + kc * P, bass.ds(col, P)].rearrange("(k p) n -> p k n", p=P)

            stream(OUT0, 1, lambda i, t: block_of(w_out, 0, KC, t * P))
            sp.wait_ge(pt_done, NU)
            load_rows(range(NJ))
            stream(OUT0 + RING, KC // RING - 1, lambda i, t: block_of(w_out, 0, KC, (i + 1) * (RING * P) + t * P))
            f0 = 0
            for g, m in enumerate(FF_GROUPS):
                stream(GU0[g], 2 * m // RING, lambda i, t: block_of(
                    (w_gate, w_up)[t % 2], 0, KC, i * (2 * P) + (f0 + t // 2) * P))
                stream(DN0[g], KC // RING, lambda i, t: block_of(
                    w_down, f0 * P, m, i * (RING * P) + t * P), kc=m)
                f0 += m

        @block.gpsimd
        def _(pool):
            pool.memset(ident[:, :], 0.0).then_inc(pool_step, 1)
            pool.memset(cmask[:, :], 1.0).then_inc(pool_step, 1)
            pool.wait_ge(pool_step, 2)
            pool.affine_select(out=ident[:, :], in_=ident[:, :], compare_op=ALU.not_equal, fill=1.0,
                               base=0, pattern=[[-1, P]], channel_multiplier=1).then_inc(const_pool, 1)
            pool.iota(dist[:, :], pattern=[[-1, 2 * P]], base=P, channel_multiplier=1,
                      allow_small_or_imprecise_dtypes=True).then_inc(const_pool, 1)
            pool.affine_select(out=cmask[:, :], in_=cmask[:, :], compare_op=ALU.is_ge, fill=0.0,
                               base=0, pattern=[[1, P]], channel_multiplier=-1).then_inc(pool_step, 1)
            pool.wait_ge(pool_step, 3)
            cm = cmask[:, :].rearrange("p (b n) -> p b n", b=4)
            pool.affine_select(out=cm, in_=cm, compare_op=ALU.is_ge, fill=0.0, base=0,
                               pattern=[[-32, 4], [0, 32]], channel_multiplier=1).then_inc(const_pool, 1)

            def low_part(slot):
                pool.tensor_tensor(w_lo[:, slot, :, :], wraw[:, slot, :, :],
                                   w_hi[:, slot, :, :].bitcast(F32), ALU.subtract).then_inc(w_split, 1)

            for n in range(RING):
                pool.wait_ge(hi_done, n + 1)
                low_part(n)
            with pool.Fori(1, N_TILES // RING) as i:
                for t in range(RING):
                    pool.wait_ge(hi_done, i * RING + (t + 1))
                    low_part(t)
            for n in range(N_TILES // RING * RING, N_TILES):
                pool.wait_ge(hi_done, n + 1)
                low_part(n % RING)

        @block.tensor
        def _(pe):
            def chunk(slot, ps, kc, last, b_hi, b_lo):
                for b in range(2):
                    cols = slice(b * TH, (b + 1) * TH)
                    o = ps[:, 512 * b:512 * b + TH]
                    pe.matmul(o, w_hi[:, slot, kc, :], b_hi[:, kc, cols], start=(kc == 0), stop=False)
                    pe.matmul(o, w_hi[:, slot, kc, :], b_lo[:, kc, cols], start=False, stop=False)
                    mm = pe.matmul(o, w_lo[:, slot, kc, :], b_hi[:, kc, cols], start=False, stop=(kc == last))
                return mm

            pe.wait_ge(const_pool, 1)
            pe.wait_ge(const_dve, 1)
            pe.wait_ge(in_small, 16 * N_SMALL)
            pe.transpose(G[0][:, 0:24], prow[:, :], ident[0:24, 0:24])
            pe.matmul(G[0][:, 512:512 + HEADS_A], ones[0:1, :], srow[:, :], start=True, stop=True)\
                .then_inc(setup_pe, 1)


            def turn_input(c):
                if c % (KC // 2) == 0:
                    pe.wait_ge(x_scaled_act, len(SCALE_ACT) * (1 + c // (KC // 2)))
                    pe.wait_ge(x_scaled_dve, len(SCALE_DVE) * (1 + c // (KC // 2)))
                if c >= 3:
                    pe.wait_ge(h_ok, c - 2)
                for j, (t0, nt) in enumerate(TOK):
                    mm = pe.transpose(TURNED[c % 3][:, t0:t0 + nt], xtok[0:nt, j, c * P:(c + 1) * P],
                                      ident[0:nt, 0:nt])
                mm.then_inc(x_turned, 1)

            for c in range(3):
                turn_input(c)

            def gate_logits(h):
                pe.wait_ge(set_free[0], 1)
                pe.wait_ge(in_caches, 16 * 4)
                pe.wait_ge(h_ok, KC)
                if h >= 2:
                    pe.wait_ge(z_free, h - 1)
                for b in range(2):
                    mm = pe.matmul(X[h % 2][:, 512 * b:512 * b + TH], wa2[:, h * DK:(h + 1) * DK],
                                   a1T[:, b * TH:(b + 1) * TH], start=True, stop=True)
                mm.then_inc(z_done, 1)

            def second_use(n):
                ps = G[n % 2]
                pe.wait_ge(set_free[n % 2], uses_before(n) + 1)
                if IN_TILES[n][0] in ("vB", "vA"):
                    for j, (t0, nt) in enumerate(TOK):
                        mm = pe.transpose(ps[0:nt, j * P:(j + 1) * P], raw[:, n % 2, t0:t0 + nt], ident[:, :])
                else:
                    for b in range(2):
                        mm = pe.matmul(ps[:, 512 * b:512 * b + TH], head_ones[:, :],
                                       sq[:, n % 2, b * TH:(b + 1) * TH], start=True, stop=True)
                mm.then_inc(post_done, 1)

            def gla_scores(h):
                pe.wait_ge(gla_in, h + 1)
                pe.wait_ge(z_free, HEADS_B)
                if h >= 1:
                    pe.wait_ge(gla_norm, h)
                for c in range(NJ - 1):
                    k = slice(c * P, (c + 1) * P)
                    pe.matmul(XB[0][:, k], kL[:, k], qL[:, k], start=True, stop=True)
                    pe.matmul(XB[1][0:64, c * P + 64:(c + 1) * P], x64[:, c * P:c * P + 64],
                              x64[:, c * P + 64:(c + 1) * P], start=True, stop=True)
                    for a in (0, 64):
                        pe.matmul(XB[1][a:a + 32, c * P + a + 32:c * P + a + 64], x32[:, c * P + a:c * P + a + 32],
                                  x32[:, c * P + a + 32:c * P + a + 64], start=True, stop=True)
                    pe.transpose(XB[3][:, k], kT[:, h % 2, k], ident[:, :])
                s = slice(SEQ, T)
                pe.matmul(XB[2][0:DEC, 0:DEC], kL[:, s], qL[:, s], start=True, stop=True)
                pe.transpose(XB[2][0:DEC, P:2 * P], kT[:, h % 2, s], ident[:, :]).then_inc(gla_att, 1)

            def gla_updates(h):
                pe.wait_ge(gla_masked, h + 1)
                pe.wait_ge(gla_kot, h + 1)
                for f in range(2):
                    n = TILE_OF["vB", 2 * h + f]
                    pe.wait_ge(set_free[n % 2], uses_before(n) + 2)
                for c in range(NJ - 1):
                    pe.matmul(XB[c // 2][:, (c % 2) * DV:(c % 2 + 1) * DV], kot[:, c, :],
                              vB[:, h % 2, c, :], start=True, stop=True)
                pe.matmul(XB[3][:, 0:DV], kot[0:DEC, SJ, :], vB[0:DEC, h % 2, SJ, :],
                          start=True, stop=True).then_inc(gla_upd, 1)

            def gla_outputs(h):
                pe.wait_ge(gla_state, h + 1)
                for f in range(2):
                    v = slice(f * P, (f + 1) * P)
                    for c in range(NJ - 1):
                        k = slice(c * P, (c + 1) * P)
                        pe.matmul(XB[2 + f][:, k], vB[:, h % 2, c, v], att[:, c, :], start=True, stop=(c == 0))
                        if c >= 1:
                            pe.matmul(XB[2 + f][:, k], S[:, c - 1, v], qT[:, h % 2, k], start=False, stop=True)
                    pe.matmul(XB[f][:, 0:DEC], vB[0:DEC, h % 2, SJ, v], att[0:DEC, SJ, 0:DEC],
                              start=True, stop=False)
                    mm = pe.matmul(XB[f][:, 0:DEC], Sin[:, h, v], qT[:, h % 2, SEQ:T], start=False, stop=True)
                mm.then_inc(gla_out, 1)

            def gla_squares(h):
                pe.wait_ge(gla_sum, h + 1)
                for b in range(2):
                    mm = pe.matmul(X[0][:, 512 * b:512 * b + TH], ones[:, :],
                                   sq[:, 0, b * TH:(b + 1) * TH], start=True, stop=True)
                mm.then_inc(gla_ssq, 1)

            def keys_out():
                pe.wait_ge(norm_done, NORMS.index(("post", TILE_OF["kA", 1])) + 1)
                pe.wait_ge(gla_norm, HEADS_B)
                for u in range(2):
                    pe.transpose(XB[0][:, u * P:(u + 1) * P], kAT[:, u, SEQ - P:SEQ], ident[:, :])
                    pe.transpose(XB[1][0:DEC, u * P:(u + 1) * P], kAT[:, u, SEQ:T], ident[:, :])
                    mm = pe.transpose(XB[2][:, u * P:(u + 1) * P], kc_tok[:, u * P:(u + 1) * P], ident[:, :])
                mm.then_inc(kt_done, 1)

            def unit_scores(u):
                g, j, par, heads, nq, lo, hi = unit_shape(u)
                if u == 0:
                    pe.wait_ge(kt_out, 1)
                    pe.wait_ge(norm_done, len(NORMS))
                if u >= 2:
                    pe.wait_ge(smax_ok, u - 1)
                hf = slice((g % 2) * HD, (g % 2) * HD + HD)
                t0 = TOK[j][0]
                for a, head in enumerate(heads):
                    q = qAT[hf, 4 * (g // 2) + head % 4, t0:t0 + nq]
                    o = XB[u % 2][0:nq, a * 2 * P:(a + 1) * 2 * P]
                    if j == SJ:
                        pe.matmul(o[:, 0:P], q, kcT[hf, g // 2, :], start=True, stop=True)
                        mm = pe.matmul(o[:, P:P + DEC], q, kAT[hf, g // 2, SEQ:T], start=True, stop=True)
                    else:
                        mm = pe.matmul(o[:, lo:hi], q, kAT[hf, g // 2, t0 - P + lo:t0 - P + hi],
                                       start=True, stop=True)
                mm.then_inc(qk_done, 1)

            def unit_turn(u):
                g, j, par, heads, nq, lo, hi = unit_shape(u)
                pe.wait_ge(prob_ok, u + 1)
                if u >= 1:
                    pe.wait_ge(pt_copied, u)
                for a in range(2):
                    for kt in range(lo // P, 2):
                        nk = min(hi - kt * P, P)
                        c0 = (2 * a + kt) * P
                        mm = pe.transpose(XB[2][0:nk, c0:c0 + nq], prob[0:nq, u % NB, a, kt * P:kt * P + nk],
                                          ident[0:nq, 0:nq])
                mm.then_inc(pt_done, 1)

            def unit_values(u):
                g, j, par, heads, nq, lo, hi = unit_shape(u)
                pe.wait_ge(pt_copied, u + 1)
                if u >= 1:
                    pe.wait_ge(oa_ok, u)
                o = XB[3][par * HD:(par + 1) * HD, 0:2 * P].rearrange("p (a n) -> p a n", a=2)[:, :, 0:nq]
                for kt in range(lo // P, 2):
                    nk = min(hi - kt * P, P)
                    if j == SJ:
                        v = vc[:, g * HD:(g + 1) * HD] if kt == 0 else vA[0:nk, SJ, g * HD:(g + 1) * HD]
                    else:
                        v = vA[:, j - 1 + kt, g * HD:(g + 1) * HD]
                    mm = pe.matmul(o, v, probT[0:nk, u % 2, :, kt, 0:nq], start=(kt == lo // P), stop=(kt == 1))
                mm.then_inc(pv_done, 1)

            beside = {}

            def put(n, k, step, *args):
                beside.setdefault((n, k), []).append((step, args))

            for c in range(3, KC):
                put(0, c - 3, turn_input, c)
            for h in range(HEADS_B):
                put(gate_tile(h), 2 + 4 * (h % 2), gate_logits, h)
            for n in POST_TILES:
                put(n + 1, 3, second_use, n)
            for h in range(HEADS_B):
                late = h == HEADS_B - 1
                put(gla_tile(h, 0), 7 if late else 3, gla_scores, h)
                put(gla_tile(h, 1), 4 if late else 1, gla_updates, h)
                put(gla_tile(h, 2) + late, 1 if late else 7, gla_outputs, h)
                put(gla_tile(h, 3), 6, gla_squares, h)
            put(KEYS_OUT, 7, keys_out)
            for u in range(NU + LAG_V):
                n, k = UNIT0 + u // 2, 3 + 4 * (u % 2)
                if u < NU:
                    put(n, k, unit_scores, u)
                if LAG_T <= u < NU + LAG_T:
                    put(n, k, unit_turn, u - LAG_T)
                if u >= LAG_V:
                    put(n, k, unit_values, u - LAG_V)

            for n in range(N_IN):
                pe.wait_ge(w_split, n + 1)
                if n >= 2:
                    pe.wait_ge(set_free[n % 2], uses_before(n))
                for kc in range(KC):
                    if n == 0:
                        if kc == 0:
                            pe.wait_ge(param_ok, 2)
                        pe.wait_ge(h_ok, kc + 1)
                    mm = chunk(n % RING, G[n % 2], kc, KC - 1, h_hi, h_lo)
                    if kc == KC - 1:
                        mm.then_inc(gemm_done, 1)
                    for step, args in beside.get((n, kc), ()):
                        step(*args)

            def turn_residual(i):
                if i == 0:
                    for j in range(NJ):
                        pe.wait_ge(in_x[j], 32)
                    pe.wait_ge(oa_ok, NU)
                else:
                    pe.wait_ge(xt_ok, i)
                for j, (t0, nt) in enumerate(TOK):
                    mm = pe.transpose(X[0][:, t0:t0 + nt], xtok[0:nt, j, i * P:(i + 1) * P], ident[0:nt, 0:nt])
                mm.then_inc(xt_done, 1)

            for i in range(KC):
                n = OUT0 + i
                pe.wait_ge(w_split, n + 1)
                pe.wait_ge(set_free[n % 2], uses_before(n))
                for kc in range(KC):
                    if i == 0:
                        pe.wait_ge(m_lo_ok, kc + 1)
                    m_hi, m_lo = (e_hi, e_lo) if kc < EARLY else (h_hi, h_lo)
                    mm = chunk(n % RING, G[n % 2], kc, KC - 1, m_hi, m_lo)
                    if kc == KC - 1:
                        mm.then_inc(gemm_done, 1)
                    if i == 1 and kc == 2:
                        turn_residual(0)
                if i >= 1:
                    turn_residual(i)

            def turn_rows(i):
                n = DN0[-1] + i
                pe.wait_ge(set_free[n % 2], uses_before(n) + 1)
                if i >= 2:
                    pe.wait_ge(y_ok, i - 1)
                for j, (t0, nt) in enumerate(TOK):
                    mm = pe.transpose(X[i % 2][0:nt, j * P:(j + 1) * P], x2T[:, i, t0:t0 + nt], ident[:, :])
                mm.then_inc(yt_done, 1)

            for n in range(GU0[0], GU0[0] + RING):
                pe.wait_ge(w_split, n + 1)
                pe.wait_ge(set_free[n % 2], uses_before(n))
                for kc in range(KC):
                    if n == GU0[0]:
                        pe.wait_ge(f_ok, kc + 1)
                    mm = chunk(n % RING, G[n % 2], kc, KC - 1, f_hi, f_lo)
                    if kc == KC - 1:
                        mm.then_inc(gemm_done, 1)
                    if n == GU0[0] and kc == KC - 1:
                        pe.wait_ge(x2_sum, KC)
                        for b in range(2):
                            mm = pe.matmul(X[1][:, 512 * b:512 * b + TH], ones[:, :],
                                           rv[:, b * TH:(b + 1) * TH], start=True, stop=True)
                        mm.then_inc(x2_ssq, 1)
            for g, m in enumerate(FF_GROUPS):
                with pe.Fori(1 if g == 0 else 0, 2 * m // RING) as i:
                    for t in range(RING):
                        n = GU0[g] + t
                        pe.wait_ge(w_split, i * RING + (n + 1))
                        pe.wait_ge(set_free[n % 2], i * 2 + uses_before(n))
                        for kc in range(KC):
                            mm = chunk(n % RING, G[n % 2], kc, KC - 1, f_hi, f_lo)
                        mm.then_inc(gemm_done, 1)
                before = sum(FF_GROUPS[:g])
                if g < len(FF_GROUPS) - 1:
                    with pe.Fori(0, KC // RING) as i:
                        for t in range(RING):
                            n = DN0[g] + t
                            pe.wait_ge(w_split, i * RING + (n + 1))
                            pe.wait_ge(set_free[n % 2], i * 2 + uses_before(n))
                            for kc in range(m):
                                if t == 0:
                                    pe.wait_ge(mid_ok, before + kc + 1)
                                mm = chunk(n % RING, G[n % 2], kc, m - 1, h_hi, h_lo)
                            mm.then_inc(gemm_done, 1)
                else:
                    for i in range(KC):
                        n = DN0[g] + i
                        pe.wait_ge(w_split, n + 1)
                        pe.wait_ge(set_free[n % 2], uses_before(n))
                        for kc in range(m):
                            if i == 0:
                                pe.wait_ge(mid_ok, before + kc + 1)
                            mm = chunk(n % RING, G[n % 2], kc, m - 1, h_hi, h_lo)
                        mm.then_inc(gemm_done, 1)
                        if i >= 1:
                            turn_rows(i - 1)
                    turn_rows(KC - 1)

        @block.scalar
        def _(act):
            steps = [0]

            def link(ins):
                steps[0] += 1
                ins.then_inc(act_step, 1)
                act.wait_ge(act_step, steps[0])

            def high_part(n, turn=None):
                slot = n % RING
                if turn is None:
                    act.wait_ge(wload[slot], 32 * (n // RING + 1))
                    if n >= RING:
                        act.wait_ge(gemm_done, n - RING + 1)
                else:
                    act.wait_ge(wload[slot], turn * 32 + 32 * (n // RING + 1))
                    act.wait_ge(gemm_done, turn * RING + (n - RING + 1))
                act.activation(w_hi[:, slot, :, :], wraw[:, slot, :, :], ACT.Copy).then_inc(hi_done, 1)

            act.preload_act_table_set(LN_EXP)

            act.wait_ge(const_dve, 3)
            for k, j in enumerate(ROWS_ACT):
                nt = TOK[j][1]
                act.wait_ge(in_x[j], 16)
                if k >= 2:
                    act.wait_ge(x_sq, k - 1)
                act.activation((G[1], X[0])[k % 2][0:nt, :], xtok[0:nt, j, :], ACT.Square,
                               accum_out=rv[0:nt, j:j + 1]).then_inc(x_sq, 1)
            act.wait_ge(x_sq, len(ROWS_ACT))
            act.wait_ge(x_sums, len(ROWS_DVE))
            link(act.activation(rs[:, 0:NJ], rv[:, 0:NJ], ACT.Ln, scale=1.0 / D, bias=eps[:, :]))
            act.activation(rt[:, 0:NJ], rs[:, 0:NJ], ACT.Exp, scale=-0.5).then_inc(r_ok, 1)
            high_part(0)
            act.wait_ge(x_root, 1)
            for part in range(2):
                for j in SCALE_ACT:
                    x = xtok[0:TOK[j][1], j, part * D // 2:(part + 1) * D // 2]
                    act.activation(x, x, ACT.Copy, scale=rt[0:TOK[j][1], j:j + 1])\
                        .then_inc(x_scaled_act, 1)
            act.wait_ge(param_ok, 1)
            for c in range(KC):
                if c in (3, 6):
                    high_part(c // 3)
                act.wait_ge(x_turned, c + 1)
                act.activation(h_hi[:, c, :], TURNED[c % 3][:, 0:T], ACT.Copy,
                               scale=param[:, G_MIX + c:G_MIX + c + 1]).then_inc(h_hi_ok, 1)

            high_part(3)

            def gate_logs(h):
                act.wait_ge(z_done, h + 1)
                if h >= 1:
                    act.wait_ge(z_ln, h)
                act.activation(h2(tB[:, 0:T]), halves(X[h % 2]), ACT.Abs,
                               bias=param[:, B_A + h:B_A + h + 1]).then_inc(z_abs, 1)
                act.wait_ge(z_abs, h + 1)
                link(act.activation(tB[:, 0:T], tB[:, 0:T], ACT.Exp, scale=-1.0))
                if h >= 1:
                    act.wait_ge(cum_ok, h)
                act.activation(tC[:, 0:T], tB[:, 0:T], ACT.Ln, bias=one[:, :]).then_inc(z_ln, 1)

            def gla_exps(h, part):
                if part == 0:
                    if h >= 2:
                        act.wait_ge(gla_state, h - 1)
                    act.wait_ge(cum_ok, HEADS_B)
                    act.activation(dec[:, h % 2, :], CB[:, h, :, P], ACT.Exp, scale=1.0 / TAU).then_inc(e_ok, 1)
                    act.wait_ge(d_ok, 5 * h + 1)
                    act.activation(tB[:, 0:T], tA[:, 0:T], ACT.Exp, scale=1.0 / TAU).then_inc(e_ok, 1)
                    act.activation(tC[:, 0:T], tA[:, 0:T], ACT.Exp, scale=-1.0 / TAU).then_inc(e_ok, 1)
                elif part == 1:
                    act.wait_ge(d_ok, 5 * h + 2)
                    act.activation(tB[:, 0:SEQ], tA[:, 0:SEQ], ACT.Exp, scale=1.0 / TAU).then_inc(e_ok, 1)
                    act.wait_ge(d_ok, 5 * h + 3)
                    act.activation(tC[:, 0:SEQ], tA[:, 0:SEQ], ACT.Exp, scale=1.0 / TAU).then_inc(e_ok, 1)
                else:
                    act.wait_ge(d_ok, 5 * h + 4)
                    act.activation(tB[:, 0:T], tA[:, 0:T], ACT.Exp, scale=1.0 / TAU).then_inc(e_ok, 1)
                    act.wait_ge(d_ok, 5 * h + 5)
                    act.activation(tC[:, :].rearrange("p (c n) -> p c n", n=P), CB[:, h, :, 1:P + 1],
                                   ACT.Exp, scale=1.0 / TAU).then_inc(e_ok, 1)

            def gla_copy_keys(h):
                act.wait_ge(gla_att, h + 1)
                link(act.activation(kot[:, 0:4, :], XB[3].rearrange("p (c n) -> p c n", c=4), ACT.Copy))
                act.activation(kot[0:DEC, SJ, :], XB[2][0:DEC, P:2 * P], ACT.Copy).then_inc(gla_kot, 1)

            def gla_copy_out(h):
                act.wait_ge(gla_out, h + 1)
                for f in range(2):
                    act.activation(obT[:, 2 * h + f, 0:SEQ], XB[2 + f], ACT.Copy)
                    ins = act.activation(obT[:, 2 * h + f, SEQ:T], XB[f][:, 0:DEC], ACT.Copy)
                    if f == 1:
                        link(ins)
                act.activation(sq[:, 0, :], obT[:, 2 * h, :], ACT.Square)
                act.activation(sq[:, 1, :], obT[:, 2 * h + 1, :], ACT.Square).then_inc(gla_sq, 1)

            def root():
                link(act.activation(rs[:, :], rv[:, :], ACT.Ln))
                act.activation(rt[:, :], rs[:, :], ACT.Exp, scale=-0.5).then_inc(r_ok, 1)

            def free_raw(n):
                last = [m for m in POST_TILES if m < n and m % 2 == n % 2]
                if last and IN_TILES[last[-1]][0] in ("kA", "qA"):
                    act.wait_ge(norm_done, NORMS.index(("post", last[-1])) + 1)
                elif last:
                    act.wait_ge(post_done, POST_TILES.index(last[-1]) + 1)

            def read_out(n):
                kind, i, _ = IN_TILES[n]
                s = n % 2
                ps = halves(G[s])
                act.wait_ge(gemm_done, n + 1)
                if kind == "a1":
                    act.activation(h2(a1T[:, :]), ps[0:RANK], ACT.Copy).then_inc(set_free[s], 1)
                elif kind in ("kB", "qB"):
                    if i >= 2:
                        act.wait_ge(gla_out, i - 1)
                    dst = (kT if kind == "kB" else qT)[:, i % 2, :]
                    act.activation(h2(dst), ps, ACT.Copy,
                                   scale=1.0 if kind == "kB" else float(DK) ** -0.5).then_inc(set_free[s], 1)
                elif kind in ("vB", "vA"):
                    free_raw(n)
                    act.activation(h2(raw[:, s, :]), ps, ACT.Copy).then_inc(set_free[s], 1)
                elif kind in ("kA", "qA"):
                    free_raw(n)
                    act.wait_ge(gla_ssq, sum(gla_tile(h, 2) < n for h in range(HEADS_B)))
                    link(act.activation(h2(sq[:, s, :]), ps, ACT.Square))
                    act.activation(h2(raw[:, s, :]), ps, ACT.Copy).then_inc(set_free[s], 1)
                elif kind == "ga":
                    if i == 0:
                        act.wait_ge(gla_norm, HEADS_B)
                        for r in range(2):
                            act.wait_ge(s_out[r], 32 * HEADS_B // 2)
                    act.activation(h2(gaT[:, i, :]), ps, ACT.Tanh, scale=0.5).then_inc(set_free[s], 1)
                elif kind == "rb":
                    if i >= 1:
                        act.wait_ge(set_free[s], uses_before(n))
                    act.activation(h2(th[:, 0, :]), ps, ACT.Tanh, scale=0.5).then_inc(tanh_ok, 1)
                elif kind == "gb":
                    if i >= 1:
                        act.wait_ge(gb_used, i)
                    act.activation(h2(th[:, 1, :]), ps, ACT.Tanh, scale=0.5).then_inc(set_free[s], 1)

            def keys_out():
                act.wait_ge(kt_done, 1)
                link(act.activation(kout[:, 0, :], XB[0][:, 0:2 * P], ACT.Copy))
                link(act.activation(kcT[:, :, :], XB[2][:, 0:2 * P].rearrange("p (u n) -> p u n", u=2), ACT.Copy))
                act.activation(kout[0:DEC, 1, :], XB[1][0:DEC, 0:2 * P], ACT.Copy).then_inc(kt_out, 1)
                act.wait_ge(kt_out, 1)
                act.dma_start(nk_p[0, 0].rearrange("t h d -> t (h d)"), kout[:, 0, :]).then_inc(out_sem, 16)
                act.dma_start(nk_s[0, 0].rearrange("t h d -> t (h d)"), kout[0:DEC, 1, :]).then_inc(out_sem, 16)
                for i in range(2):
                    n = TILE_OF["vA", i]
                    act.wait_ge(set_free[n % 2], uses_before(n) + 2)
                act.dma_start(nv_p[0, 0].rearrange("t h d -> t (h d)"), vA[:, SJ - 1, :]).then_inc(out_sem, 16)
                act.dma_start(nv_s[0, 0].rearrange("t h d -> t (h d)"), vA[0:DEC, SJ, :]).then_inc(out_sem, 16)

            def states_out(h):
                act.wait_ge(gla_state, h + 1)
                act.dma_start(ns_p[0, 0, h], Sfin[:, h % 2, :]).then_inc(s_out[h % 2], 16)
                act.dma_start(ns_s[0, 0, h], Ssmp[:, h % 2, :]).then_inc(s_out[h % 2], 16)

            def unit_exp(u):
                g, j, par, heads, nq, lo, hi = unit_shape(u)
                s = u % NB
                act.wait_ge(smax_ok, u + 1)
                for a in range(2):
                    act.activation(prob[0:nq, s, a, lo:hi], prob[0:nq, s, a, lo:hi], ACT.Exp,
                                   bias=nm[0:nq, s, a:a + 1], accum_out=sm[0:nq, s, a:a + 1])
                act.activation(es[0:nq, s, :], sd[0:nq, s, :], ACT.Exp).then_inc(exp_ok, 1)

            def unit_copy(u):
                g, j, par, heads, nq, lo, hi = unit_shape(u)
                act.wait_ge(pt_done, u + 1)
                if u >= 2:
                    act.wait_ge(pv_done, u - 1)
                src = XB[2].rearrange("p (a k n) -> p a k n", a=2, k=2)
                if j < SJ and lo == 0:
                    act.activation(probT[:, u % 2, :, :, :], src, ACT.Copy).then_inc(pt_copied, 1)
                    return
                for kt in range(lo // P, 2):
                    nk = min(hi - kt * P, P)
                    ins = act.activation(probT[0:nk, u % 2, :, kt, 0:nq], src[0:nk, :, kt, 0:nq], ACT.Copy)
                ins.then_inc(pt_copied, 1)

            def slot(u):
                if LAG_T <= u < NU + LAG_T:
                    unit_copy(u - LAG_T)
                if 0 <= u < NU:
                    unit_exp(u)

            def merged_high_part(i):
                act.wait_ge(m_ok, i + 1)
                dst = e_hi if i < EARLY else h_hi
                act.activation(dst[:, i, :], obT[:, i, :], ACT.Copy).then_inc(m_hi_ok, 1)

            for n in range(N_IN):
                for h in range(HEADS_B):
                    if n == gate_tile(h):
                        gate_logs(h)
                if n >= 1 and IN_TILES[n - 1][0] in ("kA", "qA"):
                    act.wait_ge(set_free[(n - 1) % 2], uses_before(n - 1) + 2)
                    root()
                for h in range(HEADS_B):
                    if n == gla_tile(h, 0):
                        gla_copy_keys(h)
                    if n == GLA_INPUTS[h]:
                        gla_exps(h, 0)
                        if h >= 1:
                            gla_exps(h, 1)
                    if n == GLA_FINISH[h] and h < HEADS_B - 1:
                        gla_exps(h, 2)
                for h in range(HEADS_B):
                    if n == gla_tile(h, 3):
                        act.wait_ge(gla_norm, h + 1)
                        root()
                if n == TILE_OF["ga", 0]:
                    act.preload_act_table_set(EXP_TANH)
                slot(2 * (n - UNIT0))
                if n == N_IN - 1:
                    act.wait_ge(m_ok, 2 * EARLY)
                    for i in range(EARLY):
                        merged_high_part(i)
                    act.wait_ge(gemm_done, N_IN)
                    for i in range(EARLY, SOON):
                        merged_high_part(i)
                read_out(n)
                if n == GLA_INPUTS[0]:
                    gla_exps(0, 1)
                if n == GLA_FINISH[-1]:
                    gla_exps(HEADS_B - 1, 2)
                if n < N_IN - 1:
                    high_part(n + RING)
                slot(2 * (n - UNIT0) + 1)
                for h in range(HEADS_B):
                    if n == gla_tile(h, 2):
                        states_out(h)
                        gla_copy_out(h)
                if n == KEYS_OUT:
                    keys_out()

            for i in range(SOON, KC):
                merged_high_part(i)
            high_part(N_IN - 1 + RING)
            act.wait_ge(out_sem, 64)
            for i in range(KC):
                n = OUT0 + i
                act.wait_ge(xt_done, i + 1)
                if i >= 2:
                    act.wait_ge(set_free[n % 2], uses_before(n))
                act.activation(xTi[:, i % 2, :], X[0][:, 0:T], ACT.Copy).then_inc(xt_ok, 1)
                act.wait_ge(f_in, i + 1)
                if i >= 2:
                    act.wait_ge(x2_sum, i - 1)
                act.activation(sq[:, i % 2, :], x2T[:, i, :], ACT.Square).then_inc(x2_sq, 1)
                act.activation(f_hi[:, i, :], x2g[:, i % 2, :], ACT.Copy).then_inc(f_hi_ok, 1)
                high_part(n + RING)
            act.preload_act_table_set(LN_EXP)
            act.wait_ge(norm_done, len(NORMS) + 1)
            root()
            act.preload_act_table_set(EXP_TANH)

            before = 0
            for g, m in enumerate(FF_GROUPS):
                with act.Fori(0, m // 2) as i:
                    for r in range(2):
                        n = GU0[g] + 2 * r
                        act.wait_ge(set_free[n % 2], i * 2 + (uses_before(n) + 1))
                        act.activation(ft[:, r, :], fg[:, r, :], ACT.Tanh, scale=0.5).then_inc(silu_ok, 1)
                        high_part(n + RING, i)
                        act.wait_ge(set_free[(n + 1) % 2], i * 2 + (uses_before(n + 1) + 1))
                        act.activation(h_hi[:, bass.ds(i * 2 + r, 1), :], fa[:, r:r + 1, :], ACT.Copy)\
                            .then_inc(mid_hi_ok, 1)
                        high_part(n + 1 + RING, i)
                before += m
                if g < len(FF_GROUPS) - 1:
                    with act.Fori(0, KC // RING) as i:
                        for t in range(RING):
                            high_part(DN0[g] + t + RING, i)

            def rows_out(i):
                act.wait_ge(yt_done, i + 1)
                if i >= 2:
                    act.wait_ge(y_out[i % 2], 32 * (i // 2))
                link(act.activation(ytok[:, i % 2, 0:4, :], X[i % 2][:, 0:SEQ].rearrange("p (j n) -> p j n", n=P),
                                    ACT.Copy))
                act.activation(ytok[0:DEC, i % 2, SJ, :], X[i % 2][0:DEC, SEQ:SEQ + P], ACT.Copy).then_inc(y_ok, 1)
                act.wait_ge(y_ok, i + 1)
                c = slice(i * P, (i + 1) * P)
                act.dma_start(y_prompt[0, :, c].rearrange("(j p) n -> p j n", p=P), ytok[:, i % 2, 0:4, :])\
                    .then_inc(y_out[i % 2], 16)
                act.dma_start(y_sample[0, :, c], ytok[0:DEC, i % 2, SJ, :]).then_inc(y_out[i % 2], 16)
            for i in range(KC):
                if DN0[-1] + RING + i < N_TILES:
                    high_part(DN0[-1] + RING + i)
                if i >= 1:
                    rows_out(i - 1)
            rows_out(KC - 1)
            for s in range(2):
                act.wait_ge(y_out[s], 32 * KC // 2)

        @block.vector
        def _(dve):
            steps = [0]

            def link(ins):
                steps[0] += 1
                ins.then_inc(dve_step, 1)
                dve.wait_ge(dve_step, steps[0])

            def refine(x, r, t, done=None):
                link(dve.scalar_tensor_tensor(out=t, in0=x, scalar=-0.5, in1=r, op0=ALU.mult, op1=ALU.mult))
                link(dve.tensor_tensor(t, t, r, ALU.mult))
                ins = dve.scalar_tensor_tensor(out=r, in0=t, scalar=1.5, in1=r, op0=ALU.add, op1=ALU.mult)
                if done is None:
                    link(ins)
                else:
                    ins.then_inc(done, 1)

            dve.memset(ones[:, :], 1.0).then_inc(const_dve, 1)
            dve.memset(rv[:, 0:NJ], 1.0).then_inc(const_dve, 1)
            link(dve.memset(head_ones[:, :], 0.0))
            dve.memset(head_ones[0:HD, 0:HD], 1.0)
            dve.memset(head_ones[HD:P, HD:P], 1.0)
            link(dve.memset(one[:, :], 1.0))
            dve.memset(eps[:, :], EPS).then_inc(const_dve, 1)
            link(dve.memset(lab[:, :, :], 0.0))
            link(dve.memset(reset[:, :, :], 1.0))
            link(dve.memset(reset[:, :, 0], 0.0))

            for k, j in enumerate(ROWS_DVE):
                dve.wait_ge(in_x[j], 16)
                if k >= 1:
                    dve.wait_ge(x_sums, k)
                dve.tensor_tensor_reduce(X[1][:, :], xtok[:, j, :], xtok[:, j, :], 1.0, 0.0, ALU.mult, ALU.add,
                                         rv[:, j:j + 1]).then_inc(x_sums, 1)
            dve.wait_ge(r_ok, 1)
            link(dve.tensor_scalar(rv[:, 0:NJ], rv[:, 0:NJ], 1.0 / D, EPS, ALU.mult, ALU.add))
            refine(rv[:, 0:NJ], rt[:, 0:NJ], rs[:, 0:NJ], x_root)
            dve.wait_ge(setup_pe, 1)
            dve.tensor_copy(param[:, :], G[0][:, 0:24]).then_inc(param_ok, 1)
            dve.wait_ge(x_root, 1)
            for part in range(2):
                for j in SCALE_DVE:
                    x = xtok[0:TOK[j][1], j, part * D // 2:(part + 1) * D // 2]
                    dve.tensor_scalar(x, x, rt[0:TOK[j][1], j:j + 1], None, ALU.mult).then_inc(x_scaled_dve, 1)
            dve.wait_ge(param_ok, 1)
            link(dve.tensor_scalar(param[:, G_Q:G_Q + 1], param[:, G_Q:G_Q + 1], HD ** -0.5, None, ALU.mult))
            link(dve.tensor_scalar(param[:, G_OB:G_OB + 2], param[:, G_OB:G_OB + 2], 0.25, None, ALU.mult))
            dve.tensor_copy(sinkb[:, :], G[0][:, 512:512 + HEADS_A]).then_inc(param_ok, 1)
            for c in range(KC):
                dve.wait_ge(h_hi_ok, c + 1)
                dve.scalar_tensor_tensor(out=h_lo[:, c, :], in0=TURNED[c % 3][:, 0:T],
                                         scalar=param[:, G_MIX + c:G_MIX + c + 1],
                                         in1=h_hi[:, c, :].bitcast(F32), op0=ALU.mult, op1=ALU.subtract)\
                    .then_inc(h_ok, 1)
            dve.wait_ge(const_pool, 2)
            link(dve.tensor_scalar(rs[:, 0:2 * P], dist[:, :], -1.0, None, ALU.mult))
            link(dve.tensor_tensor(dist[:, :], dist[:, :], rs[:, 0:2 * P], ALU.max))

            def gate_sums(h):
                dve.wait_ge(z_abs, h + 1)
                if h >= 1:
                    dve.wait_ge(cum_ok, h)
                dve.tensor_scalar(h2(tA[:, 0:T]), halves(X[h % 2]), param[:, B_A + h:B_A + h + 1], 0.0,
                                  ALU.add, ALU.min).then_inc(z_free, 1)
                dve.wait_ge(z_free, h + 1)
                dve.wait_ge(z_ln, h + 1)
                chunks = lambda t: t[:, 0:SEQ].rearrange("p (c n) -> p c n", n=P)
                link(dve.tensor_tensor(lab[:, 0:4, 1:P + 1], chunks(tA), chunks(tC), ALU.subtract))
                link(dve.tensor_tensor(lab[:, SJ, 1:DEC + 1], tA[:, SEQ:T], tC[:, SEQ:T], ALU.subtract))
                dve.tensor_tensor_scan(CB[:, h, :, :].rearrange("p c n -> p (c n)"),
                                       reset[:, :, :].rearrange("p c n -> p (c n)"),
                                       lab[:, :, :].rearrange("p c n -> p (c n)"), 0.0,
                                       ALU.mult, ALU.add).then_inc(cum_ok, 1)

            def gla_inputs(h, part):
                q, k = qT[:, h % 2, :], kT[:, h % 2, :]
                c = CB[:, h, :, 1:P + 1]

                def by(step, ap, count):
                    return ap.rearrange("p c (b n) -> p c b n", n=step)[:, 0:count]

                def halves_of(w, ap):
                    v = ap.rearrange("p (b a n) -> p b a n", a=2, n=w // 2)
                    return v[:, :, 0], v[:, :, 1]

                def from_boundary(w):
                    d1, d2 = halves_of(w, tA[:, 0:SEQ])
                    nb = P // w
                    cc = CB[:, h, 0:4, 1:P + 1].rearrange("p c (b n) -> p c b n", n=w)
                    edge = CB[:, h, 0:4, w // 2:P:w].unsqueeze(3).broadcast_to([P, 4, nb, w // 2])
                    d1 = d1.rearrange("p (c b) n -> p c b n", b=nb)
                    d2 = d2.rearrange("p (c b) n -> p c b n", b=nb)
                    dve.tensor_tensor(d1, edge, cc[:, :, :, 0:w // 2], ALU.subtract)
                    dve.tensor_tensor(d2, cc[:, :, :, w // 2:w], edge, ALU.subtract).then_inc(d_ok, 1)

                def decayed(w, x, t):
                    x1, x2 = halves_of(w, x[:, :])
                    e1, e2 = halves_of(w, t[:, 0:SEQ])
                    k1, _ = halves_of(w, k[:, 0:SEQ])
                    _, q2 = halves_of(w, q[:, 0:SEQ])
                    dve.tensor_tensor(x1, k1, e1, ALU.mult)
                    link(dve.tensor_tensor(x2, q2, e2, ALU.mult))

                if part == 0:
                    for kind in ("kB", "qB"):
                        n = TILE_OF[kind, h]
                        dve.wait_ge(set_free[n % 2], uses_before(n) + 1)
                    if h >= 1:
                        dve.wait_ge(gla_att, h)
                    dve.wait_ge(cum_ok, HEADS_B)
                    mid = CB[:, h, :, 16:P:32].unsqueeze(3).broadcast_to([P, NJ, 4, 32])
                    dve.tensor_tensor(by(32, tA[:, :].rearrange("p (c n) -> p c n", n=P), NJ), by(32, c, NJ),
                                      mid, ALU.subtract).then_inc(d_ok, 1)
                    dve.wait_ge(e_ok, 7 * h + 2)
                    link(dve.tensor_tensor(qL[:, :], q, tB[:, 0:T], ALU.mult))
                    dve.wait_ge(e_ok, 7 * h + 3)
                    link(dve.tensor_tensor(kL[:, :], k, tC[:, 0:T], ALU.mult))
                    from_boundary(64)
                    dve.wait_ge(e_ok, 7 * h + 4)
                    from_boundary(P)
                    decayed(64, x32, tB)
                    return
                dve.wait_ge(e_ok, 7 * h + 5)
                last = CB[:, h, :, P:P + 1].broadcast_to([P, NJ, P])
                dve.tensor_tensor(tA[:, :].rearrange("p (c n) -> p c n", n=P), last, c, ALU.subtract)\
                    .then_inc(d_ok, 1)
                x1, x2 = halves_of(P, x64[:, :])
                e1, e2 = halves_of(P, tC[:, 0:SEQ])
                dve.tensor_tensor(x1, halves_of(P, k[:, 0:SEQ])[0], e1, ALU.mult)
                dve.tensor_tensor(x2, halves_of(P, q[:, 0:SEQ])[1], e2, ALU.mult).then_inc(d_ok, 1)
                dve.wait_ge(d_ok, 5 * h + 5)
                dve.wait_ge(e_ok, 7 * h + 6)
                link(dve.tensor_tensor(k, k, tB[:, 0:T], ALU.mult))
                dve.wait_ge(e_ok, 7 * h + 7)
                dve.tensor_tensor(q, q, tC[:, 0:T], ALU.mult).then_inc(gla_in, 1)

            def gla_mask(h):
                dve.wait_ge(gla_att, h + 1)
                b4 = lambda ap: ap.rearrange("p (c n) -> p c n", n=P)
                link(dve.tensor_tensor(att[:, 0:4, :], b4(XB[0]),
                                       cmask[:, :].unsqueeze(1).broadcast_to([P, 4, P]), ALU.mult))
                link(dve.tensor_copy(att[0:64, 0:4, 64:P], b4(XB[1])[0:64, :, 64:P]))
                for a in (0, 64):
                    link(dve.tensor_copy(att[a:a + 32, 0:4, a + 32:a + 64], b4(XB[1])[a:a + 32, :, a + 32:a + 64]))
                dve.wait_ge(gla_kot, h + 1)
                dve.tensor_tensor(att[0:DEC, SJ, 0:DEC], XB[2][0:DEC, 0:DEC], cmask[0:DEC, 0:DEC],
                                  ALU.mult).then_inc(gla_masked, 1)

            def gla_states(h):
                dve.wait_ge(gla_upd, h + 1)
                if h >= 2:
                    dve.wait_ge(s_out[h % 2], 32 * (h // 2))
                add = lambda c: XB[c // 2][:, (c % 2) * DV:(c % 2 + 1) * DV]
                link(dve.tensor_copy(S[:, 0, :], add(0)))
                for c in range(1, 4):
                    dst = S[:, c, :] if c < 3 else Sfin[:, h % 2, :]
                    link(dve.scalar_tensor_tensor(out=dst, in0=S[:, c - 1, :], scalar=dec[:, h % 2, c:c + 1],
                                                  in1=add(c), op0=ALU.mult, op1=ALU.add))
                dve.scalar_tensor_tensor(out=Ssmp[:, h % 2, :], in0=Sin[:, h, :], scalar=dec[:, h % 2, SJ:SJ + 1],
                                         in1=XB[3][:, 0:DV], op0=ALU.mult, op1=ALU.add).then_inc(gla_state, 1)

            def mean_square(ps, scale, read):
                dve.tensor_scalar(h2(rv[:, :]), halves(ps), scale, EPS, ALU.mult, ALU.add).then_inc(*read)

            def gla_add(h):
                dve.wait_ge(gla_sq, h + 1)
                dve.tensor_tensor(sq[:, 0, :], sq[:, 0, :], sq[:, 1, :], ALU.add).then_inc(gla_sum, 1)

            def gla_norms(h):
                k = NORMS.index(("gla", h))
                dve.wait_ge(gla_ssq, h + 1)
                mean_square(X[0], 1.0 / DV, (gla_norm, 1))
                dve.wait_ge(gla_norm, h + 1)
                dve.wait_ge(r_ok, k + 2)
                refine(rv[:, :], rt[:, :], rs[:, :])
                for f in range(2):
                    o = obT[:, 2 * h + f, :]
                    ins = dve.scalar_tensor_tensor(out=o, in0=o, scalar=param[:, G_OB + f:G_OB + f + 1],
                                                   in1=rt[:, :], op0=ALU.mult, op1=ALU.mult)
                ins.then_inc(norm_done, 1)

            def second_use(n):
                kind, i, _ = IN_TILES[n]
                dve.wait_ge(post_done, POST_TILES.index(n) + 1)
                ps, s = G[n % 2], n % 2
                if kind in ("vB", "vA"):
                    dst = vB[:, (i // 2) % 2] if kind == "vB" else vA
                    f = slice((i % 2) * P, (i % 2) * P + P)
                    link(dve.tensor_copy(dst[:, 0:4, f], ps[:, 0:SEQ].rearrange("p (j n) -> p j n", n=P)))
                    dve.tensor_copy(dst[0:DEC, SJ, f], ps[0:DEC, SEQ:SEQ + P]).then_inc(set_free[s], 1)
                else:
                    mean_square(ps, 1.0 / HD, (set_free[s], 1))
                    dve.wait_ge(set_free[s], uses_before(n) + 2)
                    dve.wait_ge(r_ok, NORMS.index(("post", n)) + 2)
                    refine(rv[:, :], rt[:, :], rs[:, :])
                    dst, g = (kAT, G_K) if kind == "kA" else (qAT, G_Q)
                    dve.scalar_tensor_tensor(out=dst[:, i, :], in0=raw[:, s, :], scalar=param[:, g:g + 1],
                                             in1=rt[:, :], op0=ALU.mult, op1=ALU.mult).then_inc(norm_done, 1)

            def biases(pair):
                if pair == 0:
                    for r in range(2):
                        dve.wait_ge(s_out[r], 32 * HEADS_B // 2)
                    dve.wait_ge(gla_ssq, HEADS_B)
                hs = slice(2 * pair, 2 * pair + 2)
                for h in range(2 * pair, 2 * pair + 2):
                    slope = float(np.float32(2.0 ** (-8.0 * (h + 1) / HEADS_A)))
                    ins = dve.tensor_scalar(bias[:, h, :], dist[:, :], -slope, None, ALU.mult)
                link(ins)
                dve.memset(bias[0:CHUNK, hs, 2 * P - CHUNK:2 * P], NEG)
                link(dve.memset(bias[CHUNK:P, hs, 0:CHUNK], NEG))

            def unit_max(u):
                g, j, par, heads, nq, lo, hi = unit_shape(u)
                s = u % NB
                dve.wait_ge(qk_done, u + 1)
                if u >= NB:
                    dve.wait_ge(pt_done, u - NB + 1)
                for a, head in enumerate(heads):
                    ins = dve.tensor_tensor_reduce(
                        prob[0:nq, s, a, lo:hi], XB[u % 2][0:nq, a * 2 * P + lo:a * 2 * P + hi],
                        bias[0:nq, head, lo:hi], 1.0, NEG, ALU.add, ALU.max, mx[0:nq, s, a:a + 1])
                link(ins)
                sink = sinkb[0:nq, heads[0]:heads[1] + 1:2]
                link(dve.tensor_tensor(mx[0:nq, s, :], mx[0:nq, s, :], sink, ALU.max))
                link(dve.tensor_scalar(nm[0:nq, s, :], mx[0:nq, s, :], -1.0, None, ALU.mult))
                dve.tensor_tensor(sd[0:nq, s, :], sink, nm[0:nq, s, :], ALU.add).then_inc(smax_ok, 1)

            def unit_scale(u):
                g, j, par, heads, nq, lo, hi = unit_shape(u)
                s = u % NB
                dve.wait_ge(exp_ok, u + 1)
                link(dve.tensor_tensor(den[0:nq, s, :], sm[0:nq, s, :], es[0:nq, s, :], ALU.add))
                link(dve.reciprocal(rd[0:nq, s, :], den[0:nq, s, :]))
                for a in range(2):
                    o = prob[0:nq, s, a, lo:hi]
                    ins = dve.tensor_scalar(o, o, rd[0:nq, s, a:a + 1], 0.5, ALU.mult, ALU.mult)
                ins.then_inc(prob_ok, 1)

            def unit_out(u):
                g, j, par, heads, nq, lo, hi = unit_shape(u)
                dve.wait_ge(pv_done, u + 1)
                for i in (2 * g, 2 * g + 1):
                    n = TILE_OF["ga", i]
                    dve.wait_ge(set_free[n % 2], uses_before(n) + 1)
                r = slice(par * HD, (par + 1) * HD)
                o = gaT[r, 2 * g:2 * g + 2, TOK[j][0]:TOK[j][0] + nq]
                src = XB[3][r, 0:2 * P].rearrange("p (a n) -> p a n", a=2)[:, :, 0:nq]
                dve.scalar_tensor_tensor(out=o, in0=o, scalar=1.0, in1=src, op0=ALU.add, op1=ALU.mult)\
                    .then_inc(oa_ok, 1)

            def slot(u):
                if 1 <= u <= NU:
                    unit_scale(u - 1)
                if 0 <= u < NU:
                    unit_max(u)
                if LAG_V <= u < NU + LAG_V:
                    unit_out(u - LAG_V)

            def gates(n):
                kind, i, _ = IN_TILES[n]
                s = n % 2
                if kind == "rb":
                    dve.wait_ge(tanh_ok, i + 1)
                    dve.scalar_tensor_tensor(out=h2(rbu[:, :]), in0=h2(th[:, 0, :]), scalar=1.0,
                                             in1=halves(G[s]), op0=ALU.add, op1=ALU.mult)\
                        .then_inc(set_free[s], 1)
                    dve.wait_ge(set_free[s], uses_before(n) + 1)
                    link(dve.tensor_tensor(obT[:, i, :], obT[:, i, :], rbu[:, :], ALU.mult))
                elif kind == "gb":
                    dve.wait_ge(set_free[s], uses_before(n) + 1)
                    dve.scalar_tensor_tensor(out=obT[:, i, :], in0=th[:, 1, :], scalar=1.0, in1=obT[:, i, :],
                                             op0=ALU.add, op1=ALU.mult).then_inc(gb_used, 1)
                    dve.wait_ge(gb_used, i + 1)

            def merge(i):
                dve.wait_ge(oa_ok, 2 * NJ * (i // 2 + 1))
                dve.tensor_tensor(obT[:, i, :], obT[:, i, :], gaT[:, i, :], ALU.add).then_inc(m_ok, 1)

            def merged_low_part(i):
                dve.wait_ge(m_hi_ok, i + 1)
                hi, lo = (e_hi, e_lo) if i < EARLY else (h_hi, h_lo)
                dve.tensor_tensor(lo[:, i, :], obT[:, i, :], hi[:, i, :].bitcast(F32), ALU.subtract)\
                    .then_inc(m_lo_ok, 1)

            merged = 0
            for n in range(N_IN):
                for h in range(HEADS_B - 1):
                    if n == gla_tile(h, 1):
                        gla_states(h)
                if n >= 1 and USES[n - 1] == 2:
                    second_use(n - 1)
                if n == gla_tile(HEADS_B - 1, 1):
                    gla_states(HEADS_B - 1)
                for h in range(HEADS_B):
                    if n == gate_tile(h):
                        gate_sums(h)
                for h in range(HEADS_B):
                    if n == gla_tile(h, 0):
                        gla_mask(h)
                    if n == gla_tile(h, 3):
                        gla_add(h)
                for h in range(HEADS_B):
                    if n == GLA_INPUTS[h]:
                        gla_inputs(h, 0)
                    if n == GLA_FINISH[h]:
                        gla_inputs(h, 1)
                slot(2 * (n - UNIT0))
                if n == N_IN - 1:
                    dve.wait_ge(m_ok, 2 * EARLY)
                    for i in range(EARLY):
                        merged_low_part(i)
                    dve.wait_ge(gemm_done, N_IN)
                    for i in range(EARLY, SOON):
                        merged_low_part(i)
                gates(n)
                slot(2 * (n - UNIT0) + 1)
                for h in range(HEADS_B):
                    if n == gla_tile(h, 3):
                        gla_norms(h)
                if BIAS0 <= n < BIAS0 + HEADS_A // 2:
                    biases(n - BIAS0)
                while merged < KC and TILE_OF["gb", merged] <= n and \
                        UNIT0 + (2 * NJ * (merged // 2 + 1) - 1 + LAG_V) // 2 <= n:
                    merge(merged)
                    merged += 1

            for i in range(SOON, KC):
                merged_low_part(i)
            def add_squares(c):
                dve.wait_ge(x2_sq, c + 1)
                if c >= 1:
                    dve.wait_ge(x2_sum, c)
                    dve.tensor_tensor(rv[:, :], rv[:, :], sq[:, c % 2, :], ALU.add).then_inc(x2_sum, 1)
                else:
                    dve.tensor_copy(rv[:, :], sq[:, 0, :]).then_inc(x2_sum, 1)

            def f_low_part(c):
                dve.wait_ge(f_hi_ok, c + 1)
                dve.tensor_tensor(f_lo[:, c, :], x2g[:, c % 2, :], f_hi[:, c, :].bitcast(F32), ALU.subtract)\
                    .then_inc(f_ok, 1)

            dve.wait_ge(qk_done, NU)
            dve.wait_ge(out_sem, 64)
            for i in range(KC):
                n = OUT0 + i
                dve.wait_ge(gemm_done, n + 1)
                dve.wait_ge(xt_ok, i + 1)
                dve.tensor_tensor(h2(x2T[:, i, :]), halves(G[n % 2]), h2(xTi[:, i % 2, :]), ALU.add)\
                    .then_inc(set_free[n % 2], 1)
                dve.wait_ge(set_free[n % 2], uses_before(n) + 1)
                if i >= 2:
                    dve.wait_ge(f_ok, i - 1)
                dve.tensor_scalar(x2g[:, i % 2, :], x2T[:, i, :], param[:, G_FFN + i:G_FFN + i + 1], None,
                                  ALU.mult).then_inc(f_in, 1)
                if i >= 1:
                    f_low_part(i - 1)
                    add_squares(i - 1)
            f_low_part(KC - 1)
            add_squares(KC - 1)
            k = len(NORMS)
            dve.wait_ge(x2_ssq, 1)
            mean_square(X[1], 1.0 / D, (norm_done, 1))
            dve.wait_ge(norm_done, k + 1)
            dve.wait_ge(r_ok, k + 2)
            refine(rv[:, :], rt[:, :], rs[:, :])

            dve.wait_ge(xt_done, KC)
            before = 0
            for g, m in enumerate(FF_GROUPS):
                with dve.Fori(0, m // 2) as i:
                    for r in range(2):
                        n = GU0[g] + 2 * r
                        s, s1 = n % 2, (n + 1) % 2
                        gate = i * 2 + (before + r + 1)
                        dve.wait_ge(gemm_done, i * RING + (n + 1))
                        dve.tensor_tensor(h2(fg[:, r, :]), halves(G[s]), h2(rt[:, :]), ALU.mult)\
                            .then_inc(set_free[s], 1)
                        dve.wait_ge(set_free[s], i * 2 + (uses_before(n) + 1))
                        dve.wait_ge(silu_ok, gate)
                        dve.scalar_tensor_tensor(out=fs[:, r, :], in0=ft[:, r, :], scalar=1.0,
                                                 in1=fg[:, r, :], op0=ALU.add, op1=ALU.mult)\
                            .then_inc(fs_ok, 1)
                        dve.wait_ge(fs_ok, gate)
                        dve.scalar_tensor_tensor(out=fs[:, r, :], in0=fs[:, r, :], scalar=0.5,
                                                 in1=rt[:, :], op0=ALU.mult, op1=ALU.mult)\
                            .then_inc(fr_ok, 1)
                        dve.wait_ge(fr_ok, gate)
                        dve.wait_ge(gemm_done, i * RING + (n + 2))
                        dve.tensor_tensor(h2(fa[:, r, :]), h2(fs[:, r, :]), halves(G[s1]), ALU.mult)\
                            .then_inc(set_free[s1], 1)
                        dve.wait_ge(set_free[s1], i * 2 + (uses_before(n + 1) + 1))
                        dve.wait_ge(mid_hi_ok, gate)
                        at = bass.ds(i * 2 + r, 1)
                        dve.tensor_tensor(h_lo[:, at, :], fa[:, r:r + 1, :], h_hi[:, at, :].bitcast(F32),
                                          ALU.subtract).then_inc(mid_ok, 1)
                before += m
                with dve.Fori(0, KC // RING) as i:
                    for t in range(RING):
                        n = DN0[g] + t
                        dve.wait_ge(gemm_done, i * RING + (n + 1))
                        x = x2T[:, bass.ds(i * RING + t, 1), :].rearrange("p a (b n) -> p (a b) n", b=2)
                        dve.tensor_tensor(x, halves(G[n % 2]), x, ALU.add).then_inc(set_free[n % 2], 1)


_INS = ["x_prompt", "x_sample", "cache_swa_k", "cache_swa_v", "state_gla", "w_in", "w_a2", "b_a", "g_q", "g_k",
        "sinks", "g_ob", "w_out", "g_mix", "g_ffn", "w_gate", "w_up", "w_down"]
_OUTS = [(1, SEQ, D), (1, DEC, D), (1, 1, WINDOW, KV_A, HD), (1, 1, WINDOW, KV_A, HD),
         (1, 1, HEADS_B, DK, DV), (1, 1, DEC, KV_A, HD), (1, 1, DEC, KV_A, HD), (1, 1, HEADS_B, DK, DV)]


def kernel(**inputs):
    import concourse.bacc as bacc
    from concourse.bass_utils import run_bass_kernel_spmd

    nc = bacc.Bacc("TRN2", target_bir_lowering=False, num_devices=1)
    arrays, args = {}, []
    for name in _INS:
        a = np.ascontiguousarray(inputs[name])
        arrays[f"in_{name}_dram"] = a
        args.append(nc.dram_tensor(f"in_{name}_dram", a.shape, mybir.dt.from_np(a.dtype),
                                   kind="ExternalInput").ap())
    for i, shape in enumerate(_OUTS):
        args.append(nc.dram_tensor(f"out_{i}_dram", shape, F32, kind="ExternalOutput").ap())
    mixer_program(nc, *args)
    r = run_bass_kernel_spmd(nc, [arrays], core_ids=[0])
    return tuple(r.results[0][f"out_{i}_dram"] for i in range(len(_OUTS)))
```
